# Optimizing a Trainium2 kernel written in Bass

```python
import math
import jax
import jax.numpy as jnp
from jax import lax
import numpy as np

D_MODEL = 1024
BATCH = 1
SEQ = 512
DEPTH = 2
DEC_BATCH = 1
DEC_SEQ = 64
PAST_LEN = 256

CHUNK = 64
Q_BLOCK = 128
N_EVEN = (DEPTH + 1) // 2
N_ODD = DEPTH // 2
DEEP_ALPHA = (2.0 * DEPTH) ** 0.25
DEEP_BETA = (8.0 * DEPTH) ** -0.25
EPS = 1e-6
D_FF = 2816

GDN_H = 4
GDN_DK = 128
GDN_DV = 128
GDN_CONV = 4
GDN_QKV = GDN_H * (2 * GDN_DK + GDN_DV)

MLA_H = 4
MLA_NOPE = 128
MLA_ROPE = 64
MLA_V = 128
MLA_Q_LORA = 256
MLA_KV_LORA = 128
MLA_SCALE = (MLA_NOPE + MLA_ROPE) ** -0.5
ROPE_THETA = 10000.0

OFF_Z = GDN_QKV
OFF_B = OFF_Z + GDN_H * GDN_DV
OFF_A = OFF_B + GDN_H
OFF_QA = OFF_A + GDN_H
OFF_KVA = OFF_QA + MLA_Q_LORA
IN_COLS = OFF_KVA + MLA_KV_LORA + MLA_ROPE
MIX_OUT = GDN_H * GDN_DV + MLA_H * MLA_V

S5_M = 16
S5_G = D_MODEL // S5_M
S5_P = 64

kernel_name = 'hybrid_streaming_gdn_mla_s5'

def layer_norm(x, g, b):
    xf = x.astype(jnp.float32)
    mu = jnp.mean(xf, axis=-1, keepdims=True)
    var = jnp.mean(jnp.square(xf - mu), axis=-1, keepdims=True)
    y = (xf - mu) * lax.rsqrt(var + EPS) * g.astype(jnp.float32) + b.astype(jnp.float32)
    return y.astype(x.dtype)

def rms_norm(x, g):
    xf = x.astype(jnp.float32)
    y = xf * lax.rsqrt(jnp.mean(xf * xf, axis=-1, keepdims=True) + EPS) * g.astype(jnp.float32)
    return y.astype(x.dtype)

def l2_norm(x):
    xf = x.astype(jnp.float32)
    return xf * lax.rsqrt(jnp.sum(xf * xf, axis=-1, keepdims=True) + EPS)

def swiglu(u, w_in, w_out):
    gate, up = jnp.split(u @ w_in, 2, axis=-1)
    return (jax.nn.silu(gate) * up) @ w_out

def rope(x, pos):
    half = MLA_ROPE // 2
    inv = ROPE_THETA ** (-jnp.arange(half, dtype=jnp.float32) / half)
    ang = pos.astype(jnp.float32)[:, None] * inv[None, :]
    shape = (ang.shape[0],) + (1,) * (x.ndim - 3) + (half,)
    cos, sin = jnp.cos(ang).reshape(shape), jnp.sin(ang).reshape(shape)
    xf = x.astype(jnp.float32)
    x1, x2 = xf[..., :half], xf[..., half:]
    return jnp.concatenate([x1 * cos - x2 * sin, x2 * cos + x1 * sin], axis=-1).astype(x.dtype)

def causal_conv(buf, x, w):
    xp = jnp.concatenate([buf.astype(x.dtype), x], axis=1)
    L = x.shape[1]
    y = sum(xp[:, i:i + L] * w[i] for i in range(GDN_CONV))
    return y, xp[:, xp.shape[1] - (GDN_CONV - 1):]

def gdn_chunk_step(s0, inp):
    q, k, v, beta, g = inp
    C = q.shape[2]
    G = jnp.cumsum(g, axis=-1)
    incl = jnp.tril(jnp.ones((C, C), dtype=bool))
    strict = jnp.tril(jnp.ones((C, C), dtype=bool), -1)
    decay = jnp.where(incl, jnp.exp(jnp.where(incl, G[..., :, None] - G[..., None, :], 0.0)), 0.0)
    lower = jnp.where(strict, beta[..., :, None] * decay * jnp.einsum('bhtd,bhsd->bhts', k, k), 0.0)
    gam = jnp.exp(G)
    rhs = jnp.concatenate([beta[..., None] * v, (beta * gam)[..., None] * k], axis=-1)
    sol = lax.linalg.triangular_solve(lower + jnp.eye(C, dtype=lower.dtype), rhs,
                                      left_side=True, lower=True, unit_diagonal=True)
    dv = v.shape[-1]
    u = sol[..., :dv] - jnp.einsum('bhtk,bhkv->bhtv', sol[..., dv:], s0)
    o = (gam[..., None] * jnp.einsum('bhtk,bhkv->bhtv', q, s0)
         + jnp.einsum('bhts,bhsv->bhtv', jnp.einsum('bhtd,bhsd->bhts', q, k) * decay, u))
    g_end = G[..., -1:]
    s_new = (jnp.exp(g_end)[..., None] * s0
             + jnp.einsum('bhsk,bhsv->bhkv', jnp.exp(g_end - G)[..., None] * k, u))
    return s_new, o

def gated_delta(q, k, v, beta, g, s0):
    B, L, H = q.shape[:3]
    C = min(CHUNK, L)
    n = L // C

    def to_chunks(t):
        t = t.reshape(B, n, C, *t.shape[2:])
        return jnp.moveaxis(jnp.moveaxis(t, 3, 2), 1, 0)

    s_new, o = lax.scan(gdn_chunk_step, s0, tuple(to_chunks(t) for t in (q, k, v, beta, g)))
    o = jnp.moveaxis(jnp.moveaxis(o, 0, 1), 2, 3).reshape(B, L, H, o.shape[-1])
    return o, s_new

def mla_block(q_nope, q_rope, q_pos, k_nope, k_rope, v, k_pos):
    s = (jnp.einsum('bqhd,bkhd->bhqk', q_nope, k_nope)
         + jnp.einsum('bqhr,bkr->bhqk', q_rope, k_rope)).astype(jnp.float32) * MLA_SCALE
    visible = (q_pos // CHUNK)[:, None] >= (k_pos // CHUNK)[None, :]
    p = jax.nn.softmax(jnp.where(visible, s, -jnp.inf), axis=-1).astype(v.dtype)
    return jnp.einsum('bhqk,bkhd->bqhd', p, v)

def mla_attend(q_nope, q_rope, q_pos, k_nope, k_rope, v, k_pos):
    B, L = q_nope.shape[:2]
    if L <= Q_BLOCK:
        return mla_block(q_nope, q_rope, q_pos, k_nope, k_rope, v, k_pos)
    nb = L // Q_BLOCK

    def blocks(t):
        return jnp.moveaxis(t.reshape(B, nb, Q_BLOCK, *t.shape[2:]), 1, 0)

    out = lax.map(lambda a: mla_block(a[0], a[1], a[2], k_nope, k_rope, v, k_pos),
                  (blocks(q_nope), blocks(q_rope), q_pos.reshape(nb, Q_BLOCK)))
    return jnp.moveaxis(out, 0, 1).reshape(B, L, MLA_H, MLA_V)

def even_mixer(u, pos, s0, conv0, past_ckv, past_kr, w_in, conv_w, a_log, dt_bias, norm_w,
               q_norm, w_q_b, kv_norm, w_kv_b, w_out):
    f32 = jnp.float32
    B, L, _ = u.shape
    proj = u @ w_in
    qkv, conv_new = causal_conv(conv0, proj[..., :GDN_QKV], conv_w)
    qkv = jax.nn.silu(qkv)
    nq = GDN_H * GDN_DK
    q = l2_norm(qkv[..., :nq].reshape(B, L, GDN_H, GDN_DK)) * (GDN_DK ** -0.5)
    k = l2_norm(qkv[..., nq:2 * nq].reshape(B, L, GDN_H, GDN_DK))
    v = qkv[..., 2 * nq:].reshape(B, L, GDN_H, GDN_DV).astype(f32)
    z = proj[..., OFF_Z:OFF_B].reshape(B, L, GDN_H, GDN_DV)
    beta = jax.nn.sigmoid(proj[..., OFF_B:OFF_A].astype(f32))
    g = -jnp.exp(a_log.astype(f32)) * jax.nn.softplus(proj[..., OFF_A:OFF_QA].astype(f32) + dt_bias.astype(f32))
    o, s_new = gated_delta(q, k, v, beta, g, s0.astype(f32))
    o_gdn = (rms_norm(o, norm_w).astype(u.dtype) * jax.nn.silu(z)).reshape(B, L, GDN_H * GDN_DV)
    cq = rms_norm(proj[..., OFF_QA:OFF_KVA], q_norm)
    qh = (cq @ w_q_b).reshape(B, L, MLA_H, MLA_NOPE + MLA_ROPE)
    q_nope, q_rope = qh[..., :MLA_NOPE], rope(qh[..., MLA_NOPE:], pos)
    ckv = rms_norm(proj[..., OFF_KVA:OFF_KVA + MLA_KV_LORA], kv_norm)
    kr = rope(proj[..., OFF_KVA + MLA_KV_LORA:], pos)
    if past_ckv is None:
        keys_ckv, keys_kr, k_pos = ckv, kr, pos
    else:
        keys_ckv = jnp.concatenate([past_ckv.astype(ckv.dtype), ckv], axis=1)
        keys_kr = jnp.concatenate([past_kr.astype(kr.dtype), kr], axis=1)
        k_pos = jnp.arange(keys_ckv.shape[1], dtype=jnp.int32)
    kv = (keys_ckv @ w_kv_b).reshape(B, keys_ckv.shape[1], MLA_H, MLA_NOPE + MLA_V)
    o_mla = mla_attend(q_nope, q_rope, pos, kv[..., :MLA_NOPE], keys_kr, kv[..., MLA_NOPE:], k_pos)
    o_mla = o_mla.reshape(B, L, MLA_H * MLA_V)
    out = jnp.concatenate([o_gdn, o_mla], axis=-1) @ w_out
    return out, s_new, conv_new, ckv, kr

def complex_affine_combine(e1, e2):
    a1r, a1i, b1r, b1i = e1
    a2r, a2i, b2r, b2i = e2
    return (a2r * a1r - a2i * a1i, a2r * a1i + a2i * a1r,
            a2r * b1r - a2i * b1i + b2r, a2r * b1i + a2i * b1r + b2i)

def s5_mixer(u, h0_re, h0_im, lam_re, lam_im, log_dt, b_re, b_im, c_re, c_im, d_skip, w_glu, w_out):
    f32 = jnp.float32
    B, L, _ = u.shape
    dt = jnp.exp(log_dt.astype(f32))[:, None]
    lr = jnp.minimum(lam_re.astype(f32), -1e-4)
    li = lam_im.astype(f32)
    mag = jnp.exp(lr * dt)
    ab_re, ab_im = mag * jnp.cos(li * dt), mag * jnp.sin(li * dt)
    den = lr * lr + li * li
    coef_re = ((ab_re - 1.0) * lr + ab_im * li) / den
    coef_im = (ab_im * lr - (ab_re - 1.0) * li) / den
    br, bi = b_re.astype(f32), b_im.astype(f32)
    bb_re = coef_re[..., None] * br - coef_im[..., None] * bi
    bb_im = coef_re[..., None] * bi + coef_im[..., None] * br
    cr, ci = c_re.astype(f32), c_im.astype(f32)
    C = min(CHUNK, L)
    n = L // C
    ug = jnp.moveaxis(u.astype(f32).reshape(B, n, C, S5_G, S5_M), 1, 0)

    def step(h, u_c):
        h_re, h_im = h
        bu_re = jnp.einsum('bcgm,gpm->bcgp', u_c, bb_re)
        bu_im = jnp.einsum('bcgm,gpm->bcgp', u_c, bb_im)
        a_re = jnp.broadcast_to(ab_re, bu_re.shape)
        a_im = jnp.broadcast_to(ab_im, bu_re.shape)
        A_re, A_im, s_re, s_im = lax.associative_scan(complex_affine_combine, (a_re, a_im, bu_re, bu_im), axis=1)
        x_re = A_re * h_re[:, None] - A_im * h_im[:, None] + s_re
        x_im = A_re * h_im[:, None] + A_im * h_re[:, None] + s_im
        y = jnp.einsum('gmp,bcgp->bcgm', cr, x_re) - jnp.einsum('gmp,bcgp->bcgm', ci, x_im)
        return (x_re[:, -1], x_im[:, -1]), y

    (h_re, h_im), ys = lax.scan(step, (h0_re.astype(f32), h0_im.astype(f32)), ug)
    y = jnp.moveaxis(ys, 0, 1).reshape(B, L, D_MODEL).astype(u.dtype) + d_skip * u
    yg = jax.nn.gelu(y)
    out = (yg * jax.nn.sigmoid(yg @ w_glu)) @ w_out
    return out, h_re, h_im

def setup_inputs(seed: int = 0) -> dict:
    key = jax.random.key(seed)
    ks = iter(jax.random.split(key, 48))

    def nrm(shape, std=1.0):
        return std * jax.random.normal(next(ks), shape, jnp.float32)

    def uni(shape, lo, hi):
        return jax.random.uniform(next(ks), shape, jnp.float32, lo, hi)

    dt0 = jnp.exp(uni((N_EVEN, GDN_H), math.log(1e-3), math.log(1e-1)))
    lam_im0 = math.pi * jnp.arange(S5_P, dtype=jnp.float32)
    return {
        'x_prompt': nrm((BATCH, SEQ, D_MODEL)),
        'x_sample': nrm((DEC_BATCH, DEC_SEQ, D_MODEL)),
        'c_prompt': nrm((BATCH, D_MODEL)),
        'c_sample': nrm((DEC_BATCH, D_MODEL)),
        'cache_mla_latent': nrm((N_EVEN, DEC_BATCH, PAST_LEN, MLA_KV_LORA)),
        'cache_mla_krope': nrm((N_EVEN, DEC_BATCH, PAST_LEN, MLA_ROPE)),
        'state_gdn': nrm((N_EVEN, DEC_BATCH, GDN_H, GDN_DK, GDN_DV), 0.3),
        'state_gdn_conv': nrm((N_EVEN, DEC_BATCH, GDN_CONV - 1, GDN_QKV)),
        'state_s5_re': nrm((N_ODD, DEC_BATCH, S5_G, S5_P), 0.3),
        'state_s5_im': nrm((N_ODD, DEC_BATCH, S5_G, S5_P), 0.3),
        'w_ada': nrm((DEPTH, D_MODEL, 9 * D_MODEL), 0.2 * D_MODEL ** -0.5),
        'b_ada': nrm((DEPTH, 9 * D_MODEL), 0.01),
        'ln_g': 1.0 + nrm((DEPTH, 3, D_MODEL), 0.01),
        'ln_b': nrm((DEPTH, 3, D_MODEL), 0.01),
        'w_ff_in': nrm((DEPTH, 2, D_MODEL, 2 * D_FF), D_MODEL ** -0.5),
        'w_ff_out': nrm((DEPTH, 2, D_FF, D_MODEL), DEEP_BETA * D_FF ** -0.5),
        'w_mix_in': nrm((N_EVEN, D_MODEL, IN_COLS), D_MODEL ** -0.5),
        'gdn_conv_w': nrm((N_EVEN, GDN_CONV, GDN_QKV), GDN_CONV ** -0.5),
        'gdn_a_log': jnp.log(uni((N_EVEN, GDN_H), 1.0, 16.0)),
        'gdn_dt_bias': dt0 + jnp.log(-jnp.expm1(-dt0)),
        'gdn_norm_w': 1.0 + nrm((N_EVEN, GDN_DV), 0.01),
        'mla_q_norm': 1.0 + nrm((N_EVEN, MLA_Q_LORA), 0.01),
        'mla_w_q_b': nrm((N_EVEN, MLA_Q_LORA, MLA_H * (MLA_NOPE + MLA_ROPE)), MLA_Q_LORA ** -0.5),
        'mla_kv_norm': 1.0 + nrm((N_EVEN, MLA_KV_LORA), 0.01),
        'mla_w_kv_b': nrm((N_EVEN, MLA_KV_LORA, MLA_H * (MLA_NOPE + MLA_V)), MLA_KV_LORA ** -0.5),
        'w_mix_out': nrm((N_EVEN, MIX_OUT, D_MODEL), DEEP_BETA * MIX_OUT ** -0.5),
        's5_lambda_re': -0.5 + nrm((N_ODD, S5_G, S5_P), 0.01),
        's5_lambda_im': lam_im0 + nrm((N_ODD, S5_G, S5_P), 0.01),
        's5_log_dt': uni((N_ODD, S5_G), math.log(1e-3), math.log(1e-1)),
        's5_b_re': nrm((N_ODD, S5_G, S5_P, S5_M), (2 * S5_M) ** -0.5),
        's5_b_im': nrm((N_ODD, S5_G, S5_P, S5_M), (2 * S5_M) ** -0.5),
        's5_c_re': nrm((N_ODD, S5_G, S5_M, S5_P), S5_P ** -0.5),
        's5_c_im': nrm((N_ODD, S5_G, S5_M, S5_P), S5_P ** -0.5),
        's5_d': nrm((N_ODD, D_MODEL)),
        's5_w_glu': nrm((N_ODD, D_MODEL, D_MODEL), D_MODEL ** -0.5),
        's5_w_out': nrm((N_ODD, D_MODEL, D_MODEL), DEEP_BETA * D_MODEL ** -0.5),
    }

def reference(x_prompt, x_sample, c_prompt, c_sample, cache_mla_latent, cache_mla_krope, state_gdn,
              state_gdn_conv, state_s5_re, state_s5_im, w_ada, b_ada, ln_g, ln_b, w_ff_in, w_ff_out,
              w_mix_in, gdn_conv_w, gdn_a_log, gdn_dt_bias, gdn_norm_w, mla_q_norm, mla_w_q_b,
              mla_kv_norm, mla_w_kv_b, w_mix_out, s5_lambda_re, s5_lambda_im, s5_log_dt, s5_b_re,
              s5_b_im, s5_c_re, s5_c_im, s5_d, s5_w_glu, s5_w_out):

    def run_trunk(x, c, pos, gdn0, conv0, s5re0, s5im0, past_ckv, past_kr):
        B = x.shape[0]
        sc = jax.nn.silu(c)
        new_ckv, new_kr, new_gdn, new_conv, new_re, new_im = [], [], [], [], [], []
        for l in range(DEPTH):
            mod = (sc @ w_ada[l] + b_ada[l]).reshape(B, 3, 3, 1, D_MODEL)
            shift, scale, gate = mod[:, :, 0], mod[:, :, 1], 1.0 + mod[:, :, 2]
            h = swiglu(x * (1.0 + scale[:, 0]) + shift[:, 0], w_ff_in[l, 0], w_ff_out[l, 0])
            x = layer_norm(DEEP_ALPHA * x + 0.5 * gate[:, 0] * h, ln_g[l, 0], ln_b[l, 0])
            u = x * (1.0 + scale[:, 1]) + shift[:, 1]
            i = l // 2
            if l % 2 == 0:
                h, s_new, cv_new, ckv, kr = even_mixer(
                    u, pos, gdn0[i], conv0[i],
                    None if past_ckv is None else past_ckv[i], None if past_kr is None else past_kr[i],
                    w_mix_in[i], gdn_conv_w[i], gdn_a_log[i], gdn_dt_bias[i], gdn_norm_w[i],
                    mla_q_norm[i], mla_w_q_b[i], mla_kv_norm[i], mla_w_kv_b[i], w_mix_out[i])
                new_gdn.append(s_new)
                new_conv.append(cv_new)
                new_ckv.append(ckv)
                new_kr.append(kr)
            else:
                h, h_re, h_im = s5_mixer(
                    u, s5re0[i], s5im0[i], s5_lambda_re[i], s5_lambda_im[i], s5_log_dt[i],
                    s5_b_re[i], s5_b_im[i], s5_c_re[i], s5_c_im[i], s5_d[i], s5_w_glu[i], s5_w_out[i])
                new_re.append(h_re)
                new_im.append(h_im)
            x = layer_norm(DEEP_ALPHA * x + gate[:, 1] * h, ln_g[l, 1], ln_b[l, 1])
            h = swiglu(x * (1.0 + scale[:, 2]) + shift[:, 2], w_ff_in[l, 1], w_ff_out[l, 1])
            x = layer_norm(DEEP_ALPHA * x + 0.5 * gate[:, 2] * h, ln_g[l, 2], ln_b[l, 2])
        dt = x.dtype
        return (x, jnp.stack(new_ckv), jnp.stack(new_kr), jnp.stack(new_gdn).astype(dt),
                jnp.stack(new_conv), jnp.stack(new_re).astype(dt), jnp.stack(new_im).astype(dt))

    f32 = jnp.float32
    bp, sp = x_prompt.shape[0], x_prompt.shape[1]
    y_prompt, lat_p, kr_p, gdn_p, conv_p, re_p, im_p = run_trunk(
        x_prompt, c_prompt, jnp.arange(sp, dtype=jnp.int32),
        jnp.zeros((N_EVEN, bp, GDN_H, GDN_DK, GDN_DV), f32),
        jnp.zeros((N_EVEN, bp, GDN_CONV - 1, GDN_QKV), x_prompt.dtype),
        jnp.zeros((N_ODD, bp, S5_G, S5_P), f32), jnp.zeros((N_ODD, bp, S5_G, S5_P), f32),
        None, None)
    past = cache_mla_latent.shape[2]
    y_sample, lat_s, kr_s, gdn_s, conv_s, re_s, im_s = run_trunk(
        x_sample, c_sample, past + jnp.arange(x_sample.shape[1], dtype=jnp.int32),
        state_gdn, state_gdn_conv, state_s5_re, state_s5_im, cache_mla_latent, cache_mla_krope)
    return (y_prompt, y_sample, lat_p, kr_p, gdn_p, conv_p, re_p, im_p,
            lat_s, kr_s, gdn_s, conv_s, re_s, im_s)


_drawn_inputs = setup_inputs


def setup_inputs(seed=0):
    import zlib

    import numpy as np

    out = dict(_drawn_inputs(seed))
    spreads = {}
    factors = {'cache_mla_krope': 5.125,
     'gdn_norm_w': 200.0,
     'mla_q_norm': 45.625,
     'mla_kv_norm': 26.946,
     's5_lambda_re': 52.001,
     's5_c_re': 3.471,
     's5_c_im': 3.477}
    for name, (base, spread) in spreads.items():
        noise = np.random.default_rng([zlib.crc32(name.encode()), seed]).standard_normal(out[name].shape)
        drawn = base * np.exp(spread * noise) if base else spread * noise
        out[name] = jnp.asarray(drawn.astype(out[name].dtype))
    for name, factor in factors.items():
        out[name] = (out[name] * factor).astype(out[name].dtype)
    return out
```

```python
from contextlib import ExitStack

import numpy as np

import concourse.bass as bass
from concourse import mybir

F32 = mybir.dt.float32
F32R = mybir.dt.float32r
I32 = mybir.dt.int32
ALU = mybir.AluOpType
ACT = mybir.ActivationFunctionType
AX = mybir.AxisListType

P = 128
D = 1024
KD = D // P
SEQ, DEC = 512, 64
TOKENS = SEQ + DEC
HALF = TOKENS // 2
FT = 22
SEGS = ((0, 12), (12, 10))
HS = 12
ALPHA = (2.0 * 2) ** 0.25
EPS = 1e-6
BLOCK = 2048
CH = 64
PAST = 256
NMOD = 6
UNITS0 = SEGS[0][1] + KD + SEGS[1][1]
ADA_UNITS = (3 * NMOD - 2) * KD // 2
ADA_IN = {(0, 0): 0, (0, 1): SEGS[0][1] + KD, (1, 0): UNITS0, (1, 1): UNITS0 + SEGS[0][1],
          (2, 0): UNITS0 + SEGS[0][1] + SEGS[1][1]}
assert ADA_IN[2, 0] + SEGS[0][1] == ADA_UNITS
HEADS = 4
SUB = 8
NC = TOKENS // SUB
NCP = SEQ // SUB
PAIRS = 32
CONV = 4
QT = 12
PADW = (CONV - 1) + SEQ + (CONV - 1) + DEC
KEYS = TOKENS + PAST
KPAD = 896
MLA_SCALE = float((128 + 64) ** -0.5)

C_EPS = 0
C_CONV = 1
C_NORMW = C_CONV + QT * CONV
C_QN = C_NORMW + 1
C_KVN = C_QN + 2
C_DT = C_KVN + 1
C_ALOG = C_DT + 1
C_RNS = C_ALOG + 1
C_RNB = C_RNS + 1
C_OEPS = C_RNB + 1
C_HPI = C_OEPS + 1
NCOLS = C_HPI + 1


def feed_forward_blocks(f):
    return tuple((f"{k}{f}{s}", c) for s, (_, n) in enumerate(SEGS) for k, c in (("in", n), ("out", KD)))


STREAM = (feed_forward_blocks(0) + (("mix_in", 10), ("mla", 2), ("mix_out", 4)) + feed_forward_blocks(1)
          + feed_forward_blocks(2) + (("glu", 4), ("s5_out", 4)) + feed_forward_blocks(3))
OUTS = {"y": (P, KD, TOKENS), "conv_p": (P, QT, 3), "conv_s": (P, QT, 3), "gdn_p": (P, HEADS, P),
        "gdn_s": (P, HEADS, P), "latent": (P, TOKENS), "krope": (64, TOKENS), "s5_p": (P, 2, PAIRS),
        "s5_s": (P, 2, PAIRS)}
STORES = 8
N_CONST = 9 + 1


def span(t, r):
    return t[..., 0:SEQ] if r == 0 else t[..., SEQ:TOKENS]


def halves(ap):
    return ap.rearrange("p (a t) -> p a t", a=2)


class Chain:

    def __init__(self, eng, sem):
        self.eng, self.sem, self.n = eng, sem, 0

    def step(self, ins):
        self.n += 1
        ins.then_inc(self.sem, 1)
        self.eng.wait_ge(self.sem, self.n)


def trunk(nc, i, o):
    stack = ExitStack()
    sem = lambda name: stack.enter_context(nc.semaphore(name))

    X0 = 16512
    U0 = X0 + KD * TOKENS * 4
    A0 = U0 + 2 * KD * TOKENS * 4
    W0 = A0 + 2 * HS * TOKENS * 4
    E0 = W0 + 6 * BLOCK * 4
    TOP = 229344

    class Region:
        def __init__(self, at, end):
            self.at, self.end = at, end

        def __call__(self, name, shape, dt=F32):
            words = 1
            for s in shape[1:]:
                words *= s
            t = nc.alloc_sbuf_tensor_at(name, shape, dt, offset=self.at)
            self.at += -(-words * 4 // 32) * 32
            assert self.at <= self.end, (name, self.at, self.end)
            return t

    x = Region(X0, U0)("x", [P, KD, TOKENS])
    ru = Region(U0, A0)
    u_hi, u_lo = (ru(n, [P, KD, TOKENS], F32R) for n in ("u_hi", "u_lo"))
    ra = Region(A0, W0)
    h_hi, h_lo = (ra(n, [P, HS, TOKENS], F32R) for n in ("h_hi", "h_lo"))
    rw = Region(W0, E0)
    w_raw = rw("w_raw", [P, 2, BLOCK])
    w_hi, w_lo = (rw(n, [P, 2, BLOCK], F32R) for n in ("w_hi", "w_lo"))
    re = Region(E0, TOP)
    ident = re("ident", [P, P])
    mean_w = re("mean_w", [P, P])
    masks = re("masks", [P, 7, P])
    swap = re("swap", [P, 3, P])
    onecol = re("onecol", [P, 32])
    mod = re("mod", [P, 3 * NMOD, KD, 2])
    c_col = re("c_col", [P, KD, 2])
    b_ada = re("b_ada_sb", [P, 3 * NMOD, KD])
    u_scale, u_shift, res_gate = (re(n, [P, NMOD, KD, 2]) for n in ("u_scale", "u_shift", "res_gate"))
    ln_g, ln_b = (re(n, [P, NMOD, KD]) for n in ("ln_g_sb", "ln_b_sb"))
    cols = re("cols", [P, NCOLS])
    E1 = re.at
    rt = Region(E1, TOP)
    sg, hf = (rt(n, [P, 2, TOKENS]) for n in ("sg", "hf"))
    c_act = rt("c_act", [P, 2, D])
    ada_w = rt("ada_w", [P, 2, 2, D])
    ada_out = rt("ada_out", [P, 2, D])
    rln = Region(A0, W0)
    uf = rln("uf", [P, KD, TOKENS])
    sq = rln("sq", [P, 2, TOKENS])
    ln_std, ln_rstd = (rln(n, [P, TOKENS]) for n in ("ln_std", "ln_rstd"))
    ada_w0 = nc.alloc_sbuf_tensor_at("ada_w0", [P, KD, KD, P], F32, offset=U0)
    ada_w1 = nc.alloc_sbuf_tensor_at("ada_w1", [P, KD, D], F32, offset=A0)
    ps = nc.alloc_psum_tensor("ps", [P, 8, 512], F32)

    def pair(n):
        return ps[:, 2 * n:2 * n + 2, 0:HALF]

    s_in = sem("conditioning_loaded")
    s_in2 = sem("conditioning_loaded_again")
    s_cst = sem("constants_loaded")
    s_w0 = [sem(f"first_modulation_weights_{n}") for n in range(4)]
    s_w1 = [sem(f"second_modulation_weights_{n}") for n in range(4)]
    s_ada_w = [sem(f"modulation_weights_{n}") for n in range(2)]
    s_ada_c = sem("conditioning_ready")
    s_ada_t = sem("modulation_tile_summed")
    s_mod0 = sem("first_modulation_row_summed")
    s_mod1 = sem("second_modulation_row_summed")
    s_raw = [sem(f"weight_block_loaded_{n}") for n in range(2)]
    s_whi = sem("weight_hi_ready")
    s_wlo = sem("weight_lo_ready")
    s_blk = sem("block_product_done")
    s_evac = sem("block_banks_free")
    s_sg = sem("silu_ready")
    s_hh = sem("hidden_hi_ready")
    s_hl = sem("hidden_ready")
    s_mean = sem("ln_mean_ready")
    s_cen = sem("ln_centred")
    s_sq = sem("ln_square_ready")
    s_var = sem("ln_square_summed")
    s_std = sem("ln_std_ready")
    s_nrm = sem("ln_normed")
    s_uf = sem("u_modulated")
    s_uhi = sem("u_hi_ready")
    s_u = sem("u_ready")
    s_x = sem("x_ready")
    s_dve = sem("vector_step")
    s_act = sem("scalar_step")
    s_pool = sem("gpsimd_step")
    s_out = sem("outputs_stored")

    first = {}
    n = 0
    for name, count in STREAM:
        first[name] = n
        n += count
    n_blocks = n

    def stream_load(sp, name, width, src, skip=0):
        g0 = first[name]
        count = dict(STREAM)[name]
        if skip:
            for r in range(2):
                sp.dma_start(w_raw[:, r, 0:width], src(r)).then_inc(s_raw[r], 16)
        if skip == count:
            return

        def body(i):
            for r in range(2):
                sp.wait_ge(s_wlo, g0 + 2 * i + r - 1)
                sp.dma_start(w_raw[:, r, 0:width], src(2 * i + r)).then_inc(s_raw[r], 16)

        if count - skip > 2:
            with sp.Fori(skip // 2, count // 2) as i:
                body(i)
        else:
            body(skip // 2)

    def split_hi(act, g0, r, i):
        act.wait_ge(s_raw[r], 16 * (g0 // 2 + 1) + 16 * i)
        act.activation(w_hi[:, r, :], w_raw[:, r, :], ACT.Copy).then_inc(s_whi, 1)

    def split_lo(dve, g0, r, i):
        dve.wait_ge(s_raw[r], 16 * (g0 // 2 + 1) + 16 * i)
        dve.wait_ge(s_whi, g0 + r + 1 + 2 * i)
        dve.tensor_tensor(w_lo[:, r, :], w_raw[:, r, :], w_hi[:, r, :].bitcast(F32),
                          ALU.subtract).then_inc(s_wlo, 1)

    def blocks_loop(eng, count, body, peel=0, start=0):
        whole = count // 2 - peel
        for i in range(start):
            for r in range(2):
                body(i, r, True)
        if whole > 1:
            with eng.Fori(start, whole) as i:
                for r in range(2):
                    body(i, r, True)
        elif whole == 1:
            for r in range(2):
                body(0, r, True)
        for i in range(whole, count // 2):
            for r in range(2):
                body(i, r, False)

    def three(pe, out, wh, wl, mh, ml, start, stop):
        m = None
        for n_, (w, mv) in enumerate(((wh, mh), (wh, ml), (wl, mh))):
            for a in range(2):
                m = pe.matmul(out[:, a, :], w, mv[:, a, :], start=start and n_ == 0, stop=stop and n_ == 2)
        return m

    def product(pe, name, tiles, kk, mov_hi, mov_lo, ready=None):
        g0, count = first[name], dict(STREAM)[name]
        hi, lo = (t if callable(t) else (lambda k, t=t: t[:, k, :]) for t in (mov_hi, mov_lo))
        views = [(w[:, r, 0:kk * tiles * P].rearrange("p (k m c) -> p k m c", k=kk, m=tiles))
                 for r in range(2) for w in (w_hi, w_lo)]

        def body(i, r, _):
            pe.wait_ge(s_wlo, g0 + r + 1 + 2 * i)
            if g0 + r >= 2:
                pe.wait_ge(s_evac, g0 + r - 1 + 2 * i)
            elif not (isinstance(i, int) and i == 0):
                pe.wait_ge(s_evac, r + 2 * i - 1)
            for m_ in range(tiles):
                for k in range(kk):
                    if ready is not None and m_ == 0:
                        ready(k)
                    mm = three(pe, pair(2 * r + m_), views[2 * r][:, k, m_, :], views[2 * r + 1][:, k, m_, :],
                               halves(hi(k)), halves(lo(k)), k == 0, k == kk - 1)
            mm.then_inc(s_blk, 1)
        return body, count

    def ffn_sync(sp, f):
        for s, (j0, n) in enumerate(SEGS):
            win = i["w_in"][f]
            stream_load(sp, f"in{f}{s}", BLOCK, lambda b: win[j0 + b, :, :] if isinstance(b, int) else
                        win[bass.ds(j0 + b, 1), :, :].rearrange("a p c -> (a p) c"),
                        skip=2 if f == 0 and s == 0 else 0)
            wout = i[f"w_out{s}"][f]
            stream_load(sp, f"out{f}{s}", n * P, lambda b: wout[b, :, :] if isinstance(b, int) else
                        wout[bass.ds(b, 1), :, :].rearrange("a p c -> (a p) c"))

    def ffn_tensor(pe, f, u_count):
        for s, (j0, n) in enumerate(SEGS):
            body, count = product(pe, f"in{f}{s}", 2, KD, u_hi, u_lo)
            if s == 0:
                pe.wait_ge(s_u, u_count)
            blocks_loop(pe, count, body, start=1 if f == 0 and s == 0 else 0)
            h0 = FT * f + j0
            body, count = product(pe, f"out{f}{s}", 1, n, h_hi, h_lo,
                                  ready=lambda k: pe.wait_ge(s_hl, h0 + (n - 2 if k == 0 else n))
                                  if k in (0, n - 2) else None)
            blocks_loop(pe, count, body)

    def ffn_scalar(act, f):
        for s, (j0, n) in enumerate(SEGS):
            g0 = first[f"in{f}{s}"]

            def body(i, r, _):
                act.wait_ge(s_blk, g0 + r + 1 + 2 * i)
                act.activation(halves(sg[:, r, :]), pair(2 * r), ACT.Silu).then_inc(s_sg, 1)
                split_hi(act, g0 + 2, r, i)
            blocks_loop(act, n, body)
            g1 = first[f"out{f}{s}"]

            def body(i, r, more):
                if more or g1 + 2 * i + r + 2 < n_blocks:
                    act.wait_ge(s_blk, g1 + r + 1 + 2 * i)
                    split_hi(act, g1 + 2, r, i)
            blocks_loop(act, KD, body, peel=1)

    def ffn_vector(dve, f):
        for s, (j0, n) in enumerate(SEGS):
            g0, h0 = first[f"in{f}{s}"], FT * f + j0

            def body(i, r, _):
                dve.wait_ge(s_sg, h0 + r + 1 + 2 * i)
                dve.tensor_tensor(halves(hf[:, r, :]), pair(2 * r + 1), halves(sg[:, r, :]),
                                  ALU.mult).then_inc(s_evac, 1)
                split_lo(dve, g0 + 2, r, i)
                slot = bass.ds(2 * i + r, 1) if not isinstance(i, int) else slice(2 * i + r, 2 * i + r + 1)
                dve.wait_ge(s_evac, g0 + r + 1 + 2 * i)
                dve.tensor_copy(h_hi[:, slot, :], hf[:, r:r + 1, :]).then_inc(s_hh, 1)
                dve.wait_ge(s_hh, h0 + r + 1 + 2 * i)
                dve.tensor_tensor(h_lo[:, slot, :], hf[:, r:r + 1, :], h_hi[:, slot, :].bitcast(F32),
                                  ALU.subtract).then_inc(s_hl, 1)
                dve.wait_ge(s_hl, h0 + r + 1 + 2 * i)
                if (f, s) in ADA_IN:
                    ada_unit(dve, ADA_IN[f, s], i, r)
            blocks_loop(dve, n, body, start=1 if (f, s) == (0, 0) else 0)
            if s == 0:
                gate_vector(dve, (0, 2, 3, 5)[f])
            residual_vector(dve, f"out{f}{s}", (0, 2, 3, 5)[f], 1)

    def residual_vector(dve, name, site, tiles):
        g1, count = first[name], dict(STREAM)[name]

        def body(i, r, more):
            dve.wait_ge(s_blk, g1 + r + 1 + 2 * i)
            for m_ in range(tiles):
                for half in range(3):
                    a, lo, hi, st = ((0, 0, HALF, 0), (1, HALF, SEQ, 0), (1, SEQ, TOKENS, 1))[half]
                    k = (2 * i + r) * tiles + m_
                    ks = bass.ds(k, 1) if not isinstance(i, int) else slice(k, k + 1)
                    gate = res_gate[:, site, ks, st:st + 1].rearrange("p a b -> p (a b)")
                    ins = dve.scalar_tensor_tensor(
                        out=x[:, ks, lo:hi], in0=pair(2 * r + m_)[:, a:a + 1, lo - a * HALF:hi - a * HALF],
                        scalar=gate, in1=x[:, ks, lo:hi], op0=ALU.mult, op1=ALU.add)
            ins.then_inc(s_evac, 1)
            if more or g1 + 2 * i + r + 2 < n_blocks:
                split_lo(dve, g1 + 2, r, i)
            if name == "out00":
                ada_unit(dve, SEGS[0][1], i, r)
        blocks_loop(dve, count, body, peel=1)
        dve.wait_ge(s_evac, g1 + count)

    def ln_tensor(pe, n, done):
        pe.wait_ge(s_evac, done)
        for k in range(KD):
            for a in range(2):
                m = pe.matmul(pair(0)[:, a, :], mean_w[:, :], halves(x[:, k, :])[:, a, :],
                              start=k == 0, stop=k == KD - 1)
        m.then_inc(s_mean, 1)
        for k in range(KD):
            pe.wait_ge(s_sq, KD * n + k + 1)
            for a in range(2):
                m = pe.matmul(pair(1)[:, a, :], mean_w[:, :], halves(sq[:, k % 2, :])[:, a, :],
                              start=k == 0, stop=k == KD - 1)
            m.then_inc(s_var, 1)

    def ln_scalar(act, n):
        for k in range(KD):
            act.wait_ge(s_cen, KD * n + k + 1)
            if k >= 2:
                act.wait_ge(s_var, KD * n + k - 1)
            act.activation(sq[:, k % 2, :], x[:, k, :], ACT.Square).then_inc(s_sq, 1)
        act.wait_ge(s_var, KD * (n + 1))
        act.activation(halves(ln_std[:, :]), pair(1), ACT.Sqrt, bias=cols[:, C_EPS:C_EPS + 1]).then_inc(s_std, 1)
        if n < NMOD - 1:
            u_scalar(act, n + 1)

    def u_scalar(act, n):
        if n == 4:
            return
        for k in range(KD):
            act.wait_ge(s_uf, KD * n + k + 1)
            act.activation(u_hi[:, k, :], uf[:, k, :], ACT.Copy).then_inc(s_uhi, 1)

    def u_tile(dve, n, k):
        for st in range(2):
            ins = dve.tensor_scalar(span(uf[:, k, :], st), span(x[:, k, :], st), u_scale[:, n, k, st:st + 1],
                                    u_shift[:, n, k, st:st + 1], ALU.mult, ALU.add)
        ins.then_inc(s_uf, 1)

    def u_low(dve, n, k):
        if n == 4:
            return
        dve.wait_ge(s_uhi, KD * (n - (n > 4)) + k + 1)
        dve.tensor_tensor(u_lo[:, k, :], uf[:, k, :], u_hi[:, k, :].bitcast(F32), ALU.subtract).then_inc(s_u, 1)

    def ln_vector(dve, n):
        if n < NMOD - 1:
            scale_vector(dve, n + 1)
        dve.wait_ge(s_mean, n + 1)
        for k in range(KD):
            dve.tensor_tensor(halves(x[:, k, :]), halves(x[:, k, :]), pair(0), ALU.subtract).then_inc(s_cen, 1)
        dve.wait_ge(s_std, n + 1)
        link = chains["dve"]
        link.step(dve.reciprocal(ln_rstd[:, :], ln_std[:, :]))
        dve.wait_ge(s_sq, KD * (n + 1))
        dve.wait_ge(s_cen, KD * (n + 1))
        for k in range(KD):
            dve.tensor_tensor(x[:, k, :], x[:, k, :], ln_rstd[:, :], ALU.mult).then_inc(s_nrm, 1)
            if n < NMOD - 1:
                dve.wait_ge(s_nrm, KD * n + k + 1)
                u_tile(dve, n + 1, k)
                if k >= 1:
                    u_low(dve, n + 1, k - 1)
        if n < NMOD - 1:
            u_low(dve, n + 1, KD - 1)
            dve.wait_ge(s_uf, KD * (n + 2))
        dve.wait_ge(s_nrm, KD * (n + 1))
        for k in range(KD):
            dve.tensor_scalar(x[:, k, :], x[:, k, :], ln_g[:, n, k:k + 1], ln_b[:, n, k:k + 1],
                              ALU.mult, ALU.add).then_inc(s_x, 1)
        dve.wait_ge(s_x, KD * (n + 1))

    def ada_product(dve, w, t, st, n):
        flat = mod[:, :, :, :].rearrange("p c k b -> p (c k) b")
        ts = slice(t, t + 1) if isinstance(t, int) else bass.ds(t, 1)
        return dve.scalar_tensor_tensor(out=ada_out[:, n % 2, :], in0=w, scalar=1.0, in1=c_act[:, st, :],
                                        op0=ALU.mult, op1=ALU.mult,
                                        accum_out=flat[:, ts, st:st + 1].rearrange("p a b -> p (a b)"))

    def ada_sync(sp):
        sp.dma_start(c_col[:, :, :], i["c_col"]).then_inc(s_in, 16)
        sp.dma_start(c_act[:, :, :], i["c"]).then_inc(s_in, 16)
        for j in range(4):
            sp.dma_start(ada_w0[:, 2 * j:2 * j + 2, :, :], i["w_ada0"][:, 2 * j:2 * j + 2, :, :]).then_inc(s_w0[j], 16)
            sp.dma_start(ada_w1[:, 2 * j:2 * j + 2, :], i["w_ada"][:, 2 * j:2 * j + 2, :]).then_inc(s_w1[j], 16)

    def conditioning_scalar(act, loaded, again):
        act.wait_ge(loaded, 16 if again else 32)
        if not again:
            act.activation(c_col[:, :, :], c_col[:, :, :], ACT.Silu)
        act.activation(c_act[:, :, :], c_act[:, :, :], ACT.Silu).then_inc(s_ada_c, 1)

    def ada_load(pool, u0, u1):
        def body(v, fresh=False):
            for r in range(2):
                if not fresh:
                    pool.wait_ge(s_ada_t, 8 * v + 4 * r - 4)
                t = KD + 4 * v + 2 * r
                ts = slice(t, t + 2) if isinstance(v, int) else bass.ds(t, 2)
                pool.dma_start(ada_w[:, r, :, :], i["w_ada"][:, ts, :]).then_inc(s_ada_w[r], 16)
        body(u0 // 2, u0 == 0)
        with pool.Fori(u0 // 2 + 1, u1 // 2) as v:
            body(v)

    def ada_unit(dve, u0, i_, r):
        dve.wait_ge(s_ada_w[r], 16 * (u0 // 2 + 1) + 16 * i_)
        for n in range(4):
            done_ = 4 * (u0 + r) + n - 1 + 8 * i_
            if not isinstance(i_, int) or done_ > 0:
                dve.wait_ge(s_ada_t, done_)
            ada_product(dve, ada_w[:, r, n // 2, :], 2 * KD + 2 * (u0 + r) + n // 2 + 4 * i_, n % 2,
                        n).then_inc(s_ada_t, 1)

    def ada_tensor_first(pe):
        pe.wait_ge(s_ada_c, 1)
        for m_ in range(KD):
            if m_ % 2 == 0:
                pe.wait_ge(s_w0[m_ // 2], 16)
            for k in range(KD):
                mm = pe.matmul(ps[:, 0, 2 * m_:2 * m_ + 2], ada_w0[:, m_, k, :], c_col[:, k, :],
                               start=k == 0, stop=k == KD - 1)
        mm.then_inc(s_mod0, 1)

    def with_bias(dve, c, src):
        bias = b_ada[:, c, :].rearrange("p (k b) -> p k b", b=1).broadcast_to([P, KD, 2])
        return dve.tensor_tensor(mod[:, c, :, :], src, bias, ALU.add)

    def ada_vector_first(dve):
        dve.wait_ge(s_ada_c, 1)
        for t in range(KD):
            if t % 2 == 0:
                dve.wait_ge(s_w1[t // 2], 16)
            for st in range(2):
                n = 2 * t + st
                if n >= 2:
                    dve.wait_ge(s_mod1, n - 1)
                ada_product(dve, ada_w1[:, t, :], KD + t, st, n).then_inc(s_mod1, 1)
        dve.wait_ge(s_mod1, 2 * KD)
        dve.wait_ge(s_cst, 16 * N_CONST)
        dve.wait_ge(s_mod0, 1)
        with_bias(dve, 0, ps[:, 0, 0:2 * KD].rearrange("p (k b) -> p k b", b=2))

    def gate_vector(dve, n):
        dve.wait_ge(s_ada_t, 2 * KD * (3 * n + 1))
        chains["dve"].step(with_bias(dve, 3 * n + 2, mod[:, 3 * n + 2, :, :]))
        w = 1.0 if n % 3 == 1 else 0.5
        chains["dve"].step(dve.tensor_scalar(res_gate[:, n, :, :], mod[:, 3 * n + 2, :, :], 1.0, w / ALPHA,
                                             ALU.add, ALU.mult))

    def scale_vector(dve, n):
        link = chains["dve"].step
        shift, scale = mod[:, 3 * n, :, :], mod[:, 3 * n + 1, :, :]
        if n:
            dve.wait_ge(s_ada_t, 2 * KD * 3 * n)
            with_bias(dve, 3 * n, shift)
        link(with_bias(dve, 3 * n + 1, scale))
        if n == 0:
            dve.tensor_scalar(u_scale[:, 0, :, :], scale, 1.0, None, ALU.add)
            link(dve.tensor_copy(u_shift[:, 0, :, :], shift))
            return
        g = ln_g[:, n - 1, :].rearrange("p (k b) -> p k b", b=1).broadcast_to([P, KD, 2])
        b = ln_b[:, n - 1, :].rearrange("p (k b) -> p k b", b=1).broadcast_to([P, KD, 2])
        link(dve.tensor_scalar(scale, scale, 1.0, None, ALU.add))
        dve.tensor_tensor(u_scale[:, n, :, :], scale, g, ALU.mult)
        link(dve.tensor_tensor(u_shift[:, n, :, :], scale, b, ALU.mult))
        link(dve.tensor_tensor(u_shift[:, n, :, :], u_shift[:, n, :, :], shift, ALU.add))

    ra = Region(A0, W0)
    xp = ra("xp", [P, QT, PADW])
    zg = ra("zg", [P, HEADS, TOKENS])
    qa = ra("qa", [P, 2, TOKENS])
    kvraw = ra("kvraw", [P, TOKENS])
    misc = ra("misc", [P, TOKENS])
    ckv = ra("ckv", [P, KPAD])
    rows_b = Region(ra.at, W0)
    rm = rows_b("rm", [P, TOKENS])
    rd = Region(A0, A0 + 20480)
    kd = rd("kd", [P, 5 * HEADS, P])
    uv = rd("uv", [P, 5 * HEADS, P])
    rr = Region(A0 + 20480, A0 + QT * PADW * 4)
    rows, t1, gcum = (rr(n, [P, TOKENS]) for n in ("rows", "t1", "gcum"))
    rt2 = Region(E1, TOP)
    qkv = rt2("qkv", [P, QT, TOKENS])
    ctmp = rt2("ctmp", [P, 2, PADW])
    pt = rt2("pt", [P, 5 * HEADS, P])
    sqm = nc.alloc_sbuf_tensor_at("sqm", [P, 2, TOKENS], F32, offset=E1 + QT * TOKENS * 4)
    t2 = nc.alloc_sbuf_tensor_at("t2", [P, TOKENS], F32, offset=E1 + QT * TOKENS * 4)
    t3 = nc.alloc_sbuf_tensor_at("t3", [P, TOKENS], F32, offset=E1 + QT * TOKENS * 4 + 2304)
    og = nc.alloc_sbuf_tensor_at("og", [P, HEADS, TOKENS], F32, offset=E1)
    ru2 = Region(U0, A0)
    qg = ru2("qg", [P, HEADS, TOKENS])
    wt = ru2("wt", [P, 5 * HEADS, P])
    ctok = ru2("ctok", [P, 5, P])
    ge = ru2("ge", [P, HEADS, 10])
    KP0 = ru2.at
    kp, vp, dl, xi, zi, ys, cm = (ru2(n, [P, HEADS, P]) for n in ("kp", "vp", "dl", "xi", "zi", "ys", "cm"))
    st = nc.alloc_sbuf_tensor_at("st", [P, 2, HEADS, P], F32, offset=KP0)
    uu = nc.alloc_sbuf_tensor_at("uu", [P, 2, HEADS, P], F32, offset=KP0 + 4096)
    rn = nc.alloc_sbuf_tensor_at("rn", [P, TOKENS], F32, offset=KP0 + 4096)
    rstd = nc.alloc_sbuf_tensor_at("rstd", [P, TOKENS], F32, offset=KP0 + 4096 + 2304)
    rm2 = Region(A0, A0 + QT * PADW * 4)
    kn = rm2("kn", [P, HEADS, KPAD])
    kr = rm2("kr", [P, KPAD])
    cq_hi, cq_lo = (rm2(n, [P, 2, TOKENS], F32R) for n in ("cq_hi", "cq_lo"))
    rt3 = Region(E1, TOP)
    vt = rt3("vt", [P, 7, 512])
    qn = rt3("qn", [P, HEADS, TOKENS])
    qr = rt3("qr", [P, 2, TOKENS])
    ck_hi, ck_lo = (rt3(n, [P, KPAD], F32R) for n in ("ck_hi", "ck_lo"))
    rtmp = rt3("rtmp", [P, TOKENS])
    pp = rt3("pp", [P, 2, 512])
    ra3 = Region(A0 + QT * PADW * 4, W0)
    rope = ra3("rope", [P, 2, TOKENS])
    ppt = ra3("ppt", [P, 2, 4, P])
    sm = ra3("sm", [P, 4, 20])

    s_mc = sem("conv_state_loaded")
    s_mk = sem("cached_latents_loaded")
    s_pad = sem("conv_padding_ready")
    s_conv = sem("conv_step")
    s_qkv = sem("conv_silu_ready")
    s_nsq = sem("norm_square_ready")
    s_nss = sem("norm_square_summed")
    s_nst = sem("norm_std_ready")
    s_rn = sem("row_norms_ready")
    s_rb = sem("norm_broadcast_ready")
    s_ru = sem("norm_applied")
    s_ga = sem("gate_scalar_step")
    s_gv = sem("gate_vector_step")
    s_ct = sem("frame_columns_turned")
    s_col = sem("frame_columns_ready")
    s_g1 = sem("block_gram_ready")
    s_dx = sem("block_exponents_ready")
    s_de = sem("block_decays_ready")
    s_kv = sem("block_scaled_ready")
    s_cm = sem("level_part_ready")
    s_y = sem("level_first_product")
    s_ys = sem("level_first_copied")
    s_zx = sem("level_second_product")
    s_xz = sem("level_inverse_ready")
    s_uw = sem("block_solution_ready")
    s_bd = sem("block_done")
    s_s0 = sem("states_loaded")
    s_sw = sem("chunk_state_product")
    s_su = sem("chunk_update_ready")
    s_ku = sem("chunk_outer_ready")
    s_st = sem("chunk_state_ready")
    s_so = sem("chunk_output_ready")
    s_oc = sem("chunk_output_copied")
    s_zs = sem("gate_silu_ready")
    s_oh = sem("mixer_output_hi")
    s_ol = sem("mixer_output_ready")

    BLK = [(b, b * P, P if b < 4 else 64) for b in range(5)]
    g_in = first["mix_in"]

    def mix_sync(sp):
        stream_load(sp, "mix_in", BLOCK, lambda b: i["w_mix_in"][b, :, :] if isinstance(b, int) else
                    i["w_mix_in"][bass.ds(b, 1), :, :].rearrange("a p c -> (a p) c"))
        g0 = first["mla"]
        for r, (src, w) in enumerate(((i["w_q_b"], 1536), (i["w_kv_b"], 1024))):
            sp.wait_ge(s_wlo, g0 + r - 1)
            sp.dma_start(w_raw[:, r, 0:w], src).then_inc(s_raw[r], 16)
        stream_load(sp, "mix_out", BLOCK, lambda b: i["w_mix_out"][b, :, :] if isinstance(b, int) else
                    i["w_mix_out"][bass.ds(b, 1), :, :].rearrange("a p c -> (a p) c"))

    def mix_gpsimd(pool):
        pool.wait_ge(s_u, 2 * KD)
        pool.dma_start(xp[:, :, SEQ + 3:SEQ + 6], i["conv_state"]).then_inc(s_mc, 16)
        pool.dma_start(ckv[:, TOKENS:KEYS], i["cache_latent"]).then_inc(s_mk, 16)
        pool.wait_ge(s_evac, g_in + 6)
        pool.dma_start(o["conv_p"], xp[:, :, SEQ:SEQ + 3]).then_inc(s_out, 16)
        pool.dma_start(o["conv_s"], xp[:, :, PADW - 3:PADW]).then_inc(s_out, 16)
        pool.wait_ge(s_bd, 5)
        pool.dma_start(st[:, 1, :, :], i["gdn_state"]).then_inc(s_s0, 16)
        pool.wait_ge(s_st, 10)
        pool.dma_start(o["gdn_p"], st[:, 0, :, :]).then_inc(s_out, 16)
        pool.dma_start(o["gdn_s"], st[:, 1, :, :]).then_inc(s_out, 16)
        mla_gpsimd(pool)

    def mix_in_scalar(act):
        def evacuate(r, m_, dst_p0, dst_p1, dst_s):
            src = pair(2 * r + m_)
            act.activation(dst_p0, src[:, 0:1, :], ACT.Copy)
            act.activation(dst_p1, src[:, 1:2, 0:SEQ - HALF], ACT.Copy)
            return act.activation(dst_s, src[:, 1:2, SEQ - HALF:HALF], ACT.Copy)

        def body(i, r, _):
            act.wait_ge(s_blk, g_in + r + 1 + 2 * i)
            if isinstance(i, int) and i == 0 and r == 0:
                act.wait_ge(s_u, 2 * KD)
            for m_ in range(2):
                t = 4 * i + 2 * r + m_
                ts = slice(t, t + 1) if isinstance(i, int) else bass.ds(t, 1)
                last = evacuate(r, m_, xp[:, ts, 3:3 + HALF], xp[:, ts, 3 + HALF:3 + SEQ], xp[:, ts, SEQ + 6:PADW])
            last.then_inc(s_evac, 1)
            split_hi(act, g_in + 2, r, i)
            for m_ in range(2):
                t = 4 * i + 2 * r + m_
                ts = slice(t, t + 1) if isinstance(i, int) else bass.ds(t, 1)
                act.wait_ge(s_conv, 4 * t + 4)
                act.activation(qkv[:, ts, 0:SEQ], ctmp[:, m_:m_ + 1, 0:SEQ], ACT.Silu)
                act.activation(qkv[:, ts, SEQ:TOKENS], ctmp[:, m_:m_ + 1, SEQ + 3:SEQ + 3 + DEC],
                               ACT.Silu).then_inc(s_qkv, 1)
        blocks_loop(act, 6, body, start=1)
        dest = [zg[:, h, :] for h in range(HEADS)] + [qa[:, 0, :], qa[:, 1, :], kvraw[:, :], misc[:, :]]
        for b in range(4):
            r, bi = b % 2, 3 + b // 2
            act.wait_ge(s_blk, g_in + 7 + b)
            for m_ in range(2):
                last = act.activation(halves(dest[2 * b + m_]), pair(2 * r + m_), ACT.Copy)
            last.then_inc(s_evac, 1)
            split_hi(act, g_in + 2, r, bi)

    def mix_in_vector(dve):
        dve.wait_ge(s_u, 2 * KD)
        dve.memset(xp[:, :, 0:3], 0.0).then_inc(s_pad, 1)
        dve.wait_ge(s_pad, 1)
        dve.wait_ge(s_mc, 16)
        W = PADW - 3

        def body(i, r, _):
            split_lo(dve, g_in + 2, r, i)
            dve.wait_ge(s_evac, g_in + r + 1 + 2 * i)
            for m_ in range(2):
                t = 4 * i + 2 * r + m_
                ts = slice(t, t + 1) if isinstance(i, int) else bass.ds(t, 1)
                if not isinstance(t, int) or t >= 2:
                    dve.wait_ge(s_qkv, t - 1)
                for a in range(CONV):
                    wcol = (cols[:, C_CONV + 4 * t + a:C_CONV + 4 * t + a + 1] if isinstance(t, int) else
                            cols[:, bass.ds(4 * t + C_CONV + a, 1)])
                    if a:
                        dve.wait_ge(s_conv, 4 * t + a)
                        ins = dve.scalar_tensor_tensor(out=ctmp[:, m_:m_ + 1, 0:W], in0=xp[:, ts, a:a + W],
                                                       scalar=wcol, in1=ctmp[:, m_:m_ + 1, 0:W],
                                                       op0=ALU.mult, op1=ALU.add)
                    else:
                        ins = dve.tensor_scalar(ctmp[:, m_:m_ + 1, 0:W], xp[:, ts, 0:W], wcol, None, ALU.mult)
                    ins.then_inc(s_conv, 1)
        blocks_loop(dve, 6, body, start=1)
        for b in range(4):
            split_lo(dve, g_in + 2, b % 2, 3 + b // 2)

    NORM_ROW = [0, 1, 2, 3, 4, 5, 6, 7, 8, 8, 9]

    def norm_source(n_):
        return qkv[:, n_, :] if n_ < 8 else qa[:, n_ - 8, :] if n_ < 10 else kvraw[:, :]

    def norms_scalar(act):
        act.wait_ge(s_qkv, QT)
        act.wait_ge(s_evac, g_in + 10)
        for n_ in range(11):
            if n_ >= 2:
                act.wait_ge(s_nss, n_ - 1)
            act.activation(sqm[:, n_ % 2, :], norm_source(n_), ACT.Square).then_inc(s_nsq, 1)
        act.wait_ge(s_nss, 11)
        act.activation(halves(rstd[0:10, :]), pair(0)[0:10], ACT.Sqrt, bias=cols[0:10, C_RNB:C_RNB + 1],
                       scale=cols[0:10, C_RNS:C_RNS + 1]).then_inc(s_nst, 1)
        step = lambda ins, n_: (ins.then_inc(s_ga, 1), act.wait_ge(s_ga, n_))
        act.wait_ge(s_gv, 1)
        step(act.activation(rows[0:4, :], misc[64:68, :], ACT.Sigmoid), 1)
        step(act.activation(t1[0:4, :], misc[96:100, :], ACT.Identity, bias=cols[96:100, C_DT:C_DT + 1]), 2)
        step(act.activation(t2[0:4, :], t1[0:4, :], ACT.Abs), 3)
        step(act.activation(t2[0:4, :], t2[0:4, :], ACT.Exp, scale=-1.0), 4)
        step(act.activation(t2[0:4, :], t2[0:4, :], ACT.Ln, bias=1.0), 5)
        step(act.activation(cols[0:4, C_ALOG:C_ALOG + 1], cols[0:4, C_ALOG:C_ALOG + 1], ACT.Exp), 6)
        act.wait_ge(s_gv, 5)
        step(act.activation(rows[32:36, :], gcum[0:4, :], ACT.Copy), 7)
        step(act.activation(t3[0:4, :], gcum[0:4, :], ACT.Exp), 8)
        step(act.activation(rows[96:100, :], t1[0:4, :], ACT.Exp), 9)

    def norms_vector(dve):
        dve.wait_ge(s_qkv, QT)
        dve.wait_ge(s_out, 32)
        dve.memset(ckv[:, KEYS:KPAD], 0.0)
        dve.memset(rm[0:4, :], 1.0)
        dve.memset(rows[:, :], 0.0).then_inc(s_gv, 1)
        dve.wait_ge(s_gv, 1)
        dve.memset(rm[0:4, :].rearrange("p (c t) -> p c t", t=CH)[:, :, 0:1], 0.0).then_inc(s_gv, 1)
        dve.wait_ge(s_ga, 6)
        dve.scalar_tensor_tensor(out=t1[0:4, :], in0=t1[0:4, :], scalar=0.0, in1=t2[0:4, :], op0=ALU.max,
                                 op1=ALU.add).then_inc(s_gv, 1)
        dve.wait_ge(s_gv, 3)
        dve.tensor_scalar(t1[0:4, :], t1[0:4, :], cols[0:4, C_ALOG:C_ALOG + 1], -1.0, ALU.mult,
                          ALU.mult).then_inc(s_dve, 1)
        chains["dve"].n += 1
        dve.wait_ge(s_dve, chains["dve"].n)
        dve.tensor_tensor_scan(gcum[0:4, :], rm[0:4, :], t1[0:4, :], 0.0, ALU.mult, ALU.add).then_inc(s_gv, 1)
        dve.wait_ge(s_gv, 4)
        g3 = gcum[0:4, :].rearrange("p (c t) -> p c t", t=CH)
        dve.tensor_tensor(t1[0:4, :].rearrange("p (c t) -> p c t", t=CH),
                          g3[:, :, CH - 1:CH].broadcast_to([4, 9, CH]), g3, ALU.subtract).then_inc(s_gv, 1)
        dve.wait_ge(s_ga, 9)
        dve.tensor_tensor(rows[64:68, :], rows[0:4, :], t3[0:4, :], ALU.mult).then_inc(s_gv, 1)
        dve.wait_ge(s_nst, 1)
        dve.reciprocal(rn[0:10, :], rstd[0:10, :]).then_inc(s_rn, 1)
        for j in range(10):
            dve.wait_ge(s_rb, j + 1)
            spread = pair(1 + j % 3)
            if j < 8:
                ins = dve.tensor_tensor(halves(qkv[:, j, :]), halves(qkv[:, j, :]), spread, ALU.mult)
            elif j == 8:
                for m_ in range(2):
                    ins = dve.scalar_tensor_tensor(out=halves(qa[:, m_, :]), in0=halves(qa[:, m_, :]),
                                                   scalar=cols[:, C_QN + m_:C_QN + m_ + 1], in1=spread,
                                                   op0=ALU.mult, op1=ALU.mult)
            else:
                ins = dve.scalar_tensor_tensor(out=halves(ckv[:, 0:TOKENS]), in0=halves(kvraw[:, :]),
                                               scalar=cols[:, C_KVN:C_KVN + 1], in1=spread,
                                               op0=ALU.mult, op1=ALU.mult)
            ins.then_inc(s_ru, 1)
        dve.wait_ge(s_ct, 1)
        dve.tensor_copy(ctok[:, 0:4, :], ps[:, 0, :].rearrange("p (b c) -> p b c", b=4))
        dve.tensor_copy(ctok[0:64, 4, :], ps[0:64, 1, 0:P]).then_inc(s_col, 1)
        dve.wait_ge(s_ru, 10)
        dve.wait_ge(s_col, 1)

    def norms_tensor(pe):
        pe.wait_ge(s_evac, g_in + 10)
        for n_ in range(11):
            pe.wait_ge(s_nsq, n_ + 1)
            j = NORM_ROW[n_]
            for a in range(2):
                m = pe.matmul(pair(0)[0:16, a, :], onecol[:, 15 - j:31 - j], halves(sqm[:, n_ % 2, :])[:, a, :],
                              start=n_ == 0, stop=n_ == 10)
            m.then_inc(s_nss, 1)
        pe.wait_ge(s_rn, 1)
        for j in range(10):
            if j >= 3:
                pe.wait_ge(s_ru, j - 2)
            for a in range(2):
                m = pe.matmul(pair(1 + j % 3)[:, a, :], ident[0:10, j:j + 1].broadcast_to([10, P]),
                              halves(rn[0:10, :])[:, a, :], start=True, stop=True)
            m.then_inc(s_rb, 1)
        pe.wait_ge(s_gv, 6)
        pe.wait_ge(s_ru, 10)
        for b, t0, n_ in BLK:
            m = pe.transpose(ps[0:n_, b // 4, (b % 4) * P:(b % 4) * P + P], rows[:, t0:t0 + n_], ident[:, :])
        m.then_inc(s_ct, 1)

    def bank(n_, rows_=P, width=P):
        return ps[0:rows_, n_, 0:HEADS * P].rearrange("p (h c) -> p h c", h=HEADS)[:, :, 0:width]

    def gdn_tensor(pe):
        pe.wait_ge(s_col, 1)
        for b, t0, n_ in BLK:
            if b:
                pe.wait_ge(s_bd, b)
            q, k, v = (lambda h, j=j: qkv[:, 4 * j + h, t0:t0 + n_] for j in range(3))
            for h in range(HEADS):
                m = pe.matmul(bank(0, P, n_)[:, h, :], ident[0:4, h:h + 1].broadcast_to([4, P]),
                              gcum[0:4, t0:t0 + n_], start=True, stop=True)
            m.then_inc(s_g1, 1)
            for h in range(HEADS):
                m = pe.matmul(bank(1, n_, n_)[:, h, :], k(h), k(h), start=True, stop=True)
            m.then_inc(s_g1, 1)
            for h in range(HEADS):
                m = pe.matmul(bank(2, n_, n_)[:, h, :], k(h), q(h), start=True, stop=True)
            m.then_inc(s_g1, 1)
            for j, f in ((3, k), (4, v)):
                for h in range(HEADS):
                    m = pe.transpose(bank(j, n_)[:, h, :], f(h), ident[:, :])
                m.then_inc(s_g1, 1)
            for lv in range(6):
                pe.wait_ge(s_cm, 6 * b + lv + 1)
                if lv:
                    pe.wait_ge(s_xz, 6 * b + lv)
                for h in range(HEADS):
                    m = pe.matmul(bank(5, n_, n_)[:, h, :], cm[0:n_, h, 0:n_],
                                  zi[0:n_, h, 0:n_] if lv else ident[0:n_, 0:n_], start=True, stop=True)
                m.then_inc(s_y, 1)
                if lv:
                    pe.wait_ge(s_ys, 5 * b + lv)
                    for h in range(HEADS):
                        m = pe.matmul(bank(6, n_, n_)[:, h, :], xi[0:n_, h, 0:n_], ys[0:n_, h, 0:n_],
                                      start=True, stop=True)
                    if lv < 5:
                        for h in range(HEADS):
                            m = pe.matmul(bank(7, n_, n_)[:, h, :], ys[0:n_, h, 0:n_], xi[0:n_, h, 0:n_],
                                          start=True, stop=True)
                    m.then_inc(s_zx, 1)
            pe.wait_ge(s_xz, 6 * (b + 1))
            pe.wait_ge(s_kv, b + 1)
            for h in range(HEADS):
                m = pe.matmul(bank(3, n_)[:, h, :], zi[0:n_, h, 0:n_], vp[0:n_, h, :], start=True, stop=True)
            for h in range(HEADS):
                m = pe.matmul(bank(4, P, n_)[:, h, :], kp[0:n_, h, :], zi[0:n_, h, 0:n_], start=True, stop=True)
            m.then_inc(s_uw, 1)

    def gdn_scalar(act):
        for b, t0, n_ in BLK:
            act.wait_ge(s_g1, 5 * b + 1)
            if b:
                act.wait_ge(s_zx, 5 * b)
            act.activation(ys[:, :, 0:n_], bank(0, P, n_), ACT.Exp).then_inc(s_de, 1)
            act.wait_ge(s_dx, 2 * b + 1)
            act.activation(dl[0:n_, :, 0:n_], dl[0:n_, :, 0:n_], ACT.Exp, scale=-1.0)
            act.activation(pt[0:n_, 4 * b:4 * b + 4, 0:n_], pt[0:n_, 4 * b:4 * b + 4, 0:n_],
                           ACT.Exp).then_inc(s_de, 1)
            act.wait_ge(s_dx, 2 * b + 2)
            for lv in range(1, 6):
                act.wait_ge(s_y, 6 * b + lv + 1)
                act.activation(ys[0:n_, :, 0:n_], bank(5, n_, n_), ACT.Copy).then_inc(s_ys, 1)
            act.wait_ge(s_uw, b + 1)
            act.activation(uv[0:n_, 4 * b:4 * b + 4, :], bank(3, n_), ACT.Copy)
            act.activation(wt[:, 4 * b:4 * b + 4, 0:n_], bank(4, P, n_), ACT.Copy).then_inc(s_bd, 1)

    def gdn_vector(dve):
        link = chains["dve"].step
        for b, t0, n_ in BLK:
            col = lambda kind, h: ctok[0:n_, b, 32 * kind + h:32 * kind + h + 1]
            if b:
                dve.wait_ge(s_uw, b)
            dve.wait_ge(s_g1, 5 * b + 1)
            dve.wait_ge(s_de, 2 * b + 1)
            for h in range(HEADS):
                dve.tensor_scalar(dl[0:n_, h, 0:n_], bank(0, n_, n_)[:, h, :], col(1, h), 0.0, ALU.subtract, ALU.max)
            for h in range(HEADS):
                ins = dve.tensor_scalar(pt[0:n_, 4 * b + h, 0:n_], bank(0, n_, n_)[:, h, :], col(1, h), 0.0,
                                        ALU.subtract, ALU.min)
            ins.then_inc(s_dx, 1)
            dve.tensor_copy(ge[:, :, 2 * b:2 * b + n_ // CH],
                            ys[:, :, 0:n_].rearrange("p h (c t) -> p h c t", t=CH)[:, :, :, CH - 1])
            dve.tensor_tensor(qg[:, :, t0:t0 + n_], qkv[:, 0:4, t0:t0 + n_], ys[:, :, 0:n_],
                              ALU.mult).then_inc(s_dx, 1)
            dve.wait_ge(s_g1, 5 * b + 5)
            for h in range(HEADS):
                dve.tensor_scalar(kp[0:n_, h, :], bank(3, n_)[:, h, :], col(2, h), None, ALU.mult)
                dve.tensor_scalar(kd[0:n_, 4 * b + h, :], bank(3, n_)[:, h, :], col(3, h), None, ALU.mult)
                ins = dve.tensor_scalar(vp[0:n_, h, :], bank(4, n_)[:, h, :], col(0, h), None, ALU.mult)
            ins.then_inc(s_kv, 1)
            dve.wait_ge(s_de, 2 * b + 2)
            for h in range(HEADS):
                ins = dve.scalar_tensor_tensor(out=dl[0:n_, h, 0:n_], in0=bank(1, n_, n_)[:, h, :], scalar=col(0, h),
                                               in1=dl[0:n_, h, 0:n_], op0=ALU.mult, op1=ALU.mult)
            link(ins)
            mask = lambda m_: masks[0:n_, m_:m_ + 1, 0:n_].broadcast_to([n_, HEADS, n_])
            one = ident[0:n_, 0:n_].rearrange("p (a c) -> p a c", a=1).broadcast_to([n_, HEADS, n_])
            for lv in range(6):
                if lv:
                    dve.wait_ge(s_y, 6 * b + lv)
                dve.tensor_tensor(cm[0:n_, :, 0:n_], dl[0:n_, :, 0:n_], mask(lv), ALU.mult).then_inc(s_cm, 1)
                if lv == 0:
                    pts = pt[0:n_, 4 * b:4 * b + 4, 0:n_]
                    link(dve.tensor_tensor(pts, bank(2, n_, n_), pts, ALU.mult))
                    link(dve.tensor_tensor(pts, pts, mask(6), ALU.mult))
                    dve.wait_ge(s_cm, 6 * b + 1)
                    dve.wait_ge(s_y, 6 * b + 1)
                    dve.tensor_tensor(xi[0:n_, :, 0:n_], one, cm[0:n_, :, 0:n_], ALU.subtract)
                    dve.tensor_tensor(zi[0:n_, :, 0:n_], one, bank(5, n_, n_), ALU.subtract).then_inc(s_xz, 1)
                else:
                    dve.wait_ge(s_zx, 5 * b + lv)
                    if lv < 5:
                        dve.tensor_tensor(xi[0:n_, :, 0:n_], xi[0:n_, :, 0:n_], bank(7, n_, n_), ALU.subtract)
                    dve.tensor_tensor(zi[0:n_, :, 0:n_], zi[0:n_, :, 0:n_], bank(6, n_, n_),
                                      ALU.subtract).then_inc(s_xz, 1)
                dve.wait_ge(s_xz, 6 * b + lv + 1)

    def chunk(c):
        b = c // 2
        r0 = (c % 2) * CH
        return b, r0, 1 if c == 8 else 0

    def scan_tensor(pe):
        pe.wait_ge(s_bd, 5)
        for c in range(9):
            b, r0, s = chunk(c)
            tok = slice(c * CH, c * CH + CH)
            pe.wait_ge(s_st, c + 1)
            if c == 8:
                pe.wait_ge(s_s0, 16)
            for h in range(HEADS):
                m = pe.matmul(ps[r0:r0 + CH, c % 2, h * P:h * P + P], wt[:, 4 * b + h, r0:r0 + CH], st[:, s, h, :],
                              start=True, stop=True)
            m.then_inc(s_sw, 1)
            pe.wait_ge(s_su, c + 1)
            for h in range(HEADS):
                m = pe.matmul(bank(4 + c % 2)[:, h, :], kd[r0:r0 + CH, 4 * b + h, :], uu[r0:r0 + CH, c % 2, h, :],
                              start=True, stop=True)
            m.then_inc(s_ku, 1)
            if c >= 2:
                pe.wait_ge(s_oc, c - 1)
            for h in range(HEADS):
                out = ps[:, 2 + c % 2, h * CH:h * CH + CH]
                pe.matmul(out, st_old(c)[:, h, :], qg[:, h, tok], start=True, stop=False)
                m = pe.matmul(out, uu[r0:r0 + CH, c % 2, h, :], pt[r0:r0 + CH, 4 * b + h, r0:r0 + CH],
                              start=False, stop=True)
            m.then_inc(s_so, 1)

    def scan_vector(dve):
        dve.wait_ge(s_bd, 5)
        dve.memset(st[:, 0, :, :], 0.0).then_inc(s_st, 1)
        for c in range(9):
            b, r0, s = chunk(c)
            dve.wait_ge(s_sw, c + 1)
            if c >= 2:
                dve.wait_ge(s_so, c - 1)
            rows_ = slice(r0, r0 + CH)
            dve.tensor_tensor(uu[rows_, c % 2, :, :], uv[rows_, 4 * b:4 * b + 4, :],
                              ps[rows_, c % 2, :].rearrange("p (h c) -> p h c", h=HEADS), ALU.subtract).then_inc(s_su, 1)
            dve.wait_ge(s_ku, c + 1)
            dve.wait_ge(s_so, c + 1)
            for h in range(HEADS):
                ins = dve.scalar_tensor_tensor(out=st[:, s, h, :], in0=st[:, s, h, :], scalar=ge[:, h, c:c + 1],
                                               in1=bank(4 + c % 2)[:, h, :], op0=ALU.mult, op1=ALU.add)
            ins.then_inc(s_st, 1)
            if c == 7:
                dve.wait_ge(s_s0, 16)
            if c < 8:
                dve.wait_ge(s_st, c + 2)
        dve.wait_ge(s_st, 10)

    def st_old(c):
        return st[:, chunk(c)[2], :, :]

    def scan_scalar(act):
        for c in range(9):
            act.wait_ge(s_so, c + 1)
            if c == 0:
                act.wait_ge(s_bd, 5)
            act.activation(og[:, :, c * CH:c * CH + CH],
                           ps[:, 2 + c % 2, 0:HEADS * CH].rearrange("p (h t) -> p h t", h=HEADS),
                           ACT.Copy).then_inc(s_oc, 1)

    def onorm_scalar(act):
        act.activation(zg[:, :, :], zg[:, :, :], ACT.Silu).then_inc(s_zs, 1)
        act.wait_ge(s_oc, 9)
        for h in range(HEADS):
            if h >= 2:
                act.wait_ge(s_nss, 11 + h - 1)
            act.activation(sqm[:, h % 2, :], og[:, h, :], ACT.Square).then_inc(s_nsq, 1)
        act.wait_ge(s_nss, 15)
        act.activation(halves(rows[0:4, :]), pair(0)[0:4], ACT.Sqrt, bias=cols[0:4, C_OEPS:C_OEPS + 1],
                       scale=1.0 / P).then_inc(s_nst, 1)
        for h in range(HEADS):
            act.wait_ge(s_zs, h + 2)
            if h == 0:
                act.wait_ge(s_out, 64)
            act.activation(u_hi[:, h, :], og[:, h, :], ACT.Copy).then_inc(s_oh, 1)

    def onorm_tensor(pe):
        pe.wait_ge(s_oc, 9)
        for h in range(HEADS):
            pe.wait_ge(s_nsq, 11 + h + 1)
            for a in range(2):
                m = pe.matmul(pair(0)[0:16, a, :], onecol[:, 15 - h:31 - h], halves(sqm[:, h % 2, :])[:, a, :],
                              start=h == 0, stop=h == 3)
            m.then_inc(s_nss, 1)
        pe.wait_ge(s_rn, 2)
        for h in range(HEADS):
            if h == 3:
                pe.wait_ge(s_ru, 11)
            for a in range(2):
                m = pe.matmul(pair(1 + h % 3)[:, a, :], ident[0:4, h:h + 1].broadcast_to([4, P]),
                              halves(t1[0:4, :])[:, a, :], start=True, stop=True)
            m.then_inc(s_rb, 1)

    def onorm_vector(dve):
        dve.wait_ge(s_nst, 2)
        dve.reciprocal(t1[0:4, :], rows[0:4, :]).then_inc(s_rn, 1)
        dve.wait_ge(s_zs, 1)
        for h in range(HEADS):
            dve.wait_ge(s_rb, 10 + h + 1)
            dve.scalar_tensor_tensor(out=halves(og[:, h, :]), in0=halves(og[:, h, :]),
                                     scalar=cols[:, C_NORMW:C_NORMW + 1], in1=pair(1 + h % 3),
                                     op0=ALU.mult, op1=ALU.mult).then_inc(s_ru, 1)
            dve.wait_ge(s_ru, 10 + h + 1)
            dve.tensor_tensor(og[:, h, :], og[:, h, :], zg[:, h, :], ALU.mult).then_inc(s_zs, 1)
            dve.wait_ge(s_zs, h + 2)
            dve.wait_ge(s_oh, h + 1)
            dve.tensor_tensor(u_lo[:, h, :], og[:, h, :], u_hi[:, h, :].bitcast(F32), ALU.subtract).then_inc(s_ol, 1)

    s_ch = sem("latent_hi_ready")
    s_cl = sem("latent_parts_ready")
    s_mp = sem("latent_product_done")
    s_me = sem("latent_product_copied")
    s_rope = sem("rotary_tables_loaded")
    s_rp = sem("rotary_swapped")
    s_kr = sem("rotary_applied")
    s_sc = sem("scores_ready")
    s_mx = sem("row_maximum_ready")
    s_sx = sem("exponentials_ready")
    s_pn = sem("probabilities_ready")
    s_tp = sem("probabilities_turned")
    s_pc = sem("probabilities_copied")
    s_pv = sem("values_weighted")
    g_mla = first["mla"]
    UNITS = [(h, qb * P, P, 0, (qb + 1) * P) for qb in range(4) for h in range(HEADS)]
    UNITS += [(h, SEQ, DEC, SEQ, DEC + PAST) for h in range(HEADS)]
    NU = len(UNITS)

    def mla_gpsimd(pool):
        pool.wait_ge(s_out, 64)
        pool.dma_start(kr[:, TOKENS:KEYS], i["cache_rope"]).then_inc(s_rope, 16)
        pool.wait_ge(s_zs, 5)
        pool.dma_start(rope[:, :, :], i["rope"]).then_inc(s_rope, 16)
        pool.dma_start(o["latent"], ckv[:, 0:TOKENS]).then_inc(s_out, 16)
        pool.wait_ge(s_kr, 3)
        pool.dma_start(o["krope"], kr[0:64, 0:TOKENS]).then_inc(s_out, 16)
        pool.wait_ge(s_out, 96)

    def mla_tensor(pe):
        pe.wait_ge(s_cl, 3)
        pe.wait_ge(s_ru, 14)
        pe.wait_ge(s_wlo, g_mla + 1)
        wq = [w[:, 0, 0:1536].rearrange("p (k m c) -> p k m c", k=2, m=6) for w in (w_hi, w_lo)]
        for m_ in range(6):
            if m_ >= 4:
                pe.wait_ge(s_me, m_ - 3)
            for k in range(2):
                mm = three(pe, pair(m_ % 4), wq[0][:, k, m_, :], wq[1][:, k, m_, :],
                           halves(cq_hi[:, k, :]), halves(cq_lo[:, k, :]), k == 0, k == 1)
            mm.then_inc(s_mp if m_ < 5 else s_blk, 1)
        pe.wait_ge(s_wlo, g_mla + 2)
        pe.wait_ge(s_evac, g_mla + 1)
        wkv = [w[:, 1, 0:1024] for w in (w_hi, w_lo)]
        kh = [t.rearrange("p (a t) -> p a t", a=2) for t in (ck_hi[:, :], ck_lo[:, :])]
        for h in range(HEADS):
            mm = three(pe, ps[:, 2 * h:2 * h + 2, 0:KPAD // 2], wkv[0][:, h * P:h * P + P], wkv[1][:, h * P:h * P + P],
                       kh[0], kh[1], True, True)
            mm.then_inc(s_mp, 1)
        for t in range(7):
            pe.wait_ge(s_me, 6 + t // 2)
            for n_, (a, b) in enumerate(((ck_hi, 0), (ck_hi, 1), (ck_lo, 0))):
                mm = pe.matmul(ps[:, t, :], a[:, t * P:t * P + P], wkv[b][:, 512:1024], start=n_ == 0, stop=n_ == 2)
            mm.then_inc(s_mp if t < 6 else s_blk, 1)
        pe.wait_ge(s_evac, g_mla + 2)
        for n_, (w, src) in enumerate(((swap[:, 0, :], qr[:, 0, :]), (swap[:, 0, :], qr[:, 1, :]),
                                       (swap[0:64, 1, :], misc[0:64, :]), (swap[0:64, 2, :], misc[0:64, :]))):
            for a in range(2):
                mm = pe.matmul(pair(n_)[:, a, :], w, halves(src)[:, a, :], start=True, stop=True)
            mm.then_inc(s_rp, 1)
        pe.wait_ge(s_kr, 3)
        for n in range(NU + 2):
            if n < NU:
                h, q0, nq, k0, nk = UNITS[n]
                p0 = (h % 2) * 64
                if n >= 2:
                    pe.wait_ge(s_sx, n - 1)
                out = ps[0:nq, n % 2, 0:nk]
                pe.matmul(out, qn[:, h, q0:q0 + nq], kn[:, h, k0:k0 + nk], start=True, stop=False)
                pe.matmul(out, qr[p0:p0 + 64, h // 2, q0:q0 + nq], kr[p0:p0 + 64, k0:k0 + nk],
                          start=False, stop=True).then_inc(s_sc, 1)
            if 2 <= n:
                u = n - 2
                h, q0, nq, k0, nk = UNITS[u]
                pe.wait_ge(s_pc, u + 1)
                if u % 4 == 0 and u >= 8:
                    pe.wait_ge(s_ol, 4 + u // 4 - 1)
                for t in range(-(-nk // P)):
                    w = min(P, nk - t * P)
                    mm = pe.matmul(ps[:, 4 + (u // 4) % 2, h * nq:h * nq + nq], vt[0:w, k0 // P + t, h * P:h * P + P],
                                   ppt[0:w, u % 2, t, 0:nq], start=t == 0, stop=(t + 1) * P >= nk)
                mm.then_inc(s_pv, 1)
            if 1 <= n <= NU:
                u = n - 1
                h, q0, nq, k0, nk = UNITS[u]
                pe.wait_ge(s_pn, u + 1)
                if u >= 2:
                    pe.wait_ge(s_pc, u - 1)
                for t in range(-(-nk // P)):
                    w = min(P, nk - t * P)
                    mm = pe.transpose(ps[0:w, 2 + u % 2, t * P:t * P + nq], pp[0:nq, u % 2, t * P:t * P + w],
                                      ident[0:nq, 0:nq])
                mm.then_inc(s_tp, 1)

    def mla_scalar(act):
        act.wait_ge(s_so, 9)
        act.wait_ge(s_ru, 10)
        act.wait_ge(s_mk, 16)
        for m_ in range(2):
            act.activation(cq_hi[:, m_, :], qa[:, m_, :], ACT.Copy).then_inc(s_ch, 1)
        act.activation(ck_hi[:, :], ckv[:, :], ACT.Copy).then_inc(s_ch, 1)
        for m_ in range(6):
            act.wait_ge(s_mp if m_ < 5 else s_blk, m_ + 1 if m_ < 5 else g_mla + 1)
            dst = qn[:, m_, :] if m_ < 4 else qr[:, m_ - 4, :]
            act.activation(halves(dst), pair(m_ % 4), ACT.Copy).then_inc(s_me if m_ < 5 else s_evac, 1)
        split_hi(act, g_mla + 2, 0, 0)
        for h in range(HEADS):
            act.wait_ge(s_mp, 6 + h)
            act.activation(kn[:, h, :].rearrange("p (a t) -> p a t", a=2), ps[:, 2 * h:2 * h + 2, 0:KPAD // 2],
                           ACT.Copy).then_inc(s_me, 1)
        act.wait_ge(s_ol, 4)
        for t in range(7):
            act.wait_ge(s_mp if t < 6 else s_blk, 10 + t if t < 6 else g_mla + 2)
            act.activation(vt[:, t, :], ps[:, t, :], ACT.Copy).then_inc(s_me if t < 6 else s_evac, 1)
        split_hi(act, g_mla + 2, 1, 0)
        for n in range(NU + 2):
            if n < NU:
                h, q0, nq, k0, nk = UNITS[n]
                act.wait_ge(s_mx, n + 1)
                if n >= 2:
                    act.wait_ge(s_tp, n - 1)
                act.activation(pp[0:nq, n % 2, 0:nk], ps[0:nq, n % 2, 0:nk], ACT.Exp, bias=sm[0:nq, 1, n:n + 1],
                               scale=MLA_SCALE, accum_out=sm[0:nq, 2, n:n + 1]).then_inc(s_sx, 1)
            if 1 <= n <= NU:
                u = n - 1
                h, q0, nq, k0, nk = UNITS[u]
                act.wait_ge(s_tp, u + 1)
                if u >= 2:
                    act.wait_ge(s_pv, u - 1)
                full = nk // P
                src = ps[:, 2 + u % 2, :].rearrange("p (t c) -> p t c", c=P)
                ins = act.activation(ppt[:, u % 2, 0:full, 0:nq], src[:, 0:full, 0:nq], ACT.Copy)
                if nk % P:
                    ins = act.activation(ppt[0:nk % P, u % 2, full, 0:nq], src[0:nk % P, full, 0:nq], ACT.Copy)
                ins.then_inc(s_pc, 1)
            if n >= 2 and n % 4 == 1:
                h, q0, nq, k0, nk = UNITS[n - 2]
                gi = (n - 2) // 4
                act.wait_ge(s_pv, n - 1)
                act.activation(u_hi[:, 4:8, q0:q0 + nq],
                               ps[:, 4 + gi % 2, 0:HEADS * nq].rearrange("p (h t) -> p h t", h=HEADS),
                               ACT.Copy).then_inc(s_oh, 1)

    def mla_vector(dve):
        link = chains["dve"].step
        for m_ in range(2):
            dve.wait_ge(s_ch, m_ + 1)
            dve.tensor_tensor(cq_lo[:, m_, :], qa[:, m_, :], cq_hi[:, m_, :].bitcast(F32),
                              ALU.subtract).then_inc(s_cl, 1)
        dve.wait_ge(s_ch, 3)
        dve.tensor_tensor(ck_lo[:, :], ckv[:, :], ck_hi[:, :].bitcast(F32), ALU.subtract).then_inc(s_cl, 1)
        dve.wait_ge(s_blk, g_mla + 1)
        split_lo(dve, g_mla + 2, 0, 0)
        dve.wait_ge(s_blk, g_mla + 2)
        split_lo(dve, g_mla + 2, 1, 0)
        dve.wait_ge(s_rope, 32)
        for j in range(2):
            dve.wait_ge(s_rp, j + 1)
            link(dve.tensor_tensor(halves(rtmp[:, :]), pair(j), halves(rope[:, 1, :]), ALU.mult))
            link(dve.tensor_tensor(qr[:, j, :], qr[:, j, :], rope[:, 0, :], ALU.mult))
            dve.tensor_tensor(qr[:, j, :], qr[:, j, :], rtmp[:, :], ALU.add).then_inc(s_kr, 1)
            dve.wait_ge(s_kr, j + 1)
        dve.wait_ge(s_rp, 4)
        link(dve.tensor_tensor(halves(kr[:, 0:TOKENS]), pair(2), halves(rope[:, 0, :]), ALU.mult))
        link(dve.tensor_tensor(halves(rtmp[:, :]), pair(3), halves(rope[:, 1, :]), ALU.mult))
        dve.tensor_tensor(kr[:, 0:TOKENS], kr[:, 0:TOKENS], rtmp[:, :], ALU.add).then_inc(s_kr, 1)
        for n in range(NU + 2):
            if n < NU:
                h, q0, nq, k0, nk = UNITS[n]
                dve.wait_ge(s_sc, n + 1)
                if q0 < SEQ:
                    link(dve.memset(ps[0:CH, n % 2, nk - CH:nk], -1e30))
                link(dve.tensor_reduce(sm[0:nq, 0, n:n + 1], ps[0:nq, n % 2, 0:nk], AX.X, ALU.max))
                dve.tensor_scalar(sm[0:nq, 1, n:n + 1], sm[0:nq, 0, n:n + 1], -MLA_SCALE, None,
                                  ALU.mult).then_inc(s_mx, 1)
            if 1 <= n <= NU:
                u = n - 1
                h, q0, nq, k0, nk = UNITS[u]
                dve.wait_ge(s_sx, u + 1)
                link(dve.reciprocal(sm[0:nq, 3, u:u + 1], sm[0:nq, 2, u:u + 1]))
                dve.tensor_scalar(pp[0:nq, u % 2, 0:nk], pp[0:nq, u % 2, 0:nk], sm[0:nq, 3, u:u + 1], None,
                                  ALU.mult).then_inc(s_pn, 1)
            if n >= 2 and n % 4 == 1:
                h, q0, nq, k0, nk = UNITS[n - 2]
                gi = (n - 2) // 4
                dve.wait_ge(s_oh, 4 + gi + 1)
                dve.tensor_tensor(u_lo[:, 4:8, q0:q0 + nq],
                                  ps[:, 4 + gi % 2, 0:HEADS * nq].rearrange("p (h t) -> p h t", h=HEADS),
                                  u_hi[:, 4:8, q0:q0 + nq].bitcast(F32), ALU.subtract).then_inc(s_ol, 1)

    def mix_tensor(pe):
        body, count = product(pe, "mix_in", 2, KD, u_hi, u_lo)
        pe.wait_ge(s_u, 2 * KD)
        blocks_loop(pe, count, body)
        norms_tensor(pe)
        gdn_tensor(pe)
        scan_tensor(pe)
        onorm_tensor(pe)
        mla_tensor(pe)
        pe.wait_ge(s_ol, 9)
        body, count = product(pe, "mix_out", 2, KD, u_hi, u_lo)
        blocks_loop(pe, count, body)

    def out_scalar(act, name):
        g0 = first[name]

        def body(i, r, _):
            act.wait_ge(s_blk, g0 + r + 1 + 2 * i)
            split_hi(act, g0 + 2, r, i)
        blocks_loop(act, 4, body)

    def mix_scalar(act):
        act.wait_ge(s_ada_t, 4 * UNITS0)
        mix_in_scalar(act)
        norms_scalar(act)
        gdn_scalar(act)
        scan_scalar(act)
        onorm_scalar(act)
        mla_scalar(act)
        out_scalar(act, "mix_out")

    def mix_vector(dve):
        dve.wait_ge(s_ada_t, 4 * UNITS0)
        mix_in_vector(dve)
        norms_vector(dve)
        gdn_vector(dve)
        scan_vector(dve)
        onorm_vector(dve)
        mla_vector(dve)
        gate_vector(dve, 1)
        residual_vector(dve, "mix_out", 1, 2)
        dve.wait_ge(s_out, 96)

    rp = Region(U0, A0)
    rot = rp("rot", [P, 2, PAIRS, NC])
    rho = rp("rho", [P, PAIRS, NC])
    pw = rp("pw", [P, 2, PAIRS, 17])
    bb = rp("bb", [P, 2, PAIRS, 16])
    rq = Region(A0 + KD * TOKENS * 4, W0)
    eb = rq("eb", [P, 2, 2, 4, P])
    u3 = rq("u3", [P, 2, 8, P])
    u2 = rq("u2", [P, 2, 8, NC])
    hb = rq("hb", [P, 2, SUB, P])
    c_par = rq("c_par", [P, 2, PAIRS, 16])
    bp = rq("bp", [P, 2, 2, 4, 32])
    d_skip = rq("d_skip", [P, KD])
    rs = Region(E1, TOP)
    be = rs("be", [P, 2, 2, 4, P])
    wm = rs("wm", [P, 2, 2, 4, 9, 16])
    xx = rs("xx", [P, 2, 2, 4, NC + 1])
    y3 = rs("y3", [P, 2, SUB, P])
    ta, tb = (rs(n, [P, 4 * 9 * 16]) for n in ("ta", "tb"))
    bz = rs("bz", [P, 2, 4, NC])
    zz = rs("zz", [P, 2, 4, NC])
    par = rs("par", [P, 6, PAIRS])
    sc = rs("sc", [P, 8, PAIRS])
    ah = rs("ah", [P, 2, PAIRS])
    fin = rs("fin", [P, 2, 2, PAIRS])
    steps = nc.alloc_sbuf_tensor_at("steps", [P, 17 + NC], F32, offset=E1)
    b_par = nc.alloc_sbuf_tensor_at("b_par", [P, 2, PAIRS, 16], F32, offset=E1 + 512)
    bda = nc.alloc_sbuf_tensor_at("blockdiag", [P, P], F32, offset=rs.at)
    rs.at += 512
    assert rs.at <= TOP
    ang = nc.alloc_sbuf_tensor_at("ang", [P, PAIRS * NC], F32, offset=E1 + 8192)
    rnd = nc.alloc_sbuf_tensor_at("rnd", [P, PAIRS * NC], F32, offset=E1 + 8192 + 9216)

    s_par = sem("s5_parameters_loaded")
    s_pa = sem("s5_parameter_scalar")
    s_pv5 = sem("s5_parameter_vector")
    s_be = sem("s5_end_matrix_ready")
    s_w5 = sem("s5_output_matrix_ready")
    s_t3 = sem("s5_frames_turned")
    s_u3 = sem("s5_frames_copied")
    s_et = sem("s5_end_matrix_turned")
    s_eb = sem("s5_end_matrix_copied")
    s_t2 = sem("s5_frames_regrouped")
    s_u2 = sem("s5_frames_regrouped_copied")
    s_e5 = sem("s5_end_input_ready")
    s_ei = sem("s5_end_input_read")
    s_h5 = sem("s5_lags_ready")
    s_hb = sem("s5_lag_matrices_ready")
    s_x5 = sem("s5_states_ready")
    s_t4 = sem("s5_state_output_ready")
    s_y3 = sem("s5_state_output_copied")
    s_y5 = sem("s5_output_ready")
    s_ys5 = sem("s5_output_summed")
    s_yg = sem("s5_gelu_ready")
    s_yl = sem("s5_gelu_parts_ready")
    s_gs = sem("glu_sigmoid_ready")
    s_gh = sem("glu_hi_ready")
    s_gl = sem("glu_ready")
    s_s5v = sem("s5_vector_step")

    def s5_sync(sp):
        for name in ("glu", "s5_out"):
            stream_load(sp, name, BLOCK, lambda b: i["w_" + name][b, :, :] if isinstance(b, int) else
                        i["w_" + name][bass.ds(b, 1), :, :].rearrange("a p c -> (a p) c"))

    def s5_gpsimd(pool):
        pool.wait_ge(s_ada_t, 4 * ADA_UNITS)
        pool.wait_ge(s_uf, 5 * KD)
        for dst, src in ((par[:, 0:5, :], i["s5_par"]), (b_par[:, :, :, :], i["s5_b"]), (c_par[:, :, :, :], i["s5_c"]),
                         (d_skip[:, :], i["s5_d"]), (steps[:, :], i["steps"]), (bda[:, :], i["blockdiag"])):
            pool.dma_start(dst, src).then_inc(s_par, 16)
        pool.wait_ge(s_x5, KD)
        for n, k in enumerate(("s5_p", "s5_s")):
            pool.dma_start(o[k], fin[:, n, :, :]).then_inc(s_out, 16)

    def s5_parameters_vector(dve):
        link = Chain(dve, s_s5v).step
        dve.wait_ge(s_ada_t, 4 * ADA_UNITS)
        dve.wait_ge(s_par, 16 * 6)
        lr, li, ldt = par[:, 0, :], par[:, 1, :], par[:, 2, :]
        dt, lrdt, th, k1, cr, ci, den, t0 = (sc[:, n, :] for n in range(8))
        tt = lambda out, a, b, op: dve.tensor_tensor(out, a, b, op)
        dve.wait_ge(s_pa, 1)
        link(dve.tensor_scalar(lr, lr, -1e-4, None, ALU.min))
        link(tt(lrdt, lr, dt, ALU.mult))
        link(tt(th, li, dt, ALU.mult))

        C1 = 6.28125
        C2 = float(2 * np.pi - C1)
        BIG = 12582912.0

        def reduce_angle(a, r):
            link(dve.tensor_scalar(r, a, float(1 / (2 * np.pi)), BIG, ALU.mult, ALU.add))
            link(dve.tensor_scalar(r, r, BIG, None, ALU.subtract))
            link(dve.scalar_tensor_tensor(out=a, in0=r, scalar=-C1, in1=a, op0=ALU.mult, op1=ALU.add))
            link(dve.scalar_tensor_tensor(out=a, in0=r, scalar=-C2, in1=a, op0=ALU.mult, op1=ALU.add))
            link(dve.tensor_scalar(a, a, -3.1415925, 3.1415925, ALU.max, ALU.min))

        reduce_angle(th, t0)
        p3 = lambda t, w: t[:, 0:PAIRS * w].rearrange("p (q j) -> p q j", j=w)
        one = lambda v: v.rearrange("p (q j) -> p q j", j=1)
        row = lambda a, w: steps[:, a:a + w].rearrange("p (q j) -> p q j", q=1).broadcast_to([P, PAIRS, w])
        link(tt(p3(ang, 17), one(th).broadcast_to([P, PAIRS, 17]), row(0, 17), ALU.mult))
        link(tt(pw[:, 0, :, :], one(lrdt).broadcast_to([P, PAIRS, 17]), row(0, 17), ALU.mult))
        reduce_angle(ang[:, 0:PAIRS * 17], rnd[:, 0:PAIRS * 17])
        dve.tensor_copy(t0, p3(ang, 17)[:, :, 8]).then_inc(s_pv5, 1)
        dve.wait_ge(s_pa, 4)
        dve.wait_ge(s_pv5, 1)
        link(tt(pw[:, 1, :, :], pw[:, 1, :, :], pw[:, 0, :, :], ALU.mult))
        link(dve.tensor_copy(k1, pw[:, 0, :, 8]))
        link(tt(pw[:, 0, :, :], pw[:, 0, :, :], p3(rnd, 17), ALU.mult))
        link(dve.tensor_copy(rho[:, :, :], one(k1).broadcast_to([P, PAIRS, NC])))
        dve.memset(rho[:, :, 0:1], 0.0)
        link(dve.memset(rho[:, :, NCP:NCP + 1], 0.0))
        link(tt(p3(ang, NC), one(t0).broadcast_to([P, PAIRS, NC]), row(17, NC), ALU.mult))
        reduce_angle(ang[:, :], rnd[:, :])
        dve.nop().then_inc(s_pv5, 1)
        ar, ai = pw[:, 0, :, 1], pw[:, 1, :, 1]
        link(tt(den, lr, lr, ALU.mult))
        link(tt(k1, li, li, ALU.mult))
        link(tt(den, den, k1, ALU.add))
        link(dve.reciprocal(den, den))
        link(dve.tensor_scalar(t0, ar, -1.0, None, ALU.add))
        link(tt(cr, t0, lr, ALU.mult))
        link(tt(k1, ai, li, ALU.mult))
        link(tt(cr, cr, k1, ALU.add))
        link(tt(cr, cr, den, ALU.mult))
        link(tt(ci, ai, lr, ALU.mult))
        link(tt(k1, t0, li, ALU.mult))
        link(tt(ci, ci, k1, ALU.subtract))
        link(tt(ci, ci, den, ALU.mult))
        crb, cib = (one(v).broadcast_to([P, PAIRS, 16]) for v in (cr, ci))
        tq = hb[:, 0, 0:4, :].rearrange("p a (b c) -> p (a b) c", c=16)
        link(tt(bb[:, 0, :, :], b_par[:, 0, :, :], crb, ALU.mult))
        link(tt(tq, b_par[:, 1, :, :], cib, ALU.mult))
        link(tt(bb[:, 0, :, :], bb[:, 0, :, :], tq, ALU.subtract))
        link(tt(bb[:, 1, :, :], b_par[:, 1, :, :], crb, ALU.mult))
        link(tt(tq, b_par[:, 0, :, :], cib, ALU.mult))
        link(tt(bb[:, 1, :, :], bb[:, 1, :, :], tq, ALU.add))
        ar, ai, h_re, h_im = pw[:, 0, :, 8], pw[:, 1, :, 8], par[:, 3, :], par[:, 4, :]
        link(tt(ah[:, 0, :], ar, h_re, ALU.mult))
        link(tt(k1, ai, h_im, ALU.mult))
        link(tt(ah[:, 0, :], ah[:, 0, :], k1, ALU.subtract))
        link(tt(ah[:, 1, :], ar, h_im, ALU.mult))
        link(tt(k1, ai, h_re, ALU.mult))
        link(tt(ah[:, 1, :], ah[:, 1, :], k1, ALU.add))
        link(dve.memset(bp[:, :, :, :, :], 0.0))
        dve.wait_ge(s_pa, 6)
        return link

    def s5_parameters_scalar(act):
        act.wait_ge(s_par, 16 * 6)
        step = lambda ins, n_: (ins.then_inc(s_pa, 1), act.wait_ge(s_pa, n_))
        step(act.activation(sc[:, 0, :], par[:, 2, :], ACT.Exp), 1)
        act.wait_ge(s_pv5, 1)
        a17 = ang[:, 0:PAIRS * 17].rearrange("p (q j) -> p q j", j=17)
        r17 = rnd[:, 0:PAIRS * 17].rearrange("p (q j) -> p q j", j=17)
        act.activation(pw[:, 0, :, :], pw[:, 0, :, :], ACT.Exp)
        step(act.activation(pw[:, 1, :, :], a17, ACT.Sin), 2)
        step(act.activation(r17, a17, ACT.Abs), 3)
        step(act.activation(r17, r17, ACT.Sin, scale=-1.0, bias=cols[:, C_HPI:C_HPI + 1]), 4)
        act.wait_ge(s_pv5, 2)
        a72, r72 = (t[:, :].rearrange("p (q j) -> p q j", j=NC) for t in (ang, rnd))
        act.activation(rot[:, 1, :, :], a72, ACT.Sin)
        step(act.activation(r72, a72, ACT.Abs), 5)
        step(act.activation(rot[:, 0, :, :], r72, ACT.Sin, scale=-1.0, bias=cols[:, C_HPI:C_HPI + 1]), 6)

    def s5_vector(dve):
        link = s5_parameters_vector(dve)
        tt = lambda out, a, b, op: dve.tensor_tensor(out, a, b, op)

        def matrices(n):
            r, q = n % 2, slice(4 * n, 4 * n + 4)
            if n >= 2:
                dve.wait_ge(s_et, n - 1)
                dve.wait_ge(s_y5, n - 1)

            def outer(dst, p0, w, m, sub_first):
                pr, pi = (pw[:, z, q, p0:p0 + w].rearrange("p q (j b) -> p q j b", b=1).broadcast_to([P, 4, w, 16])
                          for z in range(2))
                mr, mi = (m[:, z, q, :].rearrange("p q (b c) -> p q b c", b=1).broadcast_to([P, 4, w, 16])
                          for z in range(2))
                v = lambda t: t[:, 0:4 * w * 16].rearrange("p (q j c) -> p q j c", q=4, j=w)
                d = [dst(z) for z in range(2)]
                tt(d[0], pr, mr, ALU.mult)
                tt(v(ta), pi, mi, ALU.mult)
                tt(v(tb), pr, mi, ALU.mult)
                link(tt(d[1], pi, mr, ALU.mult))
                if sub_first:
                    tt(d[0], d[0], v(ta), ALU.subtract)
                    return tt(d[1], d[1], v(tb), ALU.add)
                link(tt(d[0], d[0], v(ta), ALU.subtract))
                link(tt(v(tb), d[1], v(tb), ALU.add))
                return dve.tensor_scalar(d[1], v(tb), -1.0, None, ALU.mult)
            ins = outer(lambda z: be[:, r, z, :, :].rearrange("p q (j c) -> p q j c", c=16), 9, 8, bb, True)
            ins.then_inc(s_be, 1)
            dve.wait_ge(s_be, n + 1)
            for z in range(2):
                for half in range(2):
                    rows_ = slice(64 * half, 64 * half + 64)
                    dve.tensor_copy(bp[rows_, r, z, :, 16 * half:16 * half + 16], bb[rows_, z, q, :])
            ins = outer(lambda z: wm[:, r, z, :, :, :], 0, 9, c_par, False)
            ins.then_inc(s_w5, 1)
            dve.wait_ge(s_w5, n + 1)

        def lags(n):
            dve.wait_ge(s_h5, n + 1)
            if n >= 2:
                dve.wait_ge(s_y5, n - 1)
            src = ps[:, 0, 0:P].rearrange("p (j b c) -> p j b c", j=SUB, b=1).broadcast_to([P, SUB, 8, 16])
            m = bda[:, :].rearrange("p (a g c) -> p a g c", a=1, g=8).broadcast_to([P, SUB, 8, 16])
            tt(hb[:, n % 2, :, :].rearrange("p j (g c) -> p j g c", c=16), src, m, ALU.mult).then_inc(s_hb, 1)

        def states(n):
            r, q = n % 2, slice(4 * n, 4 * n + 4)
            co, si = rot[:, 0, q, :], rot[:, 1, q, :]
            t_a, t_b = (t[:, 0:4 * NC].rearrange("p (q c) -> p q c", q=4) for t in (ta, tb))
            e_re, e_im = (ps[:, 2 + z, 0:4 * NC].rearrange("p (q c) -> p q c", q=4) for z in range(2))
            dve.wait_ge(s_e5, n + 1)
            tt(bz[:, 0, :, :], e_re, co, ALU.mult)
            tt(t_a, e_im, si, ALU.mult)
            tt(bz[:, 1, :, :], e_im, co, ALU.mult)
            tt(t_b, e_re, si, ALU.mult).then_inc(s_ei, 1)
            dve.wait_ge(s_ei, n + 1)
            tt(bz[:, 0, :, :], bz[:, 0, :, :], t_a, ALU.add)
            link(tt(bz[:, 1, :, :], bz[:, 1, :, :], t_b, ALU.subtract))
            for z in range(2):
                ins = tt(bz[:, z, :, NCP], bz[:, z, :, NCP], ah[:, z, q], ALU.add)
            link(ins)
            for z in range(2):
                ins = dve.tensor_tensor_scan(zz[:, z, :, :].rearrange("p q c -> p (q c)"),
                                             rho[:, q, :].rearrange("p q c -> p (q c)"),
                                             bz[:, z, :, :].rearrange("p q c -> p (q c)"), 0.0, ALU.mult, ALU.add)
            link(ins)
            if n >= 2:
                dve.wait_ge(s_t4, n - 1)
            x_re, x_im = (xx[:, r, z, :, 1:NC + 1] for z in range(2))
            tt(x_re, zz[:, 0, :, :], co, ALU.mult)
            tt(t_a, zz[:, 1, :, :], si, ALU.mult)
            tt(x_im, zz[:, 1, :, :], co, ALU.mult)
            link(tt(t_b, zz[:, 0, :, :], si, ALU.mult))
            tt(x_re, x_re, t_a, ALU.subtract)
            link(tt(x_im, x_im, t_b, ALU.add))
            for z in range(2):
                dve.tensor_copy(fin[:, 0, z, q], xx[:, r, z, :, NCP])
                ins = dve.tensor_copy(fin[:, 1, z, q], xx[:, r, z, :, NC])
            link(ins)
            dve.memset(xx[:, r, :, :, 0:1], 0.0)
            for z in range(2):
                ins = dve.tensor_copy(xx[:, r, z, :, NCP], par[:, 3 + z, q])
            ins.then_inc(s_x5, 1)
            dve.wait_ge(s_x5, n + 1)

        def skip(n):
            dve.wait_ge(s_y5, n + 1)
            dve.scalar_tensor_tensor(out=halves(uf[:, n, :]), in0=halves(uf[:, n, :]), scalar=d_skip[:, n:n + 1],
                                     in1=pair(3), op0=ALU.mult, op1=ALU.add).then_inc(s_ys5, 1)

        matrices(0)
        for n in range(KD + 1):
            if n < KD:
                lags(n)
                states(n)
                if n + 1 < KD:
                    matrices(n + 1)
            if n >= 1:
                skip(n - 1)
        for k in range(KD):
            dve.wait_ge(s_yg, KD + k + 1)
            tt(u_lo[:, k, :], uf[:, k, :], u_hi[:, k, :].bitcast(F32), ALU.subtract).then_inc(s_yl, 1)
        g0 = first["glu"]
        for b in range(4):
            for m_ in range(2):
                k = 2 * b + m_
                dve.wait_ge(s_gs, k + 1)
                if m_ == 1:
                    dve.nop().then_inc(s_evac, 1)
                link(tt(hf[:, m_, :], sg[:, m_, :], uf[:, k, :], ALU.mult))
                dve.tensor_copy(glu_hi(k), hf[:, m_, :]).then_inc(s_gh, 1)
                dve.wait_ge(s_gh, k + 1)
                tt(h_lo[:, k, :], hf[:, m_, :], glu_hi(k).bitcast(F32), ALU.subtract).then_inc(s_gl, 1)
            dve.wait_ge(s_gl, 2 * b + 2)
            split_lo(dve, g0 + 2, b % 2, b // 2)
        gate_vector(dve, 4)
        residual_vector(dve, "s5_out", 4, 2)
        dve.wait_ge(s_out, 16 * STORES)

    def glu_hi(k):
        return h_hi[:, 8 + k, :] if k < 4 else h_lo[:, 4 + k, :]

    def s5_scalar(act):
        act.wait_ge(s_ada_t, 4 * ADA_UNITS)
        s5_parameters_scalar(act)
        for n in range(KD + 1):
            if n < KD:
                r = n % 2
                act.wait_ge(s_t3, n + 1)
                if n >= 2:
                    act.wait_ge(s_t2, n - 1)
                for a in range(2):
                    ins = act.activation(u3[0:NC, r, :, 64 * a:64 * a + 64].rearrange("p g (s m) -> p g s m", m=16),
                                         ps[0:NC, a, :].rearrange("p (s g m) -> p g s m", s=4, g=8), ACT.Copy)
                ins.then_inc(s_u3, 1)
                act.wait_ge(s_et, n + 1)
                if n >= 2:
                    act.wait_ge(s_e5, n - 1)
                act.activation(eb[:, r, :, :, :].rearrange("p z q c -> p z (q c)"), ps[:, 2:4, :],
                               ACT.Copy).then_inc(s_eb, 1)
                act.wait_ge(s_t2, n + 1)
                act.activation(u2[:, r, :, :].rearrange("p (a g) c -> p a (g c)", a=2), ps[:, 0:2, 0:4 * NC],
                               ACT.Copy).then_inc(s_u2, 1)
            if n >= 1:
                u = n - 1
                act.wait_ge(s_t4, u + 1)
                if u >= 2:
                    act.wait_ge(s_y5, u - 1)
                for a in range(2):
                    ins = act.activation(
                        y3[0:NC, u % 2, :, :].rearrange("p t (q a m) -> p t q a m", a=2, m=16)[:, :, :, a, :],
                        ps[0:NC, 4 + a, :].rearrange("p (q t m) -> p t q m", q=4, t=SUB), ACT.Copy)
                ins.then_inc(s_y3, 1)
                act.wait_ge(s_ys5, u + 1)
                act.activation(uf[:, u, :], uf[:, u, :], ACT.Gelu_apprx_tanh).then_inc(s_yg, 1)
        act.wait_ge(s_x5, KD)
        act.wait_ge(s_w5, KD)
        act.wait_ge(s_yg, KD)
        for k in range(KD):
            act.activation(u_hi[:, k, :], uf[:, k, :], ACT.Copy).then_inc(s_yg, 1)
        g0 = first["glu"]
        for b in range(4):
            act.wait_ge(s_blk, g0 + b + 1)
            for m_ in range(2):
                if b >= 1:
                    act.wait_ge(s_gl, 2 * b + m_ - 1)
                ins = act.activation(halves(sg[:, m_, :]), pair(2 * (b % 2) + m_), ACT.Sigmoid)
                ins.then_inc(s_gs, 1)
            act.wait_ge(s_gs, 2 * b + 2)
            split_hi(act, g0 + 2, b % 2, b // 2)
        out_scalar(act, "s5_out")

    def s5_tensor(pe):
        pe.wait_ge(s_uf, 5 * KD)
        pe.wait_ge(s_evac, first["glu"])
        for n in range(KD + 1):
            if n < KD:
                r = n % 2
                if n >= 1:
                    pe.wait_ge(s_hb, n)
                for s in range(SUB):
                    m = pe.transpose(ps[0:NC, s // 4, (s % 4) * P:(s % 4) * P + P],
                                     uf[:, n, :].rearrange("p (c s) -> p s c", s=SUB)[:, s, :], ident[:, :])
                m.then_inc(s_t3, 1)
                pe.wait_ge(s_be, n + 1)
                if n >= 1:
                    pe.wait_ge(s_ei, n)
                for z in range(2):
                    for q in range(4):
                        m = pe.transpose(ps[:, 2 + z, q * P:q * P + P], be[:, r, z, q, :], ident[:, :])
                m.then_inc(s_et, 1)
                pe.wait_ge(s_u3, n + 1)
                for g in range(8):
                    m = pe.transpose(ps[:, g // 4, (g % 4) * NC:(g % 4) * NC + NC],
                                     u3[0:NC, r, g, :], ident[0:NC, 0:NC])
                m.then_inc(s_t2, 1)
                pe.wait_ge(s_u2, n + 1)
                pe.wait_ge(s_eb, n + 1)
                for z in range(2):
                    for g in range(8):
                        q, half = g // 2, g % 2
                        m = pe.matmul(ps[64 * half:64 * half + 64, 2 + z, q * NC:q * NC + NC],
                                      eb[:, r, z, q, 64 * half:64 * half + 64], u2[:, r, g, :], start=True, stop=True)
                m.then_inc(s_e5, 1)
                pe.wait_ge(s_w5, n + 1)
                for q in range(4):
                    for z in range(2):
                        m = pe.matmul(ps[32 * q:32 * q + 32, 0, 0:P], bp[:, r, z, q, :],
                                      wm[:, r, z, q, 0:SUB, :].rearrange("p j c -> p (j c)"),
                                      start=z == 0, stop=z == 1)
                m.then_inc(s_h5, 1)
            if n >= 1:
                u = n - 1
                r = u % 2
                pe.wait_ge(s_x5, u + 1)
                if u >= 1:
                    pe.wait_ge(s_y3, u)
                for g in range(8):
                    q, rows_ = g // 2, slice(64 * (g % 2), 64 * (g % 2) + 64)
                    for z in range(2):
                        m = pe.matmul(ps[0:NC, 4 + g % 2, q * P:q * P + P], xx[rows_, r, z, q, 0:NC],
                                      wm[rows_, r, z, q, 1:9, :].rearrange("p j c -> p (j c)"),
                                      start=z == 0, stop=z == 1)
                m.then_inc(s_t4, 1)
                pe.wait_ge(s_hb, u + 1)
                if u >= 1:
                    pe.wait_ge(s_ys5, u)
                for a in range(2):
                    dst = ps[:, 6 + a, 0:HALF].rearrange("p (c t) -> p c t", t=SUB)
                    src = halves(uf[:, u, :])[:, a, :].rearrange("p (c t) -> p c t", t=SUB)
                    for j in range(SUB):
                        pe.matmul(dst[:, :, j:SUB], hb[:, r, j, :], src[:, :, 0:SUB - j], start=j == 0, stop=False)
                    if a == 0:
                        pe.wait_ge(s_y3, u + 1)
                    for s in range(SUB):
                        m = pe.matmul(dst[:, :, s], y3[0:NC, r, s, :], ident[0:NC, 36 * a:36 * a + 36],
                                      start=False, stop=s == SUB - 1)
                m.then_inc(s_y5, 1)
        pe.wait_ge(s_yl, KD)
        body, count = product(pe, "glu", 2, KD, u_hi, u_lo)
        blocks_loop(pe, count, body)
        pe.wait_ge(s_gl, KD)
        body, count = product(pe, "s5_out", 2, KD, glu_hi, lambda k: h_lo[:, k, :])
        blocks_loop(pe, count, body)
    constant_loads = [(ident[:, :], i["ident"]), (mean_w[:, :], i["mean_w"]), (masks[:, :, :], i["masks"]),
                      (swap[:, :, :], i["swap"]), (onecol[:, :], i["onecol"]), (b_ada[:, :, :], i["b_ada"]),
                      (ln_g[:, :, :], i["ln_g"]), (ln_b[:, :, :], i["ln_b"]), (cols[:, :], i["cols"])]

    chains = {}
    done = lambda name: first[name] + dict(STREAM)[name]
    block = stack.enter_context(nc.Block())

    @block.sync
    def _(sp):
        ada_sync(sp)
        ffn_sync(sp, 0)
        mix_sync(sp)
        ffn_sync(sp, 1)
        ffn_sync(sp, 2)
        s5_sync(sp)
        ffn_sync(sp, 3)

    @block.gpsimd
    def _(pool):
        ada_load(pool, 0, UNITS0)
        mix_gpsimd(pool)
        pool.wait_ge(s_ol, 9)
        pool.dma_start(c_act[:, :, :], i["c"]).then_inc(s_in2, 16)
        ada_load(pool, UNITS0, ADA_UNITS)
        s5_gpsimd(pool)
        for k in range(KD):
            pool.wait_ge(s_x, KD * (NMOD - 1) + k + 1)
            pool.dma_start(o["y"][:, k, :], x[:, k, :]).then_inc(s_out, 16)
        pool.wait_ge(s_out, 16 * (KD + STORES))

    @block.scalar
    def _(act):
        chains["act"] = Chain(act, s_act)
        act.dma_start(x[:, :, :], i["x"]).then_inc(s_cst, 16)
        for dst, src in constant_loads:
            act.dma_start(dst, src).then_inc(s_cst, 16)
        conditioning_scalar(act, s_in, False)
        for r in range(2):
            split_hi(act, 0, r, 0)
        u_scalar(act, 0)
        ffn_scalar(act, 0)
        ln_scalar(act, 0)
        mix_scalar(act)
        conditioning_scalar(act, s_in2, True)
        ln_scalar(act, 1)
        ffn_scalar(act, 1)
        ln_scalar(act, 2)
        ffn_scalar(act, 2)
        ln_scalar(act, 3)
        s5_scalar(act)
        ln_scalar(act, 4)
        ffn_scalar(act, 3)
        ln_scalar(act, 5)

    @block.vector
    def _(dve):
        chains["dve"] = Chain(dve, s_dve)
        ada_vector_first(dve)
        scale_vector(dve, 0)
        for r in range(2):
            split_lo(dve, 0, r, 0)
        for k in range(KD):
            u_tile(dve, 0, k)
            if k >= 1:
                u_low(dve, 0, k - 1)
        u_low(dve, 0, KD - 1)
        ffn_vector(dve, 0)
        ln_vector(dve, 0)
        mix_vector(dve)
        ln_vector(dve, 1)
        dve.wait_ge(s_ada_c, 2)
        ffn_vector(dve, 1)
        ln_vector(dve, 2)
        ffn_vector(dve, 2)
        ln_vector(dve, 3)
        s5_vector(dve)
        ln_vector(dve, 4)
        ffn_vector(dve, 3)
        ln_vector(dve, 5)

    @block.tensor
    def _(pe):
        ada_tensor_first(pe)
        ffn_tensor(pe, 0, KD)
        ln_tensor(pe, 0, done("out01"))
        mix_tensor(pe)
        ln_tensor(pe, 1, done("mix_out"))
        ffn_tensor(pe, 1, 3 * KD)
        ln_tensor(pe, 2, done("out11"))
        ffn_tensor(pe, 2, 4 * KD)
        ln_tensor(pe, 3, done("out21"))
        s5_tensor(pe)
        ln_tensor(pe, 4, done("s5_out"))
        ffn_tensor(pe, 3, 5 * KD)
        ln_tensor(pe, 5, done("out31"))

    stack.close()


def mixer_layout(a, n, tiles):
    w = n["w_mix_in"][0]
    z = lambda c: np.zeros((D, c), np.float32)
    w = np.concatenate([w[:, 0:2048], w[:, 2056:2312], w[:, 2312:2440], w[:, 2440:2504], w[:, 2048:2052], z(28),
                        w[:, 2052:2056], z(28)], axis=1)
    a["w_mix_in"] = tiles(w, 2, KD)
    qb = n["mla_w_q_b"][0].reshape(256, HEADS, 192)
    qb = np.concatenate([qb[:, :, 0:128].reshape(256, 512), qb[:, :, 128:].reshape(256, 256)], axis=1)
    a["w_q_b"] = tiles(qb, 6, 2)[0]
    kb = n["mla_w_kv_b"][0].reshape(128, HEADS, 256)
    a["w_kv_b"] = np.ascontiguousarray(np.concatenate([kb[:, :, 0:128].reshape(128, 512),
                                                       kb[:, :, 128:].reshape(128, 512)], axis=1))
    a["w_mix_out"] = tiles(n["w_mix_out"][0], 2, KD)
    a["conv_state"] = np.ascontiguousarray(n["state_gdn_conv"][0, 0].reshape(3, QT, P).transpose(2, 1, 0))
    a["gdn_state"] = np.ascontiguousarray(n["state_gdn"][0, 0].transpose(1, 0, 2))
    a["cache_latent"] = np.ascontiguousarray(n["cache_mla_latent"][0, 0].T)
    kt = n["cache_mla_krope"][0, 0].T
    a["cache_rope"] = np.concatenate([kt, kt])
    for k, src in (("w_glu", "s5_w_glu"), ("w_s5_out", "s5_w_out")):
        a[k] = tiles(n[src][0], 2, KD)
    two = lambda v: v.reshape(PAIRS, P, *v.shape[2:]).swapaxes(0, 1)
    a["s5_par"] = np.stack([two(v) for v in (n["s5_lambda_re"][0], n["s5_lambda_im"][0],
                                             np.repeat(n["s5_log_dt"][0][:, None], 64, axis=1),
                                             n["state_s5_re"][0, 0], n["state_s5_im"][0, 0])], axis=1)
    a["s5_b"] = np.stack([two(n["s5_b_re"][0]), two(n["s5_b_im"][0])], axis=1)
    a["s5_c"] = np.stack([two(n[k][0].swapaxes(1, 2)) for k in ("s5_c_re", "s5_c_im")], axis=1)
    a["s5_d"] = np.ascontiguousarray(n["s5_d"][0].reshape(KD, P).T)
    cols = np.zeros((P, NCOLS), np.float32)
    cols[:, C_EPS] = EPS / ALPHA ** 2
    cols[:, C_CONV:C_CONV + 48] = n["gdn_conv_w"][0].reshape(CONV, QT, P).transpose(2, 1, 0).reshape(P, 48)
    cols[:, C_NORMW] = n["gdn_norm_w"][0]
    cols[:, C_QN:C_QN + 2] = n["mla_q_norm"][0].reshape(2, P).T
    cols[:, C_KVN] = n["mla_kv_norm"][0]
    cols[96:100, C_DT] = n["gdn_dt_bias"][0]
    cols[0:4, C_ALOG] = n["gdn_a_log"][0]
    cols[0:10, C_RNS] = [128.0] * 4 + [1.0] * 4 + [1.0 / 256, 1.0 / 128]
    cols[0:10, C_RNB] = [128.0 * EPS] * 4 + [EPS] * 6
    cols[:, C_OEPS] = EPS
    cols[:, C_HPI] = np.pi / 2
    a["cols"] = cols


def returned(r):
    y = r["y"].transpose(1, 0, 2).reshape(D, TOKENS).T
    conv = {s: r["conv_" + s].transpose(2, 1, 0).reshape(1, 1, 3, QT * P) for s in "ps"}
    gdn = {s: r["gdn_" + s].transpose(1, 0, 2)[None, None] for s in "ps"}
    lat, kr = r["latent"].T, r["krope"].T
    s5 = {s: [r["s5_" + s][:, z, :].T.reshape(1, 1, 64, 64) for z in range(2)] for s in "ps"}
    return (y[None, :SEQ], y[None, SEQ:], lat[None, None, :SEQ], kr[None, None, :SEQ], gdn["p"], conv["p"],
            *s5["p"], lat[None, None, SEQ:], kr[None, None, SEQ:], gdn["s"], conv["s"], *s5["s"])


def shape_constants():
    from numpy import arange, eye, float32, zeros
    t, s = arange(P)[:, None], arange(P)[None, :]
    masks = zeros((P, 7, P), float32)
    for lv in range(6):
        b = 1 << lv
        masks[:, lv, :] = (t // (2 * b) == s // (2 * b)) & (t // b % 2 == 1) & (s // b % 2 == 0)
    masks[:, 6, :] = (t // CH == s // CH) & (t <= s)
    swap = zeros((P, 3, P), float32)
    swap[:, 0, :] = (t // 64 == s // 64) & (t % 64 == (s + 32) % 64)
    swap[:, 1, :] = (t < 64) & (t == s % 64)
    swap[:, 2, :] = (t < 64) & (t == (s + 32) % 64)
    onecol = zeros((P, 32), float32)
    onecol[:, 15] = 1.0
    half = 32
    inv = (np.float32(10000.0) ** (-arange(half, dtype=float32) / float32(half))).astype(float32)
    pos = np.concatenate([arange(SEQ), PAST + arange(DEC)]).astype(float32)
    ang = (pos[None, :] * inv[:, None]).astype(float32)
    cos, sin = np.cos(ang), np.sin(ang)
    rope = zeros((P, 2, TOKENS), float32)
    rope[:, 0] = np.concatenate([cos] * 4)
    rope[:, 1] = np.concatenate([-sin, sin] * 2)
    bd = zeros((P, 8, 16), float32)
    bd[:] = (arange(P)[:, None] // 16 == arange(8)[None, :])[:, :, None]
    steps = np.tile(np.concatenate([arange(9), arange(7, -1, -1), arange(NCP), arange(DEC // SUB)]).astype(float32),
                    (P, 1))
    return {"steps": steps, "ident": eye(P, dtype=float32), "mean_w": np.full((P, P), 1.0 / D, float32), "masks": masks,
            "swap": swap, "onecol": onecol, "rope": rope, "blockdiag": bd.reshape(P, P)}


def kernel(**inputs):
    import numpy as np
    import concourse.bacc as bacc
    from concourse.bass_utils import run_bass_kernel_spmd

    n = {k: np.asarray(v) for k, v in inputs.items()}
    feat = lambda a: np.ascontiguousarray(a.reshape(KD, P, -1).transpose(1, 0, 2))
    cat = lambda a, b: np.concatenate([a, b], axis=1)

    def tiles(w, per, kk):
        nb = w.shape[1] // (per * P)
        w = w.reshape(kk, P, nb, per, P).transpose(2, 1, 0, 3, 4)
        return np.ascontiguousarray(w.reshape(nb, P, kk * per * P))

    a = dict(shape_constants())
    a["x"] = feat(cat(n["x_prompt"][0].T, n["x_sample"][0].T))
    a["c"] = np.tile(np.stack([n["c_prompt"][0], n["c_sample"][0]])[None], (P, 1, 1))
    a["c_col"] = feat(np.stack([n["c_prompt"][0], n["c_sample"][0]], axis=1))
    a["w_ada0"] = np.ascontiguousarray(n["w_ada"][0, :, 0:D].reshape(KD, P, KD, P).transpose(1, 2, 0, 3))
    wa = n["w_ada"].transpose(0, 2, 1).reshape(18 * KD, P, D)[KD:]
    a["w_ada"] = np.ascontiguousarray(wa.transpose(1, 0, 2))
    a["b_ada"] = np.ascontiguousarray(n["b_ada"].reshape(3 * NMOD, KD, P).transpose(2, 0, 1))
    for k in ("ln_g", "ln_b"):
        a[k] = np.ascontiguousarray(n[k].reshape(NMOD, KD, P).transpose(2, 0, 1))
    w = n["w_ff_in"].reshape(4, KD, P, 2, FT, P).transpose(0, 4, 2, 1, 3, 5)
    a["w_in"] = np.ascontiguousarray(w.reshape(4, FT, P, BLOCK))
    w = n["w_ff_out"].reshape(4, FT, P, KD, P).transpose(0, 3, 2, 1, 4)
    for s, (j0, m) in enumerate(SEGS):
        a[f"w_out{s}"] = np.ascontiguousarray(w[:, :, :, j0:j0 + m]).reshape(4, KD, P, m * P)
    mixer_layout(a, n, tiles)

    nc = bacc.Bacc("TRN2", target_bir_lowering=False, num_devices=1)
    aps = {k: nc.dram_tensor(f"in_{k}", v.shape, mybir.dt.from_np(v.dtype), kind="ExternalInput").ap()
           for k, v in a.items()}
    outs = {k: nc.dram_tensor(f"out_{k}", s, F32, kind="ExternalOutput").ap() for k, s in OUTS.items()}
    trunk(nc, aps, outs)
    r = run_bass_kernel_spmd(nc, [{f"in_{k}": v for k, v in a.items()}], core_ids=[0]).results[0]
    r = {k: np.asarray(r[f"out_{k}"]) for k in OUTS}
    return returned(r)
```

```python
from contextlib import ExitStack

import numpy as np

import concourse.bass as bass
from concourse import mybir

F32 = mybir.dt.float32
F32R = mybir.dt.float32r
ALU = mybir.AluOpType
ACT = mybir.ActivationFunctionType
AX = mybir.AxisListType

P = 128
D = 1024
KD = D // P
SEQ, DEC = 512, 64
TOKENS = SEQ + DEC
HALF = TOKENS // 2
FT = 22
SEGS = ((0, 12), (12, 10))
HS = 12
ALPHA = (2.0 * 2) ** 0.25
EPS = 1e-6
BLOCK = 2048
CH = 64
PAST = 256
NMOD = 6
SQ = 4
UNITS0 = SEGS[0][1] + KD + SEGS[1][1]
ADA_UNITS = (3 * NMOD - 2) * KD // 2
ADA_IN = {(0, 0): 0, (0, 1): SEGS[0][1] + KD, (1, 0): UNITS0, (1, 1): UNITS0 + SEGS[0][1],
          (2, 0): UNITS0 + SEGS[0][1] + SEGS[1][1]}
assert ADA_IN[2, 0] + SEGS[0][1] == ADA_UNITS
HEADS = 4
SUB = 8
NC = TOKENS // SUB
NCP = SEQ // SUB
PAIRS = 32
CONV = 4
QT = 12
PADW = (CONV - 1) + SEQ + (CONV - 1) + DEC
KEYS = TOKENS + PAST
KPAD = 896
MLA_SCALE = float((128 + 64) ** -0.5)

C_EPS = 0
C_CONV = 1
C_NORMW = C_CONV + QT * CONV
C_QN = C_NORMW + 1
C_KVN = C_QN + 2
C_DT = C_KVN + 1
C_ALOG = C_DT + 1
C_RNS = C_ALOG + 1
C_RNB = C_RNS + 1
C_OEPS = C_RNB + 1
C_HPI = C_OEPS + 1
NCOLS = C_HPI + 1


def feed_forward_blocks(f):
    return tuple((f"{k}{f}{s}", c) for s, (_, n) in enumerate(SEGS) for k, c in (("in", n), ("out", KD)))


STREAM = (feed_forward_blocks(0) + (("mix_in", 10), ("mla", 2), ("mix_out", 4)) + feed_forward_blocks(1)
          + feed_forward_blocks(2) + (("glu", 4), ("s5_out", 4)) + feed_forward_blocks(3))
OUTS = {"y": (P, KD, TOKENS), "conv_p": (P, QT, 3), "conv_s": (P, QT, 3), "gdn_p": (P, HEADS, P),
        "gdn_s": (P, HEADS, P), "latent": (P, TOKENS), "krope": (64, TOKENS), "s5_p": (P, 2, PAIRS),
        "s5_s": (P, 2, PAIRS)}
STORES = 8
N_CONST = 9 + 1


def span(t, r):
    return t[..., 0:SEQ] if r == 0 else t[..., SEQ:TOKENS]


def halves(ap):
    return ap.rearrange("p (a t) -> p a t", a=2)


class Chain:

    def __init__(self, eng, sem):
        self.eng, self.sem, self.n = eng, sem, 0

    def step(self, ins):
        self.n += 1
        ins.then_inc(self.sem, 1)
        self.eng.wait_ge(self.sem, self.n)


def trunk(nc, i, o):
    stack = ExitStack()
    sem = lambda name: stack.enter_context(nc.semaphore(name))

    X0 = 16512
    U0 = X0 + KD * TOKENS * 4
    A0 = U0 + 2 * KD * TOKENS * 4
    W0 = A0 + 2 * HS * TOKENS * 4
    E0 = W0 + 6 * BLOCK * 4
    TOP = 229344

    class Region:
        def __init__(self, at, end):
            self.at, self.end = at, end

        def __call__(self, name, shape, dt=F32):
            words = 1
            for s in shape[1:]:
                words *= s
            t = nc.alloc_sbuf_tensor_at(name, shape, dt, offset=self.at)
            self.at += -(-words * 4 // 32) * 32
            assert self.at <= self.end, (name, self.at, self.end)
            return t

    x = Region(X0, U0)("x", [P, KD, TOKENS])
    ru = Region(U0, A0)
    u_hi, u_lo = (ru(n, [P, KD, TOKENS], F32R) for n in ("u_hi", "u_lo"))
    ra = Region(A0, W0)
    h_hi, h_lo = (ra(n, [P, HS, TOKENS], F32R) for n in ("h_hi", "h_lo"))
    rw = Region(W0, E0)
    w_raw = rw("w_raw", [P, 2, BLOCK])
    w_hi, w_lo = (rw(n, [P, 2, BLOCK], F32R) for n in ("w_hi", "w_lo"))
    re = Region(E0, TOP)
    ident = re("ident", [P, P])
    mean_w = re("mean_w", [P, P])
    masks = re("masks", [P, 7, P])
    swap = re("swap", [P, 3, P])
    onecol = re("onecol", [P, 32])
    mod = re("mod", [P, 3 * NMOD, KD, 2])
    c_col = re("c_col", [P, KD, 2])
    b_ada = re("b_ada_sb", [P, 3 * NMOD, KD])
    u_scale, u_shift, res_gate = (re(n, [P, NMOD, KD, 2]) for n in ("u_scale", "u_shift", "res_gate"))
    ln_g, ln_b = (re(n, [P, NMOD, KD]) for n in ("ln_g_sb", "ln_b_sb"))
    cols = re("cols", [P, NCOLS])
    E1 = re.at
    rt = Region(E1, TOP)
    sg, hf = (rt(n, [P, 2, TOKENS]) for n in ("sg", "hf"))
    c_act = rt("c_act", [P, 2, D])
    ada_w = rt("ada_w", [P, 2, 2, D])
    ada_out = rt("ada_out", [P, 2, D])
    rln = Region(A0, W0)
    uf = rln("uf", [P, KD, TOKENS])
    sq = rln("sq", [P, SQ, TOKENS])
    ln_std, ln_rstd = (rln(n, [P, TOKENS]) for n in ("ln_std", "ln_rstd"))
    ada_w0 = nc.alloc_sbuf_tensor_at("ada_w0", [P, KD, KD, P], F32, offset=U0)
    ada_w1 = nc.alloc_sbuf_tensor_at("ada_w1", [P, KD, D], F32, offset=A0)
    ps = nc.alloc_psum_tensor("ps", [P, 8, 512], F32)

    def pair(n):
        return ps[:, 2 * n:2 * n + 2, 0:HALF]

    s_in = sem("conditioning_loaded")
    s_in2 = sem("conditioning_loaded_again")
    s_cst = sem("constants_loaded")
    s_w0 = [sem(f"first_modulation_weights_{n}") for n in range(4)]
    s_w1 = [sem(f"second_modulation_weights_{n}") for n in range(4)]
    s_ada_w = [sem(f"modulation_weights_{n}") for n in range(2)]
    s_ada_c = sem("conditioning_ready")
    s_ada_t = sem("modulation_tile_summed")
    s_mod0 = sem("first_modulation_row_summed")
    s_mod1 = sem("second_modulation_row_summed")
    s_raw = [sem(f"weight_block_loaded_{n}") for n in range(2)]
    s_whi = sem("weight_hi_ready")
    s_wlo = sem("weight_lo_ready")
    s_blk = sem("block_product_done")
    s_evac = sem("block_banks_free")
    s_sg = sem("silu_ready")
    s_hh = sem("hidden_hi_ready")
    s_hl = sem("hidden_ready")
    s_mean = sem("ln_mean_ready")
    s_cen = sem("ln_centred")
    s_sq = sem("ln_square_ready")
    s_var = sem("ln_square_summed")
    s_std = sem("ln_std_ready")
    s_nrm = sem("ln_normed")
    s_uf = sem("u_prompt_modulated")
    s_us = sem("u_sample_modulated")
    s_sv = sem("u_scales_ready")
    s_uhi = sem("u_hi_ready")
    s_u = sem("u_ready_vector")
    s_up = sem("u_ready_gpsimd")
    s_x = sem("x_ready")
    s_dve = sem("vector_step")
    s_act = sem("scalar_step")
    s_out = sem("outputs_stored")

    first = {}
    n = 0
    for name, count in STREAM:
        first[name] = n
        n += count
    n_blocks = n

    def stream_load(sp, name, width, src, skip=0):
        g0 = first[name]
        count = dict(STREAM)[name]
        if skip:
            for r in range(2):
                sp.dma_start(w_raw[:, r, 0:width], src(r)).then_inc(s_raw[r], 16)
        if skip == count:
            return

        def body(i):
            for r in range(2):
                sp.wait_ge(s_wlo, g0 + 2 * i + r - 1)
                sp.dma_start(w_raw[:, r, 0:width], src(2 * i + r)).then_inc(s_raw[r], 16)

        if count - skip > 2:
            with sp.Fori(skip // 2, count // 2) as i:
                body(i)
        else:
            body(skip // 2)

    def split_hi(act, g0, r, i):
        act.wait_ge(s_raw[r], 16 * (g0 // 2 + 1) + 16 * i)
        act.activation(w_hi[:, r, :], w_raw[:, r, :], ACT.Copy).then_inc(s_whi, 1)

    def split_lo(dve, g0, r, i):
        dve.wait_ge(s_raw[r], 16 * (g0 // 2 + 1) + 16 * i)
        dve.wait_ge(s_whi, g0 + r + 1 + 2 * i)
        dve.tensor_tensor(w_lo[:, r, :], w_raw[:, r, :], w_hi[:, r, :].bitcast(F32),
                          ALU.subtract).then_inc(s_wlo, 1)

    def blocks_loop(eng, count, body, peel=0, start=0):
        whole = count // 2 - peel
        for i in range(start):
            for r in range(2):
                body(i, r, True)
        if whole - start > 1:
            with eng.Fori(start, whole) as i:
                for r in range(2):
                    body(i, r, True)
        elif whole - start == 1:
            for r in range(2):
                body(start, r, True)
        for i in range(whole, count // 2):
            for r in range(2):
                body(i, r, False)

    def three(pe, out, wh, wl, mh, ml, start, stop):
        m = None
        for n_, (w, mv) in enumerate(((wh, mh), (wh, ml), (wl, mh))):
            for a in range(2):
                m = pe.matmul(out[:, a, :], w, mv[:, a, :], start=start and n_ == 0, stop=stop and n_ == 2)
        return m

    def product(pe, name, tiles, kk, mov_hi, mov_lo, ready=None, ready_first=None, before=None):
        g0, count = first[name], dict(STREAM)[name]
        hi, lo = (t if callable(t) else (lambda k, t=t: t[:, k, :]) for t in (mov_hi, mov_lo))
        views = [(w[:, r, 0:kk * tiles * P].rearrange("p (k m c) -> p k m c", k=kk, m=tiles))
                 for r in range(2) for w in (w_hi, w_lo)]

        def body(i, r, _):
            pe.wait_ge(s_wlo, g0 + r + 1 + 2 * i)
            if g0 + r >= 2:
                pe.wait_ge(s_evac, g0 + r - 1 + 2 * i)
            elif not (isinstance(i, int) and i == 0):
                pe.wait_ge(s_evac, r + 2 * i - 1)
            if before is not None:
                before(i, r)
            for m_ in range(tiles):
                for k in range(kk):
                    if ready is not None and m_ == 0:
                        ready(k)
                    if ready_first is not None and m_ == 0 and r == 0 and isinstance(i, int) and i == 0:
                        ready_first(k)
                    mm = three(pe, pair(2 * r + m_), views[2 * r][:, k, m_, :], views[2 * r + 1][:, k, m_, :],
                               halves(hi(k)), halves(lo(k)), k == 0, k == kk - 1)
            mm.then_inc(s_blk, 1)
        return body, count

    def ffn_sync(sp, f):
        for s, (j0, n) in enumerate(SEGS):
            win = i["w_in"][f]
            stream_load(sp, f"in{f}{s}", BLOCK, lambda b: win[j0 + b, :, :] if isinstance(b, int) else
                        win[bass.ds(j0 + b, 1), :, :].rearrange("a p c -> (a p) c"),
                        skip=2 if f == 0 and s == 0 else 0)
            wout = i[f"w_out{s}"][f]
            stream_load(sp, f"out{f}{s}", n * P, lambda b: wout[b, :, :] if isinstance(b, int) else
                        wout[bass.ds(b, 1), :, :].rearrange("a p c -> (a p) c"))

    def ffn_tensor(pe, f):
        n_ln = (0, 2, 3, 5)[f]
        for s, (j0, n) in enumerate(SEGS):
            body, count = product(pe, f"in{f}{s}", 2, KD, u_hi, u_lo,
                                  ready_first=u_ready(pe, n_ln) if s == 0 else None)
            blocks_loop(pe, count, body, start=1 if s == 0 else 0)
            h0 = FT * f + j0
            body, count = product(pe, f"out{f}{s}", 1, n, h_hi, h_lo,
                                  ready=lambda k: pe.wait_ge(s_hl, h0 + (n - 2 if k == 0 else n))
                                  if k in (0, n - 2) else None, before=ln_early(pe) if s == 1 else None)
            blocks_loop(pe, count, body, start=2 if s == 1 else 0)

    def ffn_scalar(act, f):
        for s, (j0, n) in enumerate(SEGS):
            g0 = first[f"in{f}{s}"]

            def body(i, r, _):
                act.wait_ge(s_blk, g0 + r + 1 + 2 * i)
                act.activation(halves(sg[:, r, :]), pair(2 * r), ACT.Silu).then_inc(s_sg, 1)
                split_hi(act, g0 + 2, r, i)
            blocks_loop(act, n, body)
            g1 = first[f"out{f}{s}"]

            stages = s5_parameter_stages_scalar(act) if (f, s) == (2, 1) else {}

            def body(i, r, more):
                if more or g1 + 2 * i + r + 2 < n_blocks:
                    act.wait_ge(s_blk, g1 + r + 1 + 2 * i)
                    split_hi(act, g1 + 2, r, i)
                if stages and 2 * i + r in stages:
                    stages[2 * i + r]()
            blocks_loop(act, KD, body, peel=1, start=3 if stages else 0)

    def ffn_vector(dve, f):
        for s, (j0, n) in enumerate(SEGS):
            g0, h0 = first[f"in{f}{s}"], FT * f + j0

            def body(i, r, _):
                dve.wait_ge(s_sg, h0 + r + 1 + 2 * i)
                dve.tensor_tensor(halves(hf[:, r, :]), pair(2 * r + 1), halves(sg[:, r, :]),
                                  ALU.mult).then_inc(s_evac, 1)
                split_lo(dve, g0 + 2, r, i)
                slot = bass.ds(2 * i + r, 1) if not isinstance(i, int) else slice(2 * i + r, 2 * i + r + 1)
                dve.wait_ge(s_evac, g0 + r + 1 + 2 * i)
                dve.tensor_copy(h_hi[:, slot, :], hf[:, r:r + 1, :]).then_inc(s_hh, 1)
                dve.wait_ge(s_hh, h0 + r + 1 + 2 * i)
                dve.tensor_tensor(h_lo[:, slot, :], hf[:, r:r + 1, :], h_hi[:, slot, :].bitcast(F32),
                                  ALU.subtract).then_inc(s_hl, 1)
                dve.wait_ge(s_hl, h0 + r + 1 + 2 * i)
                if (f, s) in ADA_IN:
                    ada_unit(dve, ADA_IN[f, s], i, r)
            blocks_loop(dve, n, body, start=1 if (f, s) == (0, 0) else 0)
            if s == 0:
                gate_vector(dve, (0, 2, 3, 5)[f])
            residual_vector(dve, f"out{f}{s}", (0, 2, 3, 5)[f], 1)

    s5_link = []

    def residual_vector(dve, name, site, tiles):
        g1, count = first[name], dict(STREAM)[name]
        ends_sublayer = name[-1] != "0"
        stages = ()
        if name == "out21":
            link, stages = s5_parameter_stages_vector(dve)
            s5_link.append(link)

        def body(i, r, more):
            dve.wait_ge(s_blk, g1 + r + 1 + 2 * i)
            for m_ in range(tiles):
                for half in range(3):
                    a, lo, hi, st = ((0, 0, HALF, 0), (1, HALF, SEQ, 0), (1, SEQ, TOKENS, 1))[half]
                    k = (2 * i + r) * tiles + m_
                    ks = bass.ds(k, 1) if not isinstance(i, int) else slice(k, k + 1)
                    gate = res_gate[:, site, ks, st:st + 1].rearrange("p a b -> p (a b)")
                    ins = dve.scalar_tensor_tensor(
                        out=x[:, ks, lo:hi], in0=pair(2 * r + m_)[:, a:a + 1, lo - a * HALF:hi - a * HALF],
                        scalar=gate, in1=x[:, ks, lo:hi], op0=ALU.mult, op1=ALU.add)
            ins.then_inc(s_evac, 1)
            if more or (g1 + 2 * i + r + 2 < n_blocks and not (r == 1 and ends_sublayer)):
                split_lo(dve, g1 + 2, r, i)
            if name == "out00":
                ada_unit(dve, SEGS[0][1], i, r)
            if stages and 2 * i + r < len(stages):
                stages[2 * i + r]()
        blocks_loop(dve, count, body, peel=1, start=3 if stages else 0)
        dve.wait_ge(s_evac, g1 + count)

    def ln_banks(n):
        return (0, 1) if n in (1, 4) else (1, 3)

    def mean_tile(pe, n, k):
        ks = slice(k, k + 1) if isinstance(k, int) else bass.ds(k, 1)
        for a in range(2):
            m = pe.matmul(pair(ln_banks(n)[0])[:, a, :], mean_w[:, :],
                          x[:, ks, a * HALF:a * HALF + HALF].rearrange("p a t -> p (a t)"),
                          start=isinstance(k, int) and k == 0, stop=isinstance(k, int) and k == KD - 1)
        return m

    def ln_early(pe):
        def before(i, r):
            if not isinstance(i, int) or i > 0:
                mean_tile(pe, 0, 2 * i + r - 2)
        return before

    def ln_tensor(pe, n, done):
        late = range(KD) if n in (1, 4) else range(KD - 2, KD)
        for k in late:
            pe.wait_ge(s_evac, done - (k < KD - 1 and len(late) == 2))
            m = mean_tile(pe, n, k)
        m.then_inc(s_mean, 1)
        for k in range(KD):
            pe.wait_ge(s_sq, KD * n + k + 1)
            for a in range(2):
                m = pe.matmul(pair(ln_banks(n)[1])[:, a, :], mean_w[:, :], halves(sq[:, k % SQ, :])[:, a, :],
                              start=k == 0, stop=k == KD - 1)
            m.then_inc(s_var, 1)

    def ln_scalar(act, n):
        for k in range(KD):
            act.wait_ge(s_cen, KD * n + k + 1)
            if k >= SQ:
                act.wait_ge(s_var, KD * n + k - SQ + 1)
            act.activation(sq[:, k % SQ, :], x[:, k, :], ACT.Square).then_inc(s_sq, 1)
        act.wait_ge(s_var, KD * (n + 1))
        act.activation(halves(ln_std[:, :]), pair(ln_banks(n)[1]), ACT.Sqrt,
                       bias=cols[:, C_EPS:C_EPS + 1]).then_inc(s_std, 1)
        if n < NMOD - 1:
            u_scalar(act, n + 1)
            return
        for k in range(KD):
            act.wait_ge(s_nrm, KD * n + k + 1)
            act.activation(x[:, k, :], x[:, k, :], ACT.Identity, scale=ln_g[:, n, k:k + 1],
                           bias=ln_b[:, n, k:k + 1]).then_inc(s_x, 1)

    def u_scalar(act, n):
        act.wait_ge(s_sv, n + 1)
        for k in range(KD):
            if n:
                act.wait_ge(s_nrm, KD * (n - 1) + k + 1)
            act.activation(span(uf[:, k, :], 0), span(x[:, k, :], 0), ACT.Identity, scale=u_scale[:, n, k, 0:1],
                           bias=u_shift[:, n, k, 0:1]).then_inc(s_uf, 1)
            if n != 4:
                wait_modulated(act, n, k)
                act.activation(u_hi[:, k, :], uf[:, k, :], ACT.Copy).then_inc(s_uhi, 1)

    def u_sample(dve, n, k):
        if n:
            dve.wait_ge(s_nrm, KD * (n - 1) + k + 1)
        dve.tensor_scalar(span(uf[:, k, :], 1), span(x[:, k, :], 1), u_scale[:, n, k, 1:2], u_shift[:, n, k, 1:2],
                          ALU.mult, ALU.add).then_inc(s_us, 1)

    def wait_modulated(eng, n, k=KD - 1):
        eng.wait_ge(s_uf, KD * n + k + 1)
        eng.wait_ge(s_us, KD * n + k + 1)

    nth = lambda n: n - (n > 4)

    def u_low_tile(eng, n, k, sem_):
        eng.wait_ge(s_uhi, KD * nth(n) + k + 1)
        eng.tensor_tensor(u_lo[:, k, :], uf[:, k, :], u_hi[:, k, :].bitcast(F32), ALU.subtract).then_inc(sem_, 1)

    def u_vector(dve, n):
        for k in range(1, KD, 2):
            u_low_tile(dve, n, k, s_u)

    def u_gpsimd(pool, n):
        for k in range(0, KD, 2):
            u_low_tile(pool, n, k, s_up)

    def wait_u(eng, n, k=KD - 1):
        base = KD // 2 * nth(n)
        eng.wait_ge(s_up, base + k // 2 + 1)
        if k:
            eng.wait_ge(s_u, base + (k + 1) // 2)

    def u_ready(pe, n):
        return lambda k: wait_u(pe, n, k)

    def ln_vector(dve, n):
        dve.wait_ge(s_mean, n + 1)
        for k in range(KD):
            dve.tensor_tensor(halves(x[:, k, :]), halves(x[:, k, :]), pair(ln_banks(n)[0]),
                              ALU.subtract).then_inc(s_cen, 1)
        if n < NMOD - 1:
            g_next = done(("out01", "mix_out", "out11", "out21", "s5_out")[n])
            split_lo(dve, g_next, 1, 0)
            scale_vector(dve, n + 1)
        dve.wait_ge(s_std, n + 1)
        chains["dve"].step(dve.reciprocal(ln_rstd[:, :], ln_std[:, :]))
        dve.wait_ge(s_sq, KD * (n + 1))
        dve.wait_ge(s_cen, KD * (n + 1))
        for k in range(KD):
            dve.tensor_tensor(x[:, k, :], x[:, k, :], ln_rstd[:, :], ALU.mult).then_inc(s_nrm, 1)
            if n < NMOD - 1 and k:
                u_sample(dve, n + 1, k - 1)
        if n == NMOD - 1:
            return
        u_sample(dve, n + 1, KD - 1)
        if n + 1 != 4:
            u_vector(dve, n + 1)
        wait_modulated(dve, n + 1)
        dve.wait_ge(s_nrm, KD * (n + 1))
        for k in range(KD):
            dve.tensor_scalar(x[:, k, :], x[:, k, :], ln_g[:, n, k:k + 1], ln_b[:, n, k:k + 1],
                              ALU.mult, ALU.add).then_inc(s_x, 1)
        dve.wait_ge(s_x, KD * (n + 1))

    def ada_product(dve, w, t, st, n):
        flat = mod[:, :, :, :].rearrange("p c k b -> p (c k) b")
        ts = slice(t, t + 1) if isinstance(t, int) else bass.ds(t, 1)
        return dve.scalar_tensor_tensor(out=ada_out[:, n % 2, :], in0=w, scalar=1.0, in1=c_act[:, st, :],
                                        op0=ALU.mult, op1=ALU.mult,
                                        accum_out=flat[:, ts, st:st + 1].rearrange("p a b -> p (a b)"))

    def ada_sync(sp):
        sp.dma_start(c_col[:, :, :], i["c_col"]).then_inc(s_in, 16)
        sp.dma_start(c_act[:, :, :], i["c"]).then_inc(s_in, 16)
        for j in range(4):
            sp.dma_start(ada_w0[:, 2 * j:2 * j + 2, :, :],
                         i["w_ada0"][:, 2 * j:2 * j + 2, :, :]).then_inc(s_w0[j], 16)
            sp.dma_start(ada_w1[:, 2 * j:2 * j + 2, :], i["w_ada"][:, 2 * j:2 * j + 2, :]).then_inc(s_w1[j], 16)

    def conditioning_scalar(act, loaded, again):
        act.wait_ge(loaded, 16 if again else 32)
        if not again:
            act.activation(c_col[:, :, :], c_col[:, :, :], ACT.Silu)
        act.activation(c_act[:, :, :], c_act[:, :, :], ACT.Silu).then_inc(s_ada_c, 1)

    def ada_load(pool, u0, u1, part):
        def body(v, fresh=False):
            for r in range(2):
                if not fresh:
                    pool.wait_ge(s_ada_t, 8 * v + 4 * r - 4)
                t = KD + 4 * v + 2 * r
                ts = slice(t, t + 2) if isinstance(v, int) else bass.ds(t, 2)
                pool.dma_start(ada_w[:, r, :, :], i["w_ada"][:, ts, :]).then_inc(s_ada_w[r], 16)
        if part == 0:
            body(u0 // 2, u0 == 0)
            return
        with pool.Fori(u0 // 2 + 1, u1 // 2) as v:
            body(v)

    def ada_unit(dve, u0, i_, r):
        dve.wait_ge(s_ada_w[r], 16 * (u0 // 2 + 1) + 16 * i_)
        for n in range(4):
            done_ = 4 * (u0 + r) + n - 1 + 8 * i_
            if not isinstance(i_, int) or done_ > 0:
                dve.wait_ge(s_ada_t, done_)
            ada_product(dve, ada_w[:, r, n // 2, :], 2 * KD + 2 * (u0 + r) + n // 2 + 4 * i_, n % 2,
                        n).then_inc(s_ada_t, 1)

    def ada_tensor_first(pe):
        pe.wait_ge(s_ada_c, 1)
        for m_ in range(KD):
            if m_ % 2 == 0:
                pe.wait_ge(s_w0[m_ // 2], 16)
            for k in range(KD):
                mm = pe.matmul(ps[:, 0, 2 * m_:2 * m_ + 2], ada_w0[:, m_, k, :], c_col[:, k, :],
                               start=k == 0, stop=k == KD - 1)
        mm.then_inc(s_mod0, 1)

    def with_bias(dve, c, src):
        bias = b_ada[:, c, :].rearrange("p (k b) -> p k b", b=1).broadcast_to([P, KD, 2])
        return dve.tensor_tensor(mod[:, c, :, :], src, bias, ALU.add)

    def ada_vector_first(dve):
        dve.wait_ge(s_ada_c, 1)
        for t in range(KD):
            if t % 2 == 0:
                dve.wait_ge(s_w1[t // 2], 16)
            for st in range(2):
                n = 2 * t + st
                if n >= 2:
                    dve.wait_ge(s_mod1, n - 1)
                ada_product(dve, ada_w1[:, t, :], KD + t, st, n).then_inc(s_mod1, 1)
        dve.wait_ge(s_mod1, 2 * KD)
        dve.wait_ge(s_cst, 16 * N_CONST)
        dve.wait_ge(s_mod0, 1)
        with_bias(dve, 0, ps[:, 0, 0:2 * KD].rearrange("p (k b) -> p k b", b=2))

    def gate_vector(dve, n):
        dve.wait_ge(s_ada_t, 2 * KD * (3 * n + 1))
        chains["dve"].step(with_bias(dve, 3 * n + 2, mod[:, 3 * n + 2, :, :]))
        w = 1.0 if n % 3 == 1 else 0.5
        chains["dve"].step(dve.tensor_scalar(res_gate[:, n, :, :], mod[:, 3 * n + 2, :, :], 1.0, w / ALPHA,
                                             ALU.add, ALU.mult))

    def scale_vector(dve, n):
        link = chains["dve"].step
        shift, scale = mod[:, 3 * n, :, :], mod[:, 3 * n + 1, :, :]
        if n:
            dve.wait_ge(s_ada_t, 2 * KD * 3 * n)
            with_bias(dve, 3 * n, shift)
        link(with_bias(dve, 3 * n + 1, scale))
        if n == 0:
            dve.tensor_scalar(u_scale[:, 0, :, :], scale, 1.0, None, ALU.add)
            link(dve.tensor_copy(u_shift[:, 0, :, :], shift))
            dve.nop().then_inc(s_sv, 1)
            return
        g = ln_g[:, n - 1, :].rearrange("p (k b) -> p k b", b=1).broadcast_to([P, KD, 2])
        b = ln_b[:, n - 1, :].rearrange("p (k b) -> p k b", b=1).broadcast_to([P, KD, 2])
        link(dve.tensor_scalar(scale, scale, 1.0, None, ALU.add))
        dve.tensor_tensor(u_scale[:, n, :, :], scale, g, ALU.mult)
        link(dve.tensor_tensor(u_shift[:, n, :, :], scale, b, ALU.mult))
        dve.tensor_tensor(u_shift[:, n, :, :], u_shift[:, n, :, :], shift, ALU.add).then_inc(s_sv, 1)

    ra = Region(A0, W0)
    xp = ra("xp", [P, QT, PADW])
    zg = ra("zg", [P, HEADS, TOKENS])
    qa = ra("qa", [P, 2, TOKENS])
    KV0 = ra.at
    kvraw = ra("kvraw", [P, TOKENS])
    misc = ra("misc", [P, TOKENS])
    ckv = ra("ckv", [P, KPAD])
    RM0 = ra.at
    rows_b = Region(RM0, W0)
    rm = rows_b("rm", [P, TOKENS])
    rd = Region(A0, A0 + 20480)
    kd = rd("kd", [P, 5 * HEADS, P])
    uv = rd("uv", [P, 5 * HEADS, P])
    rr = Region(A0 + 20480, A0 + QT * PADW * 4)
    rows, t1, gcum = (rr(n, [P, TOKENS]) for n in ("rows", "t1", "gcum"))
    rt2 = Region(E1, TOP)
    qkv = rt2("qkv", [P, QT, TOKENS])
    ctmp = rt2("ctmp", [P, 2, PADW])
    T2 = rt2.at
    pt = rt2("pt", [P, 5 * HEADS, P])
    sqm = nc.alloc_sbuf_tensor_at("sqm", [P, 2, TOKENS], F32, offset=E1 + QT * TOKENS * 4)
    t2 = nc.alloc_sbuf_tensor_at("t2", [P, TOKENS], F32, offset=T2)
    t3 = nc.alloc_sbuf_tensor_at("t3", [P, TOKENS], F32, offset=T2 + TOKENS * 4)
    og = nc.alloc_sbuf_tensor_at("og", [P, HEADS, TOKENS], F32, offset=E1)
    ru2 = Region(U0, A0)
    qg = ru2("qg", [P, HEADS, TOKENS])
    wt = ru2("wt", [P, 5 * HEADS, P])
    ctok = ru2("ctok", [P, 5, P])
    ge = ru2("ge", [P, HEADS, 10])
    KP0 = ru2.at
    names = ("kp", "vp", "dl", "xi", "zi", "ys", "cm")
    BYTES = HEADS * P * 4
    places = (E1 + QT * TOKENS * 4, E1 + QT * TOKENS * 4 + BYTES, RM0, RM0 + BYTES, KV0, A0 + 20480, A0 + 20480 + BYTES)
    sets = [[ru2(n, [P, HEADS, P]) for n in names],
            [nc.alloc_sbuf_tensor_at(n + "2", [P, HEADS, P], F32, offset=at) for n, at in zip(names, places)]]
    assert RM0 + 2 * BYTES <= W0 and 2 * BYTES <= 2 * PADW * 4 and BYTES <= TOKENS * 4
    st = nc.alloc_sbuf_tensor_at("st", [P, 2, HEADS, P], F32, offset=KP0)
    uu = nc.alloc_sbuf_tensor_at("uu", [P, 2, HEADS, P], F32, offset=KP0 + 4096)
    rn = nc.alloc_sbuf_tensor_at("rn", [P, TOKENS], F32, offset=KP0 + 4096)
    rstd = nc.alloc_sbuf_tensor_at("rstd", [P, TOKENS], F32, offset=KP0 + 4096 + 2304)
    rm2 = Region(A0, A0 + QT * PADW * 4)
    kn = rm2("kn", [P, HEADS, KPAD])
    kr = rm2("kr", [P, KPAD])
    cq_hi, cq_lo = (rm2(n, [P, 2, TOKENS], F32R) for n in ("cq_hi", "cq_lo"))
    rt3 = Region(E1, TOP)
    vt = rt3("vt", [P, 7, 512])
    qn = rt3("qn", [P, HEADS, TOKENS])
    qr = rt3("qr", [P, 2, TOKENS])
    ck_hi, ck_lo = (rt3(n, [P, KPAD], F32R) for n in ("ck_hi", "ck_lo"))
    rtmp = rt3("rtmp", [P, TOKENS])
    pp = rt3("pp", [P, 2, 512])
    ra3 = Region(A0 + QT * PADW * 4, W0)
    rope = ra3("rope", [P, 2, TOKENS])
    ppt = ra3("ppt", [P, 2, 4, P])
    sm = ra3("sm", [P, 4, 20])

    s_mc = sem("conv_state_loaded")
    s_mk = sem("cached_latents_loaded")
    s_pad = sem("conv_padding_ready")
    s_conv = sem("conv_step")
    s_qkv = sem("conv_silu_ready")
    s_nsq = sem("norm_square_ready")
    s_nss = sem("norm_square_summed")
    s_nst = sem("norm_std_ready")
    s_rn = sem("row_norms_ready")
    s_rb = sem("norm_broadcast_ready")
    s_ru = sem("norm_applied")
    s_ga = sem("gate_scalar_step")
    s_gv = sem("gate_vector_step")
    s_ct = sem("frame_columns_turned")
    s_col = sem("frame_columns_ready")
    s_g1 = [sem(f"block_gram_ready_{w}") for w in range(2)]
    s_dx = [sem(f"block_exponents_ready_{w}") for w in range(2)]
    s_de = [sem(f"block_decays_ready_{w}") for w in range(2)]
    s_kv = [sem(f"block_scaled_ready_{w}") for w in range(2)]
    s_cm = [sem(f"level_part_ready_{w}") for w in range(2)]
    s_y = [sem(f"level_first_product_{w}") for w in range(2)]
    s_ys = [sem(f"level_first_copied_{w}") for w in range(2)]
    s_zx = [sem(f"level_second_product_{w}") for w in range(2)]
    s_xz = [sem(f"level_inverse_ready_{w}") for w in range(2)]
    s_uw = [sem(f"block_solution_ready_{w}") for w in range(2)]
    s_bd = [sem(f"block_done_{w}") for w in range(2)]
    s_s0 = sem("states_loaded")
    s_sw = sem("chunk_state_product")
    s_su = sem("chunk_update_ready")
    s_ku = sem("chunk_outer_ready")
    s_st = sem("chunk_state_ready")
    s_so = sem("chunk_output_ready")
    s_oc = sem("chunk_output_copied")
    s_zs = sem("gate_silu_ready")
    s_oh = sem("mixer_output_hi")
    s_ol = sem("mixer_output_ready")

    BLK = [(b, b * P, P if b < 4 else 64) for b in range(5)]
    g_in = first["mix_in"]

    def mix_sync(sp):
        stream_load(sp, "mix_in", BLOCK, lambda b: i["w_mix_in"][b, :, :] if isinstance(b, int) else
                    i["w_mix_in"][bass.ds(b, 1), :, :].rearrange("a p c -> (a p) c"))
        g0 = first["mla"]
        for r, (src, w) in enumerate(((i["w_q_b"], 1536), (i["w_kv_b"], 1024))):
            sp.wait_ge(s_wlo, g0 + r - 1)
            sp.dma_start(w_raw[:, r, 0:w], src).then_inc(s_raw[r], 16)
        stream_load(sp, "mix_out", BLOCK, lambda b: i["w_mix_out"][b, :, :] if isinstance(b, int) else
                    i["w_mix_out"][bass.ds(b, 1), :, :].rearrange("a p c -> (a p) c"))

    def mix_gpsimd(pool):
        wait_u(pool, 1)
        pool.dma_start(xp[:, :, SEQ + 3:SEQ + 6], i["conv_state"]).then_inc(s_mc, 16)
        pool.dma_start(ckv[:, TOKENS:KEYS], i["cache_latent"]).then_inc(s_mk, 16)
        pool.wait_ge(s_evac, g_in + 6)
        pool.dma_start(o["conv_p"], xp[:, :, SEQ:SEQ + 3]).then_inc(s_out, 16)
        pool.dma_start(o["conv_s"], xp[:, :, PADW - 3:PADW]).then_inc(s_out, 16)
        all_blocks_done(pool)
        pool.dma_start(st[:, 1, :, :], i["gdn_state"]).then_inc(s_s0, 16)
        pool.wait_ge(s_st, 10)
        pool.dma_start(o["gdn_p"], st[:, 0, :, :]).then_inc(s_out, 16)
        pool.dma_start(o["gdn_s"], st[:, 1, :, :]).then_inc(s_out, 16)
        mla_gpsimd(pool)

    def mix_in_scalar(act):
        def evacuate(r, m_, dst_p0, dst_p1, dst_s):
            src = pair(2 * r + m_)
            act.activation(dst_p0, src[:, 0:1, :], ACT.Copy)
            act.activation(dst_p1, src[:, 1:2, 0:SEQ - HALF], ACT.Copy)
            return act.activation(dst_s, src[:, 1:2, SEQ - HALF:HALF], ACT.Copy)

        def body(i, r, _):
            act.wait_ge(s_blk, g_in + r + 1 + 2 * i)
            if isinstance(i, int) and i == 0 and r == 0:
                wait_u(act, 1)
            for m_ in range(2):
                t = 4 * i + 2 * r + m_
                ts = slice(t, t + 1) if isinstance(i, int) else bass.ds(t, 1)
                last = evacuate(r, m_, xp[:, ts, 3:3 + HALF], xp[:, ts, 3 + HALF:3 + SEQ], xp[:, ts, SEQ + 6:PADW])
            last.then_inc(s_evac, 1)
            split_hi(act, g_in + 2, r, i)
            for m_ in range(2):
                t = 4 * i + 2 * r + m_
                ts = slice(t, t + 1) if isinstance(i, int) else bass.ds(t, 1)
                act.wait_ge(s_conv, 4 * t + 4)
                act.activation(qkv[:, ts, 0:SEQ], ctmp[:, m_:m_ + 1, 0:SEQ], ACT.Silu)
                act.activation(qkv[:, ts, SEQ:TOKENS], ctmp[:, m_:m_ + 1, SEQ + 3:SEQ + 3 + DEC],
                               ACT.Silu).then_inc(s_qkv, 1)
        blocks_loop(act, 6, body, start=1)
        dest = [zg[:, h, :] for h in range(HEADS)] + [qa[:, 0, :], qa[:, 1, :], kvraw[:, :], misc[:, :]]
        for b in range(4):
            r, bi = b % 2, 3 + b // 2
            act.wait_ge(s_blk, g_in + 7 + b)
            for m_ in range(2):
                last = act.activation(halves(dest[2 * b + m_]), pair(2 * r + m_), ACT.Copy)
            last.then_inc(s_evac, 1)
            split_hi(act, g_in + 2, r, bi)

    def mix_in_vector(dve):
        wait_u(dve, 1)
        dve.memset(xp[:, :, 0:3], 0.0).then_inc(s_pad, 1)
        dve.wait_ge(s_pad, 1)
        dve.wait_ge(s_mc, 16)
        W = PADW - 3

        def body(i, r, _):
            split_lo(dve, g_in + 2, r, i)
            dve.wait_ge(s_evac, g_in + r + 1 + 2 * i)
            for m_ in range(2):
                t = 4 * i + 2 * r + m_
                ts = slice(t, t + 1) if isinstance(i, int) else bass.ds(t, 1)
                if not isinstance(t, int) or t >= 2:
                    dve.wait_ge(s_qkv, t - 1)
                for a in range(CONV):
                    wcol = (cols[:, C_CONV + 4 * t + a:C_CONV + 4 * t + a + 1] if isinstance(t, int) else
                            cols[:, bass.ds(4 * t + C_CONV + a, 1)])
                    if a:
                        dve.wait_ge(s_conv, 4 * t + a)
                        ins = dve.scalar_tensor_tensor(out=ctmp[:, m_:m_ + 1, 0:W], in0=xp[:, ts, a:a + W],
                                                       scalar=wcol, in1=ctmp[:, m_:m_ + 1, 0:W],
                                                       op0=ALU.mult, op1=ALU.add)
                    else:
                        ins = dve.tensor_scalar(ctmp[:, m_:m_ + 1, 0:W], xp[:, ts, 0:W], wcol, None, ALU.mult)
                    ins.then_inc(s_conv, 1)
        blocks_loop(dve, 6, body, start=1)
        for b in range(4):
            split_lo(dve, g_in + 2, b % 2, 3 + b // 2)

    NORM_ROW = [0, 1, 2, 3, 4, 5, 6, 7, 8, 8, 9]

    def norm_source(n_):
        return qkv[:, n_, :] if n_ < 8 else qa[:, n_ - 8, :] if n_ < 10 else kvraw[:, :]

    def norms_scalar(act):
        act.wait_ge(s_qkv, QT)
        act.wait_ge(s_evac, g_in + 10)
        step = lambda ins, n_: (ins.then_inc(s_ga, 1), act.wait_ge(s_ga, n_))
        gates = (lambda: act.activation(rows[0:4, :], misc[64:68, :], ACT.Sigmoid),
                 lambda: act.activation(t1[0:4, :], misc[96:100, :], ACT.Identity, bias=cols[96:100, C_DT:C_DT + 1]),
                 lambda: act.activation(t2[0:4, :], t1[0:4, :], ACT.Abs),
                 lambda: act.activation(t2[0:4, :], t2[0:4, :], ACT.Exp, scale=-1.0),
                 lambda: act.activation(t2[0:4, :], t2[0:4, :], ACT.Ln, bias=1.0),
                 lambda: act.activation(cols[0:4, C_ALOG:C_ALOG + 1], cols[0:4, C_ALOG:C_ALOG + 1], ACT.Exp))
        act.wait_ge(s_gv, 1)
        for n_ in range(11):
            if n_ >= 2:
                act.wait_ge(s_nss, n_ - 1)
            act.activation(sqm[:, n_ % 2, :], norm_source(n_), ACT.Square).then_inc(s_nsq, 1)
            if n_ < len(gates):
                step(gates[n_](), n_ + 1)
        act.wait_ge(s_gv, 5)
        step(act.activation(rows[32:36, :], gcum[0:4, :], ACT.Copy), 7)
        step(act.activation(t3[0:4, :], gcum[0:4, :], ACT.Exp), 8)
        step(act.activation(rows[96:100, :], t1[0:4, :], ACT.Exp), 9)
        act.wait_ge(s_nss, 11)
        act.activation(halves(rstd[0:10, :]), pair(0)[0:10], ACT.Sqrt, bias=cols[0:10, C_RNB:C_RNB + 1],
                       scale=cols[0:10, C_RNS:C_RNS + 1]).then_inc(s_nst, 1)

    def norms_vector(dve):
        dve.wait_ge(s_qkv, QT)
        dve.wait_ge(s_out, 32)
        dve.memset(ckv[:, KEYS:KPAD], 0.0)
        dve.memset(rm[0:4, :], 1.0)
        dve.memset(rows[:, :], 0.0).then_inc(s_gv, 1)
        dve.wait_ge(s_gv, 1)
        dve.memset(rm[0:4, :].rearrange("p (c t) -> p c t", t=CH)[:, :, 0:1], 0.0).then_inc(s_gv, 1)
        dve.wait_ge(s_ga, 6)
        dve.scalar_tensor_tensor(out=t1[0:4, :], in0=t1[0:4, :], scalar=0.0, in1=t2[0:4, :], op0=ALU.max,
                                 op1=ALU.add).then_inc(s_gv, 1)
        dve.wait_ge(s_gv, 3)
        dve.tensor_scalar(t1[0:4, :], t1[0:4, :], cols[0:4, C_ALOG:C_ALOG + 1], -1.0, ALU.mult,
                          ALU.mult).then_inc(s_dve, 1)
        chains["dve"].n += 1
        dve.wait_ge(s_dve, chains["dve"].n)
        dve.tensor_tensor_scan(gcum[0:4, :], rm[0:4, :], t1[0:4, :], 0.0, ALU.mult, ALU.add).then_inc(s_gv, 1)
        dve.wait_ge(s_gv, 4)
        g3 = gcum[0:4, :].rearrange("p (c t) -> p c t", t=CH)
        dve.tensor_tensor(t1[0:4, :].rearrange("p (c t) -> p c t", t=CH),
                          g3[:, :, CH - 1:CH].broadcast_to([4, 9, CH]), g3, ALU.subtract).then_inc(s_gv, 1)
        dve.wait_ge(s_ga, 9)
        dve.tensor_tensor(rows[64:68, :], rows[0:4, :], t3[0:4, :], ALU.mult).then_inc(s_gv, 1)
        dve.wait_ge(s_nst, 1)
        dve.reciprocal(rn[0:10, :], rstd[0:10, :]).then_inc(s_rn, 1)
        for j in range(10):
            dve.wait_ge(s_rb, j + 1)
            spread = pair(1 + j % 3)
            if j < 8:
                ins = dve.tensor_tensor(halves(qkv[:, j, :]), halves(qkv[:, j, :]), spread, ALU.mult)
            elif j == 8:
                for m_ in range(2):
                    ins = dve.scalar_tensor_tensor(out=halves(qa[:, m_, :]), in0=halves(qa[:, m_, :]),
                                                   scalar=cols[:, C_QN + m_:C_QN + m_ + 1], in1=spread,
                                                   op0=ALU.mult, op1=ALU.mult)
            else:
                ins = dve.scalar_tensor_tensor(out=halves(ckv[:, 0:TOKENS]), in0=halves(kvraw[:, :]),
                                               scalar=cols[:, C_KVN:C_KVN + 1], in1=spread,
                                               op0=ALU.mult, op1=ALU.mult)
            ins.then_inc(s_ru, 1)
        dve.wait_ge(s_ct, 1)
        dve.tensor_copy(ctok[:, 0:4, :], ps[:, 0, :].rearrange("p (b c) -> p b c", b=4))
        dve.tensor_copy(ctok[0:64, 4, :], ps[0:64, 1, 0:P]).then_inc(s_col, 1)
        dve.wait_ge(s_ru, 10)
        dve.wait_ge(s_col, 1)

    def norms_tensor(pe):
        pe.wait_ge(s_evac, g_in + 10)
        for n_ in range(11):
            pe.wait_ge(s_nsq, n_ + 1)
            j = NORM_ROW[n_]
            for a in range(2):
                m = pe.matmul(pair(0)[0:16, a, :], onecol[:, 15 - j:31 - j], halves(sqm[:, n_ % 2, :])[:, a, :],
                              start=n_ == 0, stop=n_ == 10)
            m.then_inc(s_nss, 1)
        pe.wait_ge(s_rn, 1)
        for j in range(10):
            if j >= 3:
                pe.wait_ge(s_ru, j - 2)
            for a in range(2):
                m = pe.matmul(pair(1 + j % 3)[:, a, :], ident[0:10, j:j + 1].broadcast_to([10, P]),
                              halves(rn[0:10, :])[:, a, :], start=True, stop=True)
            m.then_inc(s_rb, 1)
        pe.wait_ge(s_gv, 6)
        pe.wait_ge(s_ru, 10)
        for b, t0, n_ in BLK:
            m = pe.transpose(ps[0:n_, b // 4, (b % 4) * P:(b % 4) * P + P], rows[:, t0:t0 + n_], ident[:, :])
        m.then_inc(s_ct, 1)

    def bank(n_, rows_=P, width=P):
        return ps[0:rows_, n_, 0:HEADS * P].rearrange("p (h c) -> p h c", h=HEADS)[:, :, 0:width]

    PAIRS_OF_BLOCKS = [BLK[0:2], BLK[2:4], BLK[4:5]]
    LEVELS = 6

    def level_banks(w):
        return (5, 6, 7) if w == 0 else (0, 1, 2)

    def all_blocks_done(eng):
        eng.wait_ge(s_bd[0], 3)
        eng.wait_ge(s_bd[1], 2)

    def gdn_tensor(pe):
        def gram(b, t0, n_):
            w, j = b % 2, b // 2
            if w:
                pe.wait_ge(s_kv[0], j + 1)
                pe.wait_ge(s_xz[0], LEVELS * j + 1)
            elif j:
                pe.wait_ge(s_bd[0], j)
                pe.wait_ge(s_bd[1], j)
            q, k, v = (lambda h, i_=i_: qkv[:, 4 * i_ + h, t0:t0 + n_] for i_ in range(3))
            for h in range(HEADS):
                m = pe.matmul(bank(0, P, n_)[:, h, :], ident[0:4, h:h + 1].broadcast_to([4, P]),
                              gcum[0:4, t0:t0 + n_], start=True, stop=True)
            m.then_inc(s_g1[w], 1)
            for h in range(HEADS):
                m = pe.matmul(bank(1, n_, n_)[:, h, :], k(h), k(h), start=True, stop=True)
            m.then_inc(s_g1[w], 1)
            for h in range(HEADS):
                m = pe.matmul(bank(2, n_, n_)[:, h, :], k(h), q(h), start=True, stop=True)
            m.then_inc(s_g1[w], 1)
            for i_, f in ((3, k), (4, v)):
                for h in range(HEADS):
                    m = pe.transpose(bank(i_, n_)[:, h, :], f(h), ident[:, :])
                m.then_inc(s_g1[w], 1)

        def first_product(b, n_, lv):
            w, j = b % 2, b // 2
            zi, cm = sets[w][4], sets[w][6]
            pe.wait_ge(s_cm[w], LEVELS * j + lv + 1)
            if lv:
                pe.wait_ge(s_xz[w], LEVELS * j + lv)
            for h in range(HEADS):
                m = pe.matmul(bank(level_banks(w)[0], n_, n_)[:, h, :], cm[0:n_, h, 0:n_],
                              zi[0:n_, h, 0:n_] if lv else ident[0:n_, 0:n_], start=True, stop=True)
            m.then_inc(s_y[w], 1)

        def updates(b, n_, lv):
            w, j = b % 2, b // 2
            xi, ys = sets[w][3], sets[w][5]
            pe.wait_ge(s_ys[w], (LEVELS - 1) * j + lv)
            for h in range(HEADS):
                m = pe.matmul(bank(level_banks(w)[1], n_, n_)[:, h, :], xi[0:n_, h, 0:n_], ys[0:n_, h, 0:n_],
                              start=True, stop=True)
            if lv < LEVELS - 1:
                for h in range(HEADS):
                    m = pe.matmul(bank(level_banks(w)[2], n_, n_)[:, h, :], ys[0:n_, h, 0:n_],
                                  xi[0:n_, h, 0:n_], start=True, stop=True)
            m.then_inc(s_zx[w], 1)

        def solution(b, n_, paired):
            w, j = b % 2, b // 2
            kp, vp, zi = sets[w][0], sets[w][1], sets[w][4]
            pe.wait_ge(s_xz[w], LEVELS * (j + 1))
            pe.wait_ge(s_kv[w], j + 1)
            if w:
                pe.wait_ge(s_bd[0], j + 1)
            elif paired:
                pe.wait_ge(s_kv[1], j + 1)
            for h in range(HEADS):
                m = pe.matmul(bank(3, n_)[:, h, :], zi[0:n_, h, 0:n_], vp[0:n_, h, :], start=True, stop=True)
            for h in range(HEADS):
                m = pe.matmul(bank(4, P, n_)[:, h, :], kp[0:n_, h, :], zi[0:n_, h, 0:n_], start=True, stop=True)
            m.then_inc(s_uw[w], 1)

        pe.wait_ge(s_col, 1)
        for blocks in PAIRS_OF_BLOCKS:
            for b, t0, n_ in blocks:
                gram(b, t0, n_)
                first_product(b, n_, 0)
            for lv in range(1, LEVELS):
                for b, t0, n_ in blocks:
                    first_product(b, n_, lv)
                for b, t0, n_ in blocks:
                    updates(b, n_, lv)
            for b, t0, n_ in blocks:
                solution(b, n_, len(blocks) == 2)

    def gdn_scalar(act):
        for blocks in PAIRS_OF_BLOCKS:
            for b, t0, n_ in blocks:
                w, j = b % 2, b // 2
                dl, ys = sets[w][2], sets[w][5]
                act.wait_ge(s_g1[w], 5 * j + 1)
                if j:
                    act.wait_ge(s_zx[w], (LEVELS - 1) * j)
                act.activation(ys[:, :, 0:n_], bank(0, P, n_), ACT.Exp).then_inc(s_de[w], 1)
                act.wait_ge(s_dx[w], 2 * j + 1)
                act.activation(dl[0:n_, :, 0:n_], dl[0:n_, :, 0:n_], ACT.Exp, scale=-1.0)
                act.activation(pt[0:n_, 4 * b:4 * b + 4, 0:n_], pt[0:n_, 4 * b:4 * b + 4, 0:n_],
                               ACT.Exp).then_inc(s_de[w], 1)
            for lv in range(1, LEVELS):
                for b, t0, n_ in blocks:
                    w, j = b % 2, b // 2
                    if lv == 1:
                        act.wait_ge(s_dx[w], 2 * j + 2)
                    act.wait_ge(s_y[w], LEVELS * j + lv + 1)
                    act.activation(sets[w][5][0:n_, :, 0:n_], bank(level_banks(w)[0], n_, n_),
                                   ACT.Copy).then_inc(s_ys[w], 1)
            for b, t0, n_ in blocks:
                w, j = b % 2, b // 2
                act.wait_ge(s_uw[w], j + 1)
                act.activation(uv[0:n_, 4 * b:4 * b + 4, :], bank(3, n_), ACT.Copy)
                act.activation(wt[:, 4 * b:4 * b + 4, 0:n_], bank(4, P, n_), ACT.Copy).then_inc(s_bd[w], 1)

    def gdn_vector(dve):
        link = chains["dve"].step
        mask = lambda m_, n_: masks[0:n_, m_:m_ + 1, 0:n_].broadcast_to([n_, HEADS, n_])

        def scaled(b, t0, n_):
            w, j = b % 2, b // 2
            kp, vp, dl, xi, zi, ys, cm = sets[w]
            col = lambda kind, h: ctok[0:n_, b, 32 * kind + h:32 * kind + h + 1]
            if j:
                dve.wait_ge(s_uw[w], j)
            dve.wait_ge(s_g1[w], 5 * j + 1)
            dve.wait_ge(s_de[w], 2 * j + 1)
            for h in range(HEADS):
                dve.tensor_scalar(dl[0:n_, h, 0:n_], bank(0, n_, n_)[:, h, :], col(1, h), 0.0, ALU.subtract, ALU.max)
            for h in range(HEADS):
                ins = dve.tensor_scalar(pt[0:n_, 4 * b + h, 0:n_], bank(0, n_, n_)[:, h, :], col(1, h), 0.0,
                                        ALU.subtract, ALU.min)
            ins.then_inc(s_dx[w], 1)
            dve.tensor_copy(ge[:, :, 2 * b:2 * b + n_ // CH],
                            ys[:, :, 0:n_].rearrange("p h (c t) -> p h c t", t=CH)[:, :, :, CH - 1])
            dve.tensor_tensor(qg[:, :, t0:t0 + n_], qkv[:, 0:4, t0:t0 + n_], ys[:, :, 0:n_],
                              ALU.mult).then_inc(s_dx[w], 1)
            dve.wait_ge(s_g1[w], 5 * j + 5)
            for h in range(HEADS):
                dve.tensor_scalar(kp[0:n_, h, :], bank(3, n_)[:, h, :], col(2, h), None, ALU.mult)
                dve.tensor_scalar(kd[0:n_, 4 * b + h, :], bank(3, n_)[:, h, :], col(3, h), None, ALU.mult)
                ins = dve.tensor_scalar(vp[0:n_, h, :], bank(4, n_)[:, h, :], col(0, h), None, ALU.mult)
            ins.then_inc(s_kv[w], 1)
            dve.wait_ge(s_de[w], 2 * j + 2)
            for h in range(HEADS):
                ins = dve.scalar_tensor_tensor(out=dl[0:n_, h, 0:n_], in0=bank(1, n_, n_)[:, h, :], scalar=col(0, h),
                                               in1=dl[0:n_, h, 0:n_], op0=ALU.mult, op1=ALU.mult)
            link(ins)

        def part(b, n_, lv):
            w, j = b % 2, b // 2
            dl, cm = sets[w][2], sets[w][6]
            if lv:
                dve.wait_ge(s_y[w], LEVELS * j + lv)
            dve.tensor_tensor(cm[0:n_, :, 0:n_], dl[0:n_, :, 0:n_], mask(lv, n_), ALU.mult).then_inc(s_cm[w], 1)

        def start(b, n_):
            w, j = b % 2, b // 2
            xi, zi, cm = sets[w][3], sets[w][4], sets[w][6]
            pts = pt[0:n_, 4 * b:4 * b + 4, 0:n_]
            one = ident[0:n_, 0:n_].rearrange("p (a c) -> p a c", a=1).broadcast_to([n_, HEADS, n_])
            link(dve.tensor_tensor(pts, bank(2, n_, n_), pts, ALU.mult))
            link(dve.tensor_tensor(pts, pts, mask(6, n_), ALU.mult))
            dve.wait_ge(s_cm[w], LEVELS * j + 1)
            dve.wait_ge(s_y[w], LEVELS * j + 1)
            dve.tensor_tensor(xi[0:n_, :, 0:n_], one, cm[0:n_, :, 0:n_], ALU.subtract)
            dve.tensor_tensor(zi[0:n_, :, 0:n_], one, bank(level_banks(w)[0], n_, n_),
                              ALU.subtract).then_inc(s_xz[w], 1)
            dve.wait_ge(s_xz[w], LEVELS * j + 1)

        def update(b, n_, lv):
            w, j = b % 2, b // 2
            xi, zi = sets[w][3], sets[w][4]
            _, zb, xb = level_banks(w)
            dve.wait_ge(s_zx[w], (LEVELS - 1) * j + lv)
            if lv < LEVELS - 1:
                dve.tensor_tensor(xi[0:n_, :, 0:n_], xi[0:n_, :, 0:n_], bank(xb, n_, n_), ALU.subtract)
            dve.tensor_tensor(zi[0:n_, :, 0:n_], zi[0:n_, :, 0:n_], bank(zb, n_, n_),
                              ALU.subtract).then_inc(s_xz[w], 1)
            dve.wait_ge(s_xz[w], LEVELS * j + lv + 1)

        for blocks in PAIRS_OF_BLOCKS:
            for b, t0, n_ in blocks:
                scaled(b, t0, n_)
                part(b, n_, 0)
                start(b, n_)
                part(b, n_, 1)
            for lv in range(1, LEVELS):
                for b, t0, n_ in blocks:
                    update(b, n_, lv)
                    if lv + 1 < LEVELS:
                        part(b, n_, lv + 1)

    def chunk(c):
        b = c // 2
        r0 = (c % 2) * CH
        return b, r0, 1 if c == 8 else 0

    def scan_tensor(pe):
        all_blocks_done(pe)
        for c in range(9):
            b, r0, s = chunk(c)
            tok = slice(c * CH, c * CH + CH)
            pe.wait_ge(s_st, c + 1)
            if c == 8:
                pe.wait_ge(s_s0, 16)
            for h in range(HEADS):
                m = pe.matmul(ps[r0:r0 + CH, c % 2, h * P:h * P + P], wt[:, 4 * b + h, r0:r0 + CH], st[:, s, h, :],
                              start=True, stop=True)
            m.then_inc(s_sw, 1)
            if c >= 2:
                pe.wait_ge(s_oc, c - 1)
            out = lambda h: ps[:, 2 + c % 2, h * CH:h * CH + CH]
            for h in range(HEADS):
                pe.matmul(out(h), st_old(c)[:, h, :], qg[:, h, tok], start=h == 0, stop=False)
            pe.wait_ge(s_su, c + 1)
            for h in range(HEADS):
                m = pe.matmul(bank(4 + c % 2)[:, h, :], kd[r0:r0 + CH, 4 * b + h, :], uu[r0:r0 + CH, c % 2, h, :],
                              start=True, stop=True)
            m.then_inc(s_ku, 1)
            for h in range(HEADS):
                m = pe.matmul(out(h), uu[r0:r0 + CH, c % 2, h, :], pt[r0:r0 + CH, 4 * b + h, r0:r0 + CH],
                              start=False, stop=h == HEADS - 1)
            m.then_inc(s_so, 1)

    def scan_vector(dve):
        all_blocks_done(dve)
        dve.memset(st[:, 0, :, :], 0.0).then_inc(s_st, 1)
        for c in range(9):
            b, r0, s = chunk(c)
            dve.wait_ge(s_sw, c + 1)
            if c >= 2:
                dve.wait_ge(s_so, c - 1)
            rows_ = slice(r0, r0 + CH)
            dve.tensor_tensor(uu[rows_, c % 2, :, :], uv[rows_, 4 * b:4 * b + 4, :],
                              ps[rows_, c % 2, :].rearrange("p (h c) -> p h c", h=HEADS),
                              ALU.subtract).then_inc(s_su, 1)
            dve.wait_ge(s_ku, c + 1)
            for h in range(HEADS):
                ins = dve.scalar_tensor_tensor(out=st[:, s, h, :], in0=st[:, s, h, :], scalar=ge[:, h, c:c + 1],
                                               in1=bank(4 + c % 2)[:, h, :], op0=ALU.mult, op1=ALU.add)
            ins.then_inc(s_st, 1)
            if c == 7:
                dve.wait_ge(s_s0, 16)
            if c < 8:
                dve.wait_ge(s_st, c + 2)
        dve.wait_ge(s_st, 10)

    def st_old(c):
        return st[:, chunk(c)[2], :, :]

    def scan_scalar(act):
        act.activation(zg[:, :, :], zg[:, :, :], ACT.Silu).then_inc(s_zs, 1)
        for c in range(9):
            act.wait_ge(s_so, c + 1)
            if c == 0:
                all_blocks_done(act)
            act.activation(og[:, :, c * CH:c * CH + CH],
                           ps[:, 2 + c % 2, 0:HEADS * CH].rearrange("p (h t) -> p h t", h=HEADS),
                           ACT.Copy).then_inc(s_oc, 1)

    def onorm_scalar(act):
        act.wait_ge(s_oc, 9)
        for h in range(HEADS):
            if h >= 2:
                act.wait_ge(s_nss, 11 + h - 1)
            act.activation(sqm[:, h % 2, :], og[:, h, :], ACT.Square).then_inc(s_nsq, 1)
        act.wait_ge(s_nss, 15)
        act.activation(halves(rows[0:4, :]), pair(0)[0:4], ACT.Sqrt, bias=cols[0:4, C_OEPS:C_OEPS + 1],
                       scale=1.0 / P).then_inc(s_nst, 1)
        for h in range(HEADS):
            act.wait_ge(s_ru, 10 + h + 1)
            if h == 0:
                act.wait_ge(s_out, 64)
            act.activation(u_hi[:, h, :], og[:, h, :], ACT.Copy).then_inc(s_oh, 1)

    def onorm_tensor(pe):
        pe.wait_ge(s_oc, 9)
        for h in range(HEADS):
            pe.wait_ge(s_nsq, 11 + h + 1)
            for a in range(2):
                m = pe.matmul(pair(0)[0:16, a, :], onecol[:, 15 - h:31 - h], halves(sqm[:, h % 2, :])[:, a, :],
                              start=h == 0, stop=h == 3)
            m.then_inc(s_nss, 1)
        pe.wait_ge(s_rn, 2)
        for h in range(HEADS):
            if h == 3:
                pe.wait_ge(s_ru, 11)
            for a in range(2):
                m = pe.matmul(pair(1 + h % 3)[:, a, :], ident[0:4, h:h + 1].broadcast_to([4, P]),
                              halves(t1[0:4, :])[:, a, :], start=True, stop=True)
            m.then_inc(s_rb, 1)

    def onorm_vector(dve):
        dve.wait_ge(s_zs, 1)
        for h in range(HEADS):
            dve.wait_ge(s_nsq, 11 + h + 1)
            dve.scalar_tensor_tensor(out=og[:, h, :], in0=og[:, h, :], scalar=cols[:, C_NORMW:C_NORMW + 1],
                                     in1=zg[:, h, :], op0=ALU.mult, op1=ALU.mult).then_inc(s_zs, 1)
        dve.wait_ge(s_nst, 2)
        dve.reciprocal(t1[0:4, :], rows[0:4, :]).then_inc(s_rn, 1)

        def low(h):
            dve.wait_ge(s_ru, 10 + h + 1)
            dve.wait_ge(s_oh, h + 1)
            dve.tensor_tensor(u_lo[:, h, :], og[:, h, :], u_hi[:, h, :].bitcast(F32), ALU.subtract).then_inc(s_ol, 1)

        for h in range(HEADS):
            dve.wait_ge(s_rb, 10 + h + 1)
            dve.wait_ge(s_zs, h + 2)
            dve.tensor_tensor(halves(og[:, h, :]), halves(og[:, h, :]), pair(1 + h % 3), ALU.mult).then_inc(s_ru, 1)
            if h:
                low(h - 1)
        low(HEADS - 1)

    s_ch = sem("latent_hi_ready")
    s_cl = sem("latent_parts_ready")
    s_mp = sem("latent_product_done")
    s_me = sem("latent_product_copied")
    s_rope = sem("rotary_tables_loaded")
    s_rp = sem("rotary_swapped")
    s_kr = sem("rotary_applied")
    s_sc = sem("scores_ready")
    s_mx = sem("row_maximum_ready")
    s_sx = sem("exponentials_ready")
    s_pn = sem("probabilities_ready")
    s_tp = sem("probabilities_turned")
    s_pc = sem("probabilities_copied")
    s_pv = sem("values_weighted")
    g_mla = first["mla"]
    UNITS = [(h, qb * P, P, 0, (qb + 1) * P) for qb in range(4) for h in range(HEADS)]
    UNITS += [(h, SEQ, DEC, SEQ, DEC + PAST) for h in range(HEADS)]
    NU = len(UNITS)

    def mla_gpsimd(pool):
        pool.wait_ge(s_out, 64)
        pool.dma_start(kr[:, TOKENS:KEYS], i["cache_rope"]).then_inc(s_rope, 16)
        pool.wait_ge(s_zs, 5)
        pool.dma_start(rope[:, :, :], i["rope"]).then_inc(s_rope, 16)
        pool.dma_start(o["latent"], ckv[:, 0:TOKENS]).then_inc(s_out, 16)
        pool.wait_ge(s_kr, 3)
        pool.dma_start(o["krope"], kr[0:64, 0:TOKENS]).then_inc(s_out, 16)
        pool.wait_ge(s_out, 96)

    def mla_tensor(pe):
        pe.wait_ge(s_cl, 3)
        pe.wait_ge(s_ru, 14)
        pe.wait_ge(s_wlo, g_mla + 1)
        wq = [w[:, 0, 0:1536].rearrange("p (k m c) -> p k m c", k=2, m=6) for w in (w_hi, w_lo)]
        for m_ in range(6):
            if m_ >= 4:
                pe.wait_ge(s_me, m_ - 3)
            for k in range(2):
                mm = three(pe, pair(m_ % 4), wq[0][:, k, m_, :], wq[1][:, k, m_, :],
                           halves(cq_hi[:, k, :]), halves(cq_lo[:, k, :]), k == 0, k == 1)
            mm.then_inc(s_mp if m_ < 5 else s_blk, 1)
        pe.wait_ge(s_wlo, g_mla + 2)
        pe.wait_ge(s_evac, g_mla + 1)
        wkv = [w[:, 1, 0:1024] for w in (w_hi, w_lo)]
        kh = [t.rearrange("p (a t) -> p a t", a=2) for t in (ck_hi[:, :], ck_lo[:, :])]
        for h in range(HEADS):
            mm = three(pe, ps[:, 2 * h:2 * h + 2, 0:KPAD // 2], wkv[0][:, h * P:h * P + P], wkv[1][:, h * P:h * P + P],
                       kh[0], kh[1], True, True)
            mm.then_inc(s_mp, 1)
        for t in range(7):
            pe.wait_ge(s_me, 6 + t // 2)
            for n_, (a, b) in enumerate(((ck_hi, 0), (ck_hi, 1), (ck_lo, 0))):
                mm = pe.matmul(ps[:, t, :], a[:, t * P:t * P + P], wkv[b][:, 512:1024], start=n_ == 0, stop=n_ == 2)
            mm.then_inc(s_mp if t < 6 else s_blk, 1)
        pe.wait_ge(s_evac, g_mla + 2)
        for n_, (w, src) in enumerate(((swap[:, 0, :], qr[:, 0, :]), (swap[:, 0, :], qr[:, 1, :]),
                                       (swap[0:64, 1, :], misc[0:64, :]), (swap[0:64, 2, :], misc[0:64, :]))):
            for a in range(2):
                mm = pe.matmul(pair(n_)[:, a, :], w, halves(src)[:, a, :], start=True, stop=True)
            mm.then_inc(s_rp, 1)
        pe.wait_ge(s_kr, 3)
        for n in range(NU + 2):
            if n < NU:
                h, q0, nq, k0, nk = UNITS[n]
                p0 = (h % 2) * 64
                if n >= 2:
                    pe.wait_ge(s_sx, n - 1)
                out = ps[0:nq, n % 2, 0:nk]
                pe.matmul(out, qn[:, h, q0:q0 + nq], kn[:, h, k0:k0 + nk], start=True, stop=False)
                pe.matmul(out, qr[p0:p0 + 64, h // 2, q0:q0 + nq], kr[p0:p0 + 64, k0:k0 + nk],
                          start=False, stop=True).then_inc(s_sc, 1)
            if 2 <= n:
                u = n - 2
                h, q0, nq, k0, nk = UNITS[u]
                pe.wait_ge(s_pc, u + 1)
                if u % 4 == 0 and u >= 8:
                    pe.wait_ge(s_ol, 4 + u // 4 - 1)
                for t in range(-(-nk // P)):
                    w = min(P, nk - t * P)
                    mm = pe.matmul(ps[:, 4 + (u // 4) % 2, h * nq:h * nq + nq], vt[0:w, k0 // P + t, h * P:h * P + P],
                                   ppt[0:w, u % 2, t, 0:nq], start=t == 0, stop=(t + 1) * P >= nk)
                mm.then_inc(s_pv, 1)
            if 1 <= n <= NU:
                u = n - 1
                h, q0, nq, k0, nk = UNITS[u]
                pe.wait_ge(s_pn, u + 1)
                if u >= 2:
                    pe.wait_ge(s_pc, u - 1)
                for t in range(-(-nk // P)):
                    w = min(P, nk - t * P)
                    mm = pe.transpose(ps[0:w, 2 + u % 2, t * P:t * P + nq], pp[0:nq, u % 2, t * P:t * P + w],
                                      ident[0:nq, 0:nq])
                mm.then_inc(s_tp, 1)

    def mla_scalar(act):
        act.wait_ge(s_so, 9)
        act.wait_ge(s_ru, 10)
        act.wait_ge(s_mk, 16)
        for m_ in range(2):
            act.activation(cq_hi[:, m_, :], qa[:, m_, :], ACT.Copy).then_inc(s_ch, 1)
        act.activation(ck_hi[:, :], ckv[:, :], ACT.Copy).then_inc(s_ch, 1)
        for m_ in range(6):
            act.wait_ge(s_mp if m_ < 5 else s_blk, m_ + 1 if m_ < 5 else g_mla + 1)
            dst = qn[:, m_, :] if m_ < 4 else qr[:, m_ - 4, :]
            act.activation(halves(dst), pair(m_ % 4), ACT.Copy).then_inc(s_me if m_ < 5 else s_evac, 1)
        split_hi(act, g_mla + 2, 0, 0)
        for h in range(HEADS):
            act.wait_ge(s_mp, 6 + h)
            act.activation(kn[:, h, :].rearrange("p (a t) -> p a t", a=2), ps[:, 2 * h:2 * h + 2, 0:KPAD // 2],
                           ACT.Copy).then_inc(s_me, 1)
        act.wait_ge(s_ol, 4)
        for t in range(7):
            act.wait_ge(s_mp if t < 6 else s_blk, 10 + t if t < 6 else g_mla + 2)
            act.activation(vt[:, t, :], ps[:, t, :], ACT.Copy).then_inc(s_me if t < 6 else s_evac, 1)
        split_hi(act, g_mla + 2, 1, 0)
        for n in range(NU + 2):
            if n < NU:
                h, q0, nq, k0, nk = UNITS[n]
                act.wait_ge(s_mx, n + 1)
                if n >= 2:
                    act.wait_ge(s_tp, n - 1)
                act.activation(pp[0:nq, n % 2, 0:nk], ps[0:nq, n % 2, 0:nk], ACT.Exp, bias=sm[0:nq, 1, n:n + 1],
                               scale=MLA_SCALE, accum_out=sm[0:nq, 2, n:n + 1]).then_inc(s_sx, 1)
            if 1 <= n <= NU:
                u = n - 1
                h, q0, nq, k0, nk = UNITS[u]
                act.wait_ge(s_tp, u + 1)
                if u >= 2:
                    act.wait_ge(s_pv, u - 1)
                full = nk // P
                src = ps[:, 2 + u % 2, :].rearrange("p (t c) -> p t c", c=P)
                ins = act.activation(ppt[:, u % 2, 0:full, 0:nq], src[:, 0:full, 0:nq], ACT.Copy)
                if nk % P:
                    ins = act.activation(ppt[0:nk % P, u % 2, full, 0:nq], src[0:nk % P, full, 0:nq], ACT.Copy)
                ins.then_inc(s_pc, 1)
            if n >= 2 and n % 4 == 1:
                h, q0, nq, k0, nk = UNITS[n - 2]
                gi = (n - 2) // 4
                act.wait_ge(s_pv, n - 1)
                act.activation(u_hi[:, 4:8, q0:q0 + nq],
                               ps[:, 4 + gi % 2, 0:HEADS * nq].rearrange("p (h t) -> p h t", h=HEADS),
                               ACT.Copy).then_inc(s_oh, 1)

    def mla_vector(dve):
        link = chains["dve"].step
        for m_ in range(2):
            dve.wait_ge(s_ch, m_ + 1)
            dve.tensor_tensor(cq_lo[:, m_, :], qa[:, m_, :], cq_hi[:, m_, :].bitcast(F32),
                              ALU.subtract).then_inc(s_cl, 1)
        dve.wait_ge(s_ch, 3)
        dve.tensor_tensor(ck_lo[:, :], ckv[:, :], ck_hi[:, :].bitcast(F32), ALU.subtract).then_inc(s_cl, 1)
        dve.wait_ge(s_blk, g_mla + 1)
        split_lo(dve, g_mla + 2, 0, 0)
        dve.wait_ge(s_blk, g_mla + 2)
        split_lo(dve, g_mla + 2, 1, 0)
        dve.wait_ge(s_rope, 32)
        for j in range(2):
            dve.wait_ge(s_rp, j + 1)
            link(dve.tensor_tensor(halves(rtmp[:, :]), pair(j), halves(rope[:, 1, :]), ALU.mult))
            link(dve.tensor_tensor(qr[:, j, :], qr[:, j, :], rope[:, 0, :], ALU.mult))
            dve.tensor_tensor(qr[:, j, :], qr[:, j, :], rtmp[:, :], ALU.add).then_inc(s_kr, 1)
            dve.wait_ge(s_kr, j + 1)
        dve.wait_ge(s_rp, 4)
        link(dve.tensor_tensor(halves(kr[:, 0:TOKENS]), pair(2), halves(rope[:, 0, :]), ALU.mult))
        link(dve.tensor_tensor(halves(rtmp[:, :]), pair(3), halves(rope[:, 1, :]), ALU.mult))
        dve.tensor_tensor(kr[:, 0:TOKENS], kr[:, 0:TOKENS], rtmp[:, :], ALU.add).then_inc(s_kr, 1)
        for n in range(NU + 2):
            if n < NU:
                h, q0, nq, k0, nk = UNITS[n]
                dve.wait_ge(s_sc, n + 1)
                if q0 < SEQ:
                    link(dve.memset(ps[0:CH, n % 2, nk - CH:nk], -1e30))
                link(dve.tensor_reduce(sm[0:nq, 0, n:n + 1], ps[0:nq, n % 2, 0:nk], AX.X, ALU.max))
                dve.tensor_scalar(sm[0:nq, 1, n:n + 1], sm[0:nq, 0, n:n + 1], -MLA_SCALE, None,
                                  ALU.mult).then_inc(s_mx, 1)
            if 1 <= n <= NU:
                u = n - 1
                h, q0, nq, k0, nk = UNITS[u]
                dve.wait_ge(s_sx, u + 1)
                link(dve.reciprocal(sm[0:nq, 3, u:u + 1], sm[0:nq, 2, u:u + 1]))
                dve.tensor_scalar(pp[0:nq, u % 2, 0:nk], pp[0:nq, u % 2, 0:nk], sm[0:nq, 3, u:u + 1], None,
                                  ALU.mult).then_inc(s_pn, 1)
            if n >= 2 and n % 4 == 1:
                h, q0, nq, k0, nk = UNITS[n - 2]
                gi = (n - 2) // 4
                dve.wait_ge(s_oh, 4 + gi + 1)
                dve.tensor_tensor(u_lo[:, 4:8, q0:q0 + nq],
                                  ps[:, 4 + gi % 2, 0:HEADS * nq].rearrange("p (h t) -> p h t", h=HEADS),
                                  u_hi[:, 4:8, q0:q0 + nq].bitcast(F32), ALU.subtract).then_inc(s_ol, 1)

    def mix_tensor(pe):
        body, count = product(pe, "mix_in", 2, KD, u_hi, u_lo, ready_first=u_ready(pe, 1))
        blocks_loop(pe, count, body, start=1)
        norms_tensor(pe)
        gdn_tensor(pe)
        scan_tensor(pe)
        onorm_tensor(pe)
        mla_tensor(pe)
        pe.wait_ge(s_ol, 9)
        body, count = product(pe, "mix_out", 2, KD, u_hi, u_lo)
        blocks_loop(pe, count, body)

    def out_scalar(act, name):
        g0 = first[name]

        def body(i, r, _):
            act.wait_ge(s_blk, g0 + r + 1 + 2 * i)
            split_hi(act, g0 + 2, r, i)
        blocks_loop(act, 4, body)

    def mix_scalar(act):
        act.wait_ge(s_ada_t, 4 * UNITS0)
        mix_in_scalar(act)
        norms_scalar(act)
        gdn_scalar(act)
        scan_scalar(act)
        onorm_scalar(act)
        mla_scalar(act)
        out_scalar(act, "mix_out")

    def mix_vector(dve):
        dve.wait_ge(s_ada_t, 4 * UNITS0)
        mix_in_vector(dve)
        norms_vector(dve)
        gdn_vector(dve)
        scan_vector(dve)
        onorm_vector(dve)
        mla_vector(dve)
        gate_vector(dve, 1)
        residual_vector(dve, "mix_out", 1, 2)
        dve.wait_ge(s_out, 96)

    rp = Region(U0, A0)
    rot = rp("rot", [P, 2, PAIRS, NC])
    rho = rp("rho", [P, PAIRS, NC])
    pw = rp("pw", [P, 2, PAIRS, 17])
    bb = rp("bb", [P, 2, PAIRS, 16])
    steps = rp("steps", [P, 17 + NC])
    rq = Region(A0 + KD * TOKENS * 4, W0)
    eb = rq("eb", [P, 2, 2, 4, P])
    u3 = rq("u3", [P, 2, 8, P])
    u2 = rq("u2", [P, 2, 8, NC])
    hb = rq("hb", [P, 2, SUB, P])
    c_par = rq("c_par", [P, 2, PAIRS, 16])
    bp = rq("bp", [P, 2, 2, 4, 32])
    d_skip = rq("d_skip", [P, KD])
    rs = Region(E1, TOP)
    be = rs("be", [P, 2, 2, 4, P])
    wm = rs("wm", [P, 2, 2, 4, 9, 16])
    xx = rs("xx", [P, 2, 2, 4, NC + 1])
    y3 = rs("y3", [P, 2, SUB, P])
    ta, tb = (rs(n, [P, 4 * 9 * 16]) for n in ("ta", "tb"))
    bz = rs("bz", [P, 2, 4, NC])
    zz = rs("zz", [P, 2, 4, NC])
    par = rs("par", [P, 6, PAIRS])
    sc = rs("sc", [P, 8, PAIRS])
    ah = rs("ah", [P, 2, PAIRS])
    fin = rs("fin", [P, 2, 2, PAIRS])
    bda = rs("blockdiag", [P, P])
    b_par = nc.alloc_sbuf_tensor_at("b_par", [P, 2, PAIRS, 16], F32, offset=E1)
    ang = nc.alloc_sbuf_tensor_at("ang", [P, PAIRS * 17], F32, offset=E1 + 8192)
    rnd = nc.alloc_sbuf_tensor_at("rnd", [P, PAIRS * 17], F32, offset=E1 + 8192 + 2304)

    s_par = sem("s5_parameters_loaded")
    s_par2 = sem("s5_output_parameters_loaded")
    s_pa = sem("s5_parameter_scalar")
    s_pv5 = sem("s5_parameter_vector")
    s_be = sem("s5_end_matrix_ready")
    s_w5 = sem("s5_output_matrix_ready")
    s_t3 = sem("s5_frames_turned")
    s_u3 = sem("s5_frames_copied")
    s_et = sem("s5_end_matrix_turned")
    s_eb = sem("s5_end_matrix_copied")
    s_t2 = sem("s5_frames_regrouped")
    s_u2 = sem("s5_frames_regrouped_copied")
    s_e5 = sem("s5_end_input_ready")
    s_ei = sem("s5_end_input_read")
    s_h5 = sem("s5_lags_ready")
    s_hb = sem("s5_lag_matrices_ready")
    s_x5 = sem("s5_states_ready")
    s_t4 = sem("s5_state_output_ready")
    s_y3 = sem("s5_state_output_copied")
    s_y5 = sem("s5_output_ready")
    s_ys5 = sem("s5_output_summed")
    s_yg = sem("s5_gelu_ready")
    s_yl = sem("s5_gelu_parts_ready")
    s_gs = sem("glu_sigmoid_ready")
    s_gh = sem("glu_hi_ready")
    s_gl = sem("glu_ready")
    s_s5v = sem("s5_vector_step")

    def s5_sync(sp):
        for name in ("glu", "s5_out"):
            stream_load(sp, name, BLOCK, lambda b: i["w_" + name][b, :, :] if isinstance(b, int) else
                        i["w_" + name][bass.ds(b, 1), :, :].rearrange("a p c -> (a p) c"))

    def s5_gpsimd(pool):
        pool.wait_ge(s_ada_t, 4 * ADA_UNITS)
        pool.wait_ge(s_hl, 3 * FT)
        pool.wait_ge(s_blk, first["out21"])
        for dst, src in ((par[:, 0:5, :], i["s5_par"]), (b_par[:, :, :, :], i["s5_b"]), (steps[:, :], i["steps"]),
                         (bda[:, :], i["blockdiag"])):
            pool.dma_start(dst, src).then_inc(s_par, 16)
        wait_modulated(pool, 4)
        for dst, src in ((c_par[:, :, :, :], i["s5_c"]), (d_skip[:, :], i["s5_d"])):
            pool.dma_start(dst, src).then_inc(s_par2, 16)
        pool.wait_ge(s_x5, KD)
        for n, k in enumerate(("s5_p", "s5_s")):
            pool.dma_start(o[k], fin[:, n, :, :]).then_inc(s_out, 16)

    def s5_parameter_stages_vector(dve):
        link = Chain(dve, s_s5v).step
        lr, li = par[:, 0, :], par[:, 1, :]
        theta = par[:, 2, :]
        dt, lrdt, th, k1, cr, ci, den, t0 = (sc[:, n, :] for n in range(8))
        tt = lambda out, a, b, op: dve.tensor_tensor(out, a, b, op)
        p3 = lambda t, w: t[:, 0:PAIRS * w].rearrange("p (q j) -> p q j", j=w)
        one = lambda v: v.rearrange("p (q j) -> p q j", j=1)
        row = lambda a, w: steps[:, a:a + w].rearrange("p (q j) -> p q j", q=1).broadcast_to([P, PAIRS, w])

        C1 = 6.28125
        C2 = float(2 * np.pi - C1)
        BIG = 12582912.0

        CLIP = 3.1415925

        def turns(a, r):
            link(dve.tensor_scalar(r, a, float(1 / (2 * np.pi)), BIG, ALU.mult, ALU.add))
            link(dve.tensor_scalar(r, r, BIG, None, ALU.subtract))

        def without_turns(a, r):
            link(dve.scalar_tensor_tensor(out=a, in0=r, scalar=-C1, in1=a, op0=ALU.mult, op1=ALU.add))
            link(dve.scalar_tensor_tensor(out=a, in0=r, scalar=-C2, in1=a, op0=ALU.mult, op1=ALU.add))
            link(dve.tensor_scalar(a, a, -CLIP, CLIP, ALU.max, ALU.min))

        def one_frame():
            dve.wait_ge(s_ada_t, 4 * ADA_UNITS)
            dve.wait_ge(s_par, 16 * 4)
            dve.wait_ge(s_pa, 1)
            link(dve.tensor_scalar(lr, lr, -1e-4, None, ALU.min))
            link(tt(lrdt, lr, dt, ALU.mult))
            link(tt(th, li, dt, ALU.mult))
            turns(th, t0)
            without_turns(th, t0)

        def power_angles():
            link(tt(p3(ang, 17), one(th).broadcast_to([P, PAIRS, 17]), row(0, 17), ALU.mult))
            link(tt(pw[:, 0, :, :], one(lrdt).broadcast_to([P, PAIRS, 17]), row(0, 17), ALU.mult))
            turns(ang[:, :], rnd[:, :])
            without_turns(ang[:, :], rnd[:, :])
            dve.tensor_copy(theta, p3(ang, 17)[:, :, 8]).then_inc(s_pv5, 1)

        def powers():
            dve.wait_ge(s_pa, 4)
            dve.wait_ge(s_pv5, 1)
            link(tt(pw[:, 1, :, :], pw[:, 1, :, :], pw[:, 0, :, :], ALU.mult))
            link(dve.tensor_copy(k1, pw[:, 0, :, 8]))
            link(tt(pw[:, 0, :, :], pw[:, 0, :, :], p3(rnd, 17), ALU.mult))
            link(dve.tensor_copy(rho[:, :, :], one(k1).broadcast_to([P, PAIRS, NC])))
            dve.memset(rho[:, :, 0:1], 0.0)
            link(dve.memset(rho[:, :, NCP:NCP + 1], 0.0))

        def turning_angles():
            link(tt(rot[:, 1, :, :], one(theta).broadcast_to([P, PAIRS, NC]), row(17, NC), ALU.mult))

        def turning_turns():
            turns(rot[:, 1, :, :], rot[:, 0, :, :])

        def turning_reduced():
            without_turns(rot[:, 1, :, :], rot[:, 0, :, :])
            dve.nop().then_inc(s_pv5, 1)

        def input_matrix():
            ar, ai = pw[:, 0, :, 1], pw[:, 1, :, 1]
            link(tt(den, lr, lr, ALU.mult))
            link(tt(k1, li, li, ALU.mult))
            link(tt(den, den, k1, ALU.add))
            link(dve.reciprocal(den, den))
            link(dve.tensor_scalar(t0, ar, -1.0, None, ALU.add))
            link(tt(cr, t0, lr, ALU.mult))
            link(tt(k1, ai, li, ALU.mult))
            link(tt(cr, cr, k1, ALU.add))
            link(tt(cr, cr, den, ALU.mult))
            link(tt(ci, ai, lr, ALU.mult))
            link(tt(k1, t0, li, ALU.mult))
            link(tt(ci, ci, k1, ALU.subtract))
            link(tt(ci, ci, den, ALU.mult))
            crb, cib = (one(v).broadcast_to([P, PAIRS, 16]) for v in (cr, ci))
            tq = ta[:, 0:PAIRS * 16].rearrange("p (q c) -> p q c", c=16)
            link(tt(bb[:, 0, :, :], b_par[:, 0, :, :], crb, ALU.mult))
            link(tt(tq, b_par[:, 1, :, :], cib, ALU.mult))
            link(tt(bb[:, 0, :, :], bb[:, 0, :, :], tq, ALU.subtract))
            link(tt(bb[:, 1, :, :], b_par[:, 1, :, :], crb, ALU.mult))
            link(tt(tq, b_par[:, 0, :, :], cib, ALU.mult))
            link(tt(bb[:, 1, :, :], bb[:, 1, :, :], tq, ALU.add))
            ar, ai, h_re, h_im = pw[:, 0, :, 8], pw[:, 1, :, 8], par[:, 3, :], par[:, 4, :]
            link(tt(ah[:, 0, :], ar, h_re, ALU.mult))
            link(tt(k1, ai, h_im, ALU.mult))
            link(tt(ah[:, 0, :], ah[:, 0, :], k1, ALU.subtract))
            link(tt(ah[:, 1, :], ar, h_im, ALU.mult))
            link(tt(k1, ai, h_re, ALU.mult))
            link(tt(ah[:, 1, :], ah[:, 1, :], k1, ALU.add))

        return link, (one_frame, power_angles, powers, turning_angles, turning_turns, turning_reduced, input_matrix)

    def s5_parameter_stages_scalar(act):
        step = lambda ins, n_: (ins.then_inc(s_pa, 1), act.wait_ge(s_pa, n_))

        def time_step():
            act.wait_ge(s_ada_t, 4 * ADA_UNITS)
            act.wait_ge(s_par, 16 * 4)
            step(act.activation(sc[:, 0, :], par[:, 2, :], ACT.Exp), 1)

        def powers():
            act.wait_ge(s_pv5, 1)
            a17 = ang[:, :].rearrange("p (q j) -> p q j", j=17)
            r17 = rnd[:, :].rearrange("p (q j) -> p q j", j=17)
            act.activation(pw[:, 0, :, :], pw[:, 0, :, :], ACT.Exp)
            step(act.activation(pw[:, 1, :, :], a17, ACT.Sin), 2)
            step(act.activation(r17, a17, ACT.Abs), 3)
            step(act.activation(r17, r17, ACT.Sin, scale=-1.0, bias=cols[:, C_HPI:C_HPI + 1]), 4)

        def frame():
            act.wait_ge(s_pv5, 2)
            step(act.activation(rot[:, 0, :, :], rot[:, 1, :, :], ACT.Abs), 5)
            act.activation(rot[:, 1, :, :], rot[:, 1, :, :], ACT.Sin)
            step(act.activation(rot[:, 0, :, :], rot[:, 0, :, :], ACT.Sin, scale=-1.0,
                                bias=cols[:, C_HPI:C_HPI + 1]), 6)
        return {0: time_step, 1: powers, 6: frame}

    def s5_vector(dve):
        link = s5_link[0]
        tt = lambda out, a, b, op: dve.tensor_tensor(out, a, b, op)

        def matrices(n):
            r, q = n % 2, slice(4 * n, 4 * n + 4)
            if n >= 2:
                dve.wait_ge(s_et, n - 1)
                dve.wait_ge(s_t4, n - 1)

            def outer(dst, p0, w, m, sub_first):
                pr, pi = (pw[:, z, q, p0:p0 + w].rearrange("p q (j b) -> p q j b", b=1).broadcast_to([P, 4, w, 16])
                          for z in range(2))
                mr, mi = (m[:, z, q, :].rearrange("p q (b c) -> p q b c", b=1).broadcast_to([P, 4, w, 16])
                          for z in range(2))
                v = lambda t: t[:, 0:4 * w * 16].rearrange("p (q j c) -> p q j c", q=4, j=w)
                d = [dst(z) for z in range(2)]
                tt(d[0], pr, mr, ALU.mult)
                tt(v(ta), pi, mi, ALU.mult)
                tt(v(tb), pr, mi, ALU.mult)
                link(tt(d[1], pi, mr, ALU.mult))
                if sub_first:
                    tt(d[0], d[0], v(ta), ALU.subtract)
                    return tt(d[1], d[1], v(tb), ALU.add)
                link(tt(d[0], d[0], v(ta), ALU.subtract))
                link(tt(v(tb), d[1], v(tb), ALU.add))
                return dve.tensor_scalar(d[1], v(tb), -1.0, None, ALU.mult)
            ins = outer(lambda z: be[:, r, z, :, :].rearrange("p q (j c) -> p q j c", c=16), 9, 8, bb, True)
            ins.then_inc(s_be, 1)
            dve.wait_ge(s_be, n + 1)
            for z in range(2):
                for half in range(2):
                    rows_ = slice(64 * half, 64 * half + 64)
                    dve.tensor_copy(bp[rows_, r, z, :, 16 * half:16 * half + 16], bb[rows_, z, q, :])
            ins = outer(lambda z: wm[:, r, z, :, :, :], 0, 9, c_par, False)
            ins.then_inc(s_w5, 1)
            dve.wait_ge(s_w5, n + 1)

        def lags(n):
            dve.wait_ge(s_h5, n + 1)
            if n >= 2:
                dve.wait_ge(s_y5, n - 1)
            src = ps[:, 0, 0:P].rearrange("p (j b c) -> p j b c", j=SUB, b=1).broadcast_to([P, SUB, 8, 16])
            m = bda[:, :].rearrange("p (a g c) -> p a g c", a=1, g=8).broadcast_to([P, SUB, 8, 16])
            tt(hb[:, n % 2, :, :].rearrange("p j (g c) -> p j g c", c=16), src, m, ALU.mult).then_inc(s_hb, 1)

        def states(n):
            r, q = n % 2, slice(4 * n, 4 * n + 4)
            co, si = rot[:, 0, q, :], rot[:, 1, q, :]
            t_a, t_b = (t[:, 0:4 * NC].rearrange("p (q c) -> p q c", q=4) for t in (ta, tb))
            e_re, e_im = (ps[:, 2 + z, 0:4 * NC].rearrange("p (q c) -> p q c", q=4) for z in range(2))
            dve.wait_ge(s_e5, n + 1)
            tt(bz[:, 0, :, :], e_re, co, ALU.mult)
            tt(t_a, e_im, si, ALU.mult)
            tt(bz[:, 1, :, :], e_im, co, ALU.mult)
            tt(t_b, e_re, si, ALU.mult).then_inc(s_ei, 1)
            dve.wait_ge(s_ei, n + 1)
            tt(bz[:, 0, :, :], bz[:, 0, :, :], t_a, ALU.add)
            link(tt(bz[:, 1, :, :], bz[:, 1, :, :], t_b, ALU.subtract))
            for z in range(2):
                ins = tt(bz[:, z, :, NCP], bz[:, z, :, NCP], ah[:, z, q], ALU.add)
            link(ins)
            for z in range(2):
                ins = dve.tensor_tensor_scan(zz[:, z, :, :].rearrange("p q c -> p (q c)"),
                                             rho[:, q, :].rearrange("p q c -> p (q c)"),
                                             bz[:, z, :, :].rearrange("p q c -> p (q c)"), 0.0, ALU.mult, ALU.add)
            link(ins)
            if n >= 2:
                dve.wait_ge(s_t4, n - 1)
            x_re, x_im = (xx[:, r, z, :, 1:NC + 1] for z in range(2))
            tt(x_re, zz[:, 0, :, :], co, ALU.mult)
            tt(t_a, zz[:, 1, :, :], si, ALU.mult)
            tt(x_im, zz[:, 1, :, :], co, ALU.mult)
            link(tt(t_b, zz[:, 0, :, :], si, ALU.mult))
            tt(x_re, x_re, t_a, ALU.subtract)
            link(tt(x_im, x_im, t_b, ALU.add))
            for z in range(2):
                dve.tensor_copy(fin[:, 0, z, q], xx[:, r, z, :, NCP])
                ins = dve.tensor_copy(fin[:, 1, z, q], xx[:, r, z, :, NC])
            link(ins)
            dve.memset(xx[:, r, :, :, 0:1], 0.0)
            for z in range(2):
                ins = dve.tensor_copy(xx[:, r, z, :, NCP], par[:, 3 + z, q])
            ins.then_inc(s_x5, 1)
            dve.wait_ge(s_x5, n + 1)

        def skip(n):
            dve.wait_ge(s_y5, n + 1)
            dve.scalar_tensor_tensor(out=halves(uf[:, n, :]), in0=halves(uf[:, n, :]), scalar=d_skip[:, n:n + 1],
                                     in1=pair(3), op0=ALU.mult, op1=ALU.add).then_inc(s_ys5, 1)

        dve.wait_ge(s_par2, 32)
        link(dve.memset(bp[:, :, :, :, :], 0.0))
        matrices(0)
        for n in range(KD + 1):
            if n < KD:
                if n + 1 < KD:
                    matrices(n + 1)
                lags(n)
                if n == 0:
                    dve.wait_ge(s_pa, 6)
                states(n)
            if n >= 1:
                skip(n - 1)
        for k in range(KD):
            dve.wait_ge(s_yg, KD + k + 1)
            tt(u_lo[:, k, :], uf[:, k, :], u_hi[:, k, :].bitcast(F32), ALU.subtract).then_inc(s_yl, 1)
        g0 = first["glu"]
        for b in range(4):
            for m_ in range(2):
                k = 2 * b + m_
                dve.wait_ge(s_gs, k + 1)
                if m_ == 1:
                    dve.nop().then_inc(s_evac, 1)
                link(tt(hf[:, m_, :], sg[:, m_, :], uf[:, k, :], ALU.mult))
                dve.tensor_copy(glu_hi(k), hf[:, m_, :]).then_inc(s_gh, 1)
                dve.wait_ge(s_gh, k + 1)
                tt(h_lo[:, k, :], hf[:, m_, :], glu_hi(k).bitcast(F32), ALU.subtract).then_inc(s_gl, 1)
            dve.wait_ge(s_gl, 2 * b + 2)
            split_lo(dve, g0 + 2, b % 2, b // 2)
        gate_vector(dve, 4)
        residual_vector(dve, "s5_out", 4, 2)
        dve.wait_ge(s_out, 16 * STORES)

    def glu_hi(k):
        return h_hi[:, 8 + k, :] if k < 4 else h_lo[:, 4 + k, :]

    def s5_scalar(act):

        def gelu(u):
            act.wait_ge(s_ys5, u + 1)
            act.activation(uf[:, u, :], uf[:, u, :], ACT.Gelu_apprx_tanh).then_inc(s_yg, 1)

        for n in range(KD + 1):
            r = n % 2
            if n < KD:
                act.wait_ge(s_t3, n + 1)
                if n >= 2:
                    act.wait_ge(s_t2, n - 1)
                for a in range(2):
                    ins = act.activation(u3[0:NC, r, :, 64 * a:64 * a + 64].rearrange("p g (s m) -> p g s m", m=16),
                                         ps[0:NC, a, :].rearrange("p (s g m) -> p g s m", s=4, g=8), ACT.Copy)
                ins.then_inc(s_u3, 1)
                act.wait_ge(s_et, n + 1)
                if n >= 2:
                    act.wait_ge(s_e5, n - 1)
                act.activation(eb[:, r, :, :, :].rearrange("p z q c -> p z (q c)"), ps[:, 2:4, :],
                               ACT.Copy).then_inc(s_eb, 1)
            if n >= 2:
                gelu(n - 2)
            if n >= 1:
                u = n - 1
                act.wait_ge(s_t4, u + 1)
                if u >= 2:
                    act.wait_ge(s_y5, u - 1)
                for a in range(2):
                    ins = act.activation(
                        y3[0:NC, u % 2, :, :].rearrange("p t (q a m) -> p t q a m", a=2, m=16)[:, :, :, a, :],
                        ps[0:NC, 4 + a, :].rearrange("p (q t m) -> p t q m", q=4, t=SUB), ACT.Copy)
                ins.then_inc(s_y3, 1)
            if n < KD:
                act.wait_ge(s_t2, n + 1)
                act.activation(u2[:, r, :, :].rearrange("p (a g) c -> p a (g c)", a=2), ps[:, 0:2, 0:4 * NC],
                               ACT.Copy).then_inc(s_u2, 1)
        gelu(KD - 1)
        act.wait_ge(s_x5, KD)
        act.wait_ge(s_w5, KD)
        act.wait_ge(s_yg, KD)
        for k in range(KD):
            act.activation(u_hi[:, k, :], uf[:, k, :], ACT.Copy).then_inc(s_yg, 1)
        g0 = first["glu"]
        for b in range(4):
            act.wait_ge(s_blk, g0 + b + 1)
            for m_ in range(2):
                if b >= 1:
                    act.wait_ge(s_gl, 2 * b + m_ - 1)
                ins = act.activation(halves(sg[:, m_, :]), pair(2 * (b % 2) + m_), ACT.Sigmoid)
                ins.then_inc(s_gs, 1)
            act.wait_ge(s_gs, 2 * b + 2)
            split_hi(act, g0 + 2, b % 2, b // 2)
        out_scalar(act, "s5_out")

    def s5_tensor(pe):
        wait_modulated(pe, 4)
        pe.wait_ge(s_evac, first["glu"])

        def turn(n):
            if n >= 1:
                pe.wait_ge(s_hb, n)
            for s in range(SUB):
                m = pe.transpose(ps[0:NC, s // 4, (s % 4) * P:(s % 4) * P + P],
                                 uf[:, n, :].rearrange("p (c s) -> p s c", s=SUB)[:, s, :], ident[:, :])
            m.then_inc(s_t3, 1)
            pe.wait_ge(s_be, n + 1)
            if n >= 1:
                pe.wait_ge(s_ei, n)
            for z in range(2):
                for q in range(4):
                    m = pe.transpose(ps[:, 2 + z, q * P:q * P + P], be[:, n % 2, z, q, :], ident[:, :])
            m.then_inc(s_et, 1)

        def regroup(n):
            pe.wait_ge(s_u3, n + 1)
            for g in range(8):
                m = pe.transpose(ps[:, g // 4, (g % 4) * NC:(g % 4) * NC + NC], u3[0:NC, n % 2, g, :],
                                 ident[0:NC, 0:NC])
            m.then_inc(s_t2, 1)

        def end_inputs_and_lags(n):
            r = n % 2
            pe.wait_ge(s_u2, n + 1)
            pe.wait_ge(s_eb, n + 1)
            for z in range(2):
                for g in range(8):
                    q, half = g // 2, g % 2
                    m = pe.matmul(ps[64 * half:64 * half + 64, 2 + z, q * NC:q * NC + NC],
                                  eb[:, r, z, q, 64 * half:64 * half + 64], u2[:, r, g, :], start=True, stop=True)
            m.then_inc(s_e5, 1)
            pe.wait_ge(s_w5, n + 1)
            for q in range(4):
                for z in range(2):
                    m = pe.matmul(ps[32 * q:32 * q + 32, 0, 0:P], bp[:, r, z, q, :],
                                  wm[:, r, z, q, 0:SUB, :].rearrange("p j c -> p (j c)"),
                                  start=z == 0, stop=z == 1)
            m.then_inc(s_h5, 1)

        def state_output(u):
            r = u % 2
            pe.wait_ge(s_x5, u + 1)
            if u >= 1:
                pe.wait_ge(s_y3, u)
            for g in range(8):
                q, rows_ = g // 2, slice(64 * (g % 2), 64 * (g % 2) + 64)
                for z in range(2):
                    m = pe.matmul(ps[0:NC, 4 + g % 2, q * P:q * P + P], xx[rows_, r, z, q, 0:NC],
                                  wm[rows_, r, z, q, 1:9, :].rearrange("p j c -> p (j c)"),
                                  start=z == 0, stop=z == 1)
            m.then_inc(s_t4, 1)

        def output(u, a):
            r = u % 2
            if a == 0:
                pe.wait_ge(s_hb, u + 1)
                if u >= 1:
                    pe.wait_ge(s_ys5, u)
            dst = ps[:, 6 + a, 0:HALF].rearrange("p (c t) -> p c t", t=SUB)
            src = halves(uf[:, u, :])[:, a, :].rearrange("p (c t) -> p c t", t=SUB)
            for j in range(SUB):
                pe.matmul(dst[:, :, j:SUB], hb[:, r, j, :], src[:, :, 0:SUB - j], start=j == 0, stop=False)
            if a == 0:
                pe.wait_ge(s_y3, u + 1)
            for s in range(SUB):
                m = pe.matmul(dst[:, :, s], y3[0:NC, r, s, :], ident[0:NC, 36 * a:36 * a + 36],
                              start=False, stop=s == SUB - 1)
            if a == 1:
                m.then_inc(s_y5, 1)

        for n in range(KD + 1):
            if n < KD:
                turn(n)
            if n >= 1:
                state_output(n - 1)
            if n < KD:
                regroup(n)
            if n >= 1:
                output(n - 1, 0)
            if n < KD:
                end_inputs_and_lags(n)
            if n >= 1:
                output(n - 1, 1)
        pe.wait_ge(s_yl, KD)
        body, count = product(pe, "glu", 2, KD, u_hi, u_lo)
        blocks_loop(pe, count, body)
        pe.wait_ge(s_gl, KD)
        body, count = product(pe, "s5_out", 2, KD, glu_hi, lambda k: h_lo[:, k, :])
        blocks_loop(pe, count, body)
    constant_loads = [(ident[:, :], i["ident"]), (mean_w[:, :], i["mean_w"]), (masks[:, :, :], i["masks"]),
                      (swap[:, :, :], i["swap"]), (onecol[:, :], i["onecol"]), (b_ada[:, :, :], i["b_ada"]),
                      (ln_g[:, :, :], i["ln_g"]), (ln_b[:, :, :], i["ln_b"]), (cols[:, :], i["cols"])]

    chains = {}
    done = lambda name: first[name] + dict(STREAM)[name]
    block = stack.enter_context(nc.Block())

    @block.sync
    def _(sp):
        ada_sync(sp)
        ffn_sync(sp, 0)
        mix_sync(sp)
        ffn_sync(sp, 1)
        ffn_sync(sp, 2)
        s5_sync(sp)
        ffn_sync(sp, 3)

    @block.gpsimd
    def _(pool):
        ada_load(pool, 0, UNITS0, 0)
        u_gpsimd(pool, 0)
        ada_load(pool, 0, UNITS0, 1)
        u_gpsimd(pool, 1)
        mix_gpsimd(pool)
        pool.wait_ge(s_ol, 9)
        pool.dma_start(c_act[:, :, :], i["c"]).then_inc(s_in2, 16)
        ada_load(pool, UNITS0, ADA_IN[2, 0], 0)
        u_gpsimd(pool, 2)
        ada_load(pool, UNITS0, ADA_IN[2, 0], 1)
        ada_load(pool, ADA_IN[2, 0], ADA_UNITS, 0)
        u_gpsimd(pool, 3)
        ada_load(pool, ADA_IN[2, 0], ADA_UNITS, 1)
        s5_gpsimd(pool)
        u_gpsimd(pool, 5)
        for k in range(KD):
            pool.wait_ge(s_x, KD * (NMOD - 1) + k + 1)
            pool.dma_start(o["y"][:, k, :], x[:, k, :]).then_inc(s_out, 16)
        pool.wait_ge(s_out, 16 * (KD + STORES))

    @block.scalar
    def _(act):
        chains["act"] = Chain(act, s_act)
        act.dma_start(x[:, :, :], i["x"]).then_inc(s_cst, 16)
        for dst, src in constant_loads:
            act.dma_start(dst, src).then_inc(s_cst, 16)
        conditioning_scalar(act, s_in, False)
        for r in range(2):
            split_hi(act, 0, r, 0)
        u_scalar(act, 0)
        ffn_scalar(act, 0)
        ln_scalar(act, 0)
        mix_scalar(act)
        conditioning_scalar(act, s_in2, True)
        ln_scalar(act, 1)
        ffn_scalar(act, 1)
        ln_scalar(act, 2)
        ffn_scalar(act, 2)
        ln_scalar(act, 3)
        s5_scalar(act)
        ln_scalar(act, 4)
        ffn_scalar(act, 3)
        ln_scalar(act, 5)

    @block.vector
    def _(dve):
        chains["dve"] = Chain(dve, s_dve)
        ada_vector_first(dve)
        scale_vector(dve, 0)
        for r in range(2):
            split_lo(dve, 0, r, 0)
        for k in range(KD):
            u_sample(dve, 0, k)
        u_vector(dve, 0)
        ffn_vector(dve, 0)
        ln_vector(dve, 0)
        mix_vector(dve)
        ln_vector(dve, 1)
        dve.wait_ge(s_ada_c, 2)
        ffn_vector(dve, 1)
        ln_vector(dve, 2)
        ffn_vector(dve, 2)
        ln_vector(dve, 3)
        s5_vector(dve)
        ln_vector(dve, 4)
        ffn_vector(dve, 3)
        ln_vector(dve, 5)

    @block.tensor
    def _(pe):
        ada_tensor_first(pe)
        ffn_tensor(pe, 0)
        ln_tensor(pe, 0, done("out01"))
        mix_tensor(pe)
        ln_tensor(pe, 1, done("mix_out"))
        ffn_tensor(pe, 1)
        ln_tensor(pe, 2, done("out11"))
        ffn_tensor(pe, 2)
        ln_tensor(pe, 3, done("out21"))
        s5_tensor(pe)
        ln_tensor(pe, 4, done("s5_out"))
        ffn_tensor(pe, 3)
        ln_tensor(pe, 5, done("out31"))

    stack.close()


def mixer_layout(a, n, tiles):
    w = n["w_mix_in"][0]
    z = lambda c: np.zeros((D, c), np.float32)
    w = np.concatenate([w[:, 0:2048], w[:, 2056:2312], w[:, 2312:2440], w[:, 2440:2504], w[:, 2048:2052], z(28),
                        w[:, 2052:2056], z(28)], axis=1)
    a["w_mix_in"] = tiles(w, 2, KD)
    qb = n["mla_w_q_b"][0].reshape(256, HEADS, 192)
    qb = np.concatenate([qb[:, :, 0:128].reshape(256, 512), qb[:, :, 128:].reshape(256, 256)], axis=1)
    a["w_q_b"] = tiles(qb, 6, 2)[0]
    kb = n["mla_w_kv_b"][0].reshape(128, HEADS, 256)
    a["w_kv_b"] = np.ascontiguousarray(np.concatenate([kb[:, :, 0:128].reshape(128, 512),
                                                       kb[:, :, 128:].reshape(128, 512)], axis=1))
    a["w_mix_out"] = tiles(n["w_mix_out"][0], 2, KD)
    a["conv_state"] = np.ascontiguousarray(n["state_gdn_conv"][0, 0].reshape(3, QT, P).transpose(2, 1, 0))
    a["gdn_state"] = np.ascontiguousarray(n["state_gdn"][0, 0].transpose(1, 0, 2))
    a["cache_latent"] = np.ascontiguousarray(n["cache_mla_latent"][0, 0].T)
    kt = n["cache_mla_krope"][0, 0].T
    a["cache_rope"] = np.concatenate([kt, kt])
    for k, src in (("w_glu", "s5_w_glu"), ("w_s5_out", "s5_w_out")):
        a[k] = tiles(n[src][0], 2, KD)
    two = lambda v: v.reshape(PAIRS, P, *v.shape[2:]).swapaxes(0, 1)
    a["s5_par"] = np.stack([two(v) for v in (n["s5_lambda_re"][0], n["s5_lambda_im"][0],
                                             np.repeat(n["s5_log_dt"][0][:, None], 64, axis=1),
                                             n["state_s5_re"][0, 0], n["state_s5_im"][0, 0])], axis=1)
    a["s5_b"] = np.stack([two(n["s5_b_re"][0]), two(n["s5_b_im"][0])], axis=1)
    a["s5_c"] = np.stack([two(n[k][0].swapaxes(1, 2)) for k in ("s5_c_re", "s5_c_im")], axis=1)
    a["s5_d"] = np.ascontiguousarray(n["s5_d"][0].reshape(KD, P).T)
    cols = np.zeros((P, NCOLS), np.float32)
    cols[:, C_EPS] = EPS / ALPHA ** 2
    cols[:, C_CONV:C_CONV + 48] = n["gdn_conv_w"][0].reshape(CONV, QT, P).transpose(2, 1, 0).reshape(P, 48)
    cols[:, C_NORMW] = n["gdn_norm_w"][0]
    cols[:, C_QN:C_QN + 2] = n["mla_q_norm"][0].reshape(2, P).T
    cols[:, C_KVN] = n["mla_kv_norm"][0]
    cols[96:100, C_DT] = n["gdn_dt_bias"][0]
    cols[0:4, C_ALOG] = n["gdn_a_log"][0]
    cols[0:10, C_RNS] = [128.0] * 4 + [1.0] * 4 + [1.0 / 256, 1.0 / 128]
    cols[0:10, C_RNB] = [128.0 * EPS] * 4 + [EPS] * 6
    cols[:, C_OEPS] = EPS
    cols[:, C_HPI] = np.pi / 2
    a["cols"] = cols


def returned(r):
    y = r["y"].transpose(1, 0, 2).reshape(D, TOKENS).T
    conv = {s: r["conv_" + s].transpose(2, 1, 0).reshape(1, 1, 3, QT * P) for s in "ps"}
    gdn = {s: r["gdn_" + s].transpose(1, 0, 2)[None, None] for s in "ps"}
    lat, kr = r["latent"].T, r["krope"].T
    s5 = {s: [r["s5_" + s][:, z, :].T.reshape(1, 1, 64, 64) for z in range(2)] for s in "ps"}
    return (y[None, :SEQ], y[None, SEQ:], lat[None, None, :SEQ], kr[None, None, :SEQ], gdn["p"], conv["p"],
            *s5["p"], lat[None, None, SEQ:], kr[None, None, SEQ:], gdn["s"], conv["s"], *s5["s"])


def shape_constants():
    from numpy import arange, eye, float32, zeros
    t, s = arange(P)[:, None], arange(P)[None, :]
    masks = zeros((P, 7, P), float32)
    for lv in range(6):
        b = 1 << lv
        masks[:, lv, :] = (t // (2 * b) == s // (2 * b)) & (t // b % 2 == 1) & (s // b % 2 == 0)
    masks[:, 6, :] = (t // CH == s // CH) & (t <= s)
    swap = zeros((P, 3, P), float32)
    swap[:, 0, :] = (t // 64 == s // 64) & (t % 64 == (s + 32) % 64)
    swap[:, 1, :] = (t < 64) & (t == s % 64)
    swap[:, 2, :] = (t < 64) & (t == (s + 32) % 64)
    onecol = zeros((P, 32), float32)
    onecol[:, 15] = 1.0
    half = 32
    inv = (np.float32(10000.0) ** (-arange(half, dtype=float32) / float32(half))).astype(float32)
    pos = np.concatenate([arange(SEQ), PAST + arange(DEC)]).astype(float32)
    ang = (pos[None, :] * inv[:, None]).astype(float32)
    cos, sin = np.cos(ang), np.sin(ang)
    rope = zeros((P, 2, TOKENS), float32)
    rope[:, 0] = np.concatenate([cos] * 4)
    rope[:, 1] = np.concatenate([-sin, sin] * 2)
    bd = zeros((P, 8, 16), float32)
    bd[:] = (arange(P)[:, None] // 16 == arange(8)[None, :])[:, :, None]
    steps = np.tile(np.concatenate([arange(9), arange(7, -1, -1), arange(NCP), arange(DEC // SUB)]).astype(float32),
                    (P, 1))
    return {"steps": steps, "ident": eye(P, dtype=float32), "mean_w": np.full((P, P), 1.0 / D, float32), "masks": masks,
            "swap": swap, "onecol": onecol, "rope": rope, "blockdiag": bd.reshape(P, P)}


def kernel(**inputs):
    import numpy as np
    import concourse.bacc as bacc
    from concourse.bass_utils import run_bass_kernel_spmd

    n = {k: np.asarray(v) for k, v in inputs.items()}
    feat = lambda a: np.ascontiguousarray(a.reshape(KD, P, -1).transpose(1, 0, 2))
    cat = lambda a, b: np.concatenate([a, b], axis=1)

    def tiles(w, per, kk):
        nb = w.shape[1] // (per * P)
        w = w.reshape(kk, P, nb, per, P).transpose(2, 1, 0, 3, 4)
        return np.ascontiguousarray(w.reshape(nb, P, kk * per * P))

    a = dict(shape_constants())
    a["x"] = feat(cat(n["x_prompt"][0].T, n["x_sample"][0].T))
    a["c"] = np.tile(np.stack([n["c_prompt"][0], n["c_sample"][0]])[None], (P, 1, 1))
    a["c_col"] = feat(np.stack([n["c_prompt"][0], n["c_sample"][0]], axis=1))
    a["w_ada0"] = np.ascontiguousarray(n["w_ada"][0, :, 0:D].reshape(KD, P, KD, P).transpose(1, 2, 0, 3))
    wa = n["w_ada"].transpose(0, 2, 1).reshape(18 * KD, P, D)[KD:]
    a["w_ada"] = np.ascontiguousarray(wa.transpose(1, 0, 2))
    a["b_ada"] = np.ascontiguousarray(n["b_ada"].reshape(3 * NMOD, KD, P).transpose(2, 0, 1))
    for k in ("ln_g", "ln_b"):
        a[k] = np.ascontiguousarray(n[k].reshape(NMOD, KD, P).transpose(2, 0, 1))
    w = n["w_ff_in"].reshape(4, KD, P, 2, FT, P).transpose(0, 4, 2, 1, 3, 5)
    a["w_in"] = np.ascontiguousarray(w.reshape(4, FT, P, BLOCK))
    w = n["w_ff_out"].reshape(4, FT, P, KD, P).transpose(0, 3, 2, 1, 4)
    for s, (j0, m) in enumerate(SEGS):
        a[f"w_out{s}"] = np.ascontiguousarray(w[:, :, :, j0:j0 + m]).reshape(4, KD, P, m * P)
    mixer_layout(a, n, tiles)

    nc = bacc.Bacc("TRN2", target_bir_lowering=False, num_devices=1)
    aps = {k: nc.dram_tensor(f"in_{k}", v.shape, mybir.dt.from_np(v.dtype), kind="ExternalInput").ap()
           for k, v in a.items()}
    outs = {k: nc.dram_tensor(f"out_{k}", s, F32, kind="ExternalOutput").ap() for k, s in OUTS.items()}
    trunk(nc, aps, outs)
    r = run_bass_kernel_spmd(nc, [{f"in_{k}": v for k, v in a.items()}], core_ids=[0]).results[0]
    r = {k: np.asarray(r[f"out_{k}"]) for k in OUTS}
    return returned(r)
```
